# Optimizing a Trainium2 kernel written in Bass

```python
import functools
import jax, jax.numpy as jnp
from jax import lax
import numpy as np

D_MODEL = 1024
BATCH = 1
SEQ = 1024
DEPTH = 2
DEC_BATCH = 8
DEC_SEQ = 16
PAST_LEN = 2048

CHUNK = 64
N_MIXERS = 2
N_HGRN_LAYERS = (DEPTH + 1) // 2
N_DSA_LAYERS = DEPTH // 2
EPS = 1e-6
HG_HEADS = 8
HG_KDIM = 128
HG_VDIM = D_MODEL // HG_HEADS
HG_FDIM = HG_HEADS * HG_KDIM
HG_IN = 2 * HG_FDIM + 2 * D_MODEL
REC_BLOCK = 32
N_HEADS = 16
HEAD_DIM = D_MODEL // N_HEADS
N_KV_HEADS = 4
N_GROUPS = N_HEADS // N_KV_HEADS
IDX_HEADS = 8
IDX_DIM = 64
TOPK_MAX = 256
Q_BLOCK = 64
ROPE_THETA = 500000.0
DSA_IN = N_HEADS * HEAD_DIM + 2 * N_KV_HEADS * HEAD_DIM + IDX_HEADS * IDX_DIM + IDX_DIM + IDX_HEADS
D_FF = 2816
CONV_W = 3

kernel_name = 'hybrid_hgrn2_dsa_stream_step'

F32 = jnp.float32

def rms_norm(x, g):
    xf = x.astype(F32)
    y = xf * lax.rsqrt(jnp.mean(xf * xf, axis=-1, keepdims=True) + EPS)
    return (y * g.astype(F32)).astype(x.dtype)

def layer_norm(x, w, b):
    xf = x.astype(F32)
    mu = jnp.mean(xf, axis=-1, keepdims=True)
    var = jnp.mean(jnp.square(xf - mu), axis=-1, keepdims=True)
    return ((xf - mu) * lax.rsqrt(var + EPS) * w.astype(F32) + b.astype(F32)).astype(x.dtype)

def partial_rope(x, pos):
    rot = x.shape[-1] // 4
    half = rot // 2
    inv_freq = ROPE_THETA ** (-jnp.arange(half, dtype=F32) / half)
    ang = pos.astype(F32)[:, None] * inv_freq[None, :]
    cos = jnp.cos(ang)[:, None, :]
    sin = jnp.sin(ang)[:, None, :]
    xf = x.astype(F32)
    x1, x2, rest = xf[..., :half], xf[..., half:rot], xf[..., rot:]
    out = jnp.concatenate([x1 * cos - x2 * sin, x2 * cos + x1 * sin, rest], axis=-1)
    return out.astype(x.dtype)

def hgrn_recurrence(S0, q, k, v, logf, block):
    B, T, H, K = q.shape
    V = v.shape[-1]
    n = T // block

    def to_blocks(a):
        return a.reshape(B, n, block, H, a.shape[-1]).transpose(1, 0, 3, 2, 4)

    tri = jnp.tril(jnp.ones((block, block), dtype=bool))

    def step(S, xs):
        qb, kb, vb, gb = xs
        G = jnp.cumsum(gb, axis=2)
        diff = G[:, :, :, None, :] - G[:, :, None, :, :]
        decay = jnp.exp(jnp.where(tri[:, :, None], diff, -jnp.inf))
        A = jnp.einsum('bhtk,bhsk,bhtsk->bhts', qb, kb, decay)
        o = jnp.einsum('bhts,bhsv->bhtv', A, vb) + jnp.einsum('bhtk,bhkv->bhtv', qb * jnp.exp(G), S)
        G_last = G[:, :, -1:, :]
        S_new = jnp.exp(G_last[:, :, 0, :])[..., None] * S + jnp.einsum(
            'bhsk,bhsv->bhkv', kb * jnp.exp(G_last - G), vb)
        return S_new, o

    S, o = lax.scan(step, S0, (to_blocks(q), to_blocks(k), to_blocks(v), to_blocks(logf)))
    o = o.transpose(1, 0, 3, 2, 4).reshape(B, T, H, V)
    return o, S

def hgrn_mixer(h, S0, w_in, lb, norm_g, w_out):
    B, T, _ = h.shape
    proj = h @ w_in
    q = proj[..., :HG_FDIM].astype(F32)
    f = proj[..., HG_FDIM:2 * HG_FDIM].astype(F32)
    i = proj[..., 2 * HG_FDIM:2 * HG_FDIM + D_MODEL].astype(F32)
    g = proj[..., 2 * HG_FDIM + D_MODEL:].astype(F32)
    fg = lb + (1.0 - lb) * jax.nn.sigmoid(f)
    q = jax.nn.silu(q).reshape(B, T, HG_HEADS, HG_KDIM)
    k = (1.0 - fg).reshape(B, T, HG_HEADS, HG_KDIM)
    logf = jnp.log(fg).reshape(B, T, HG_HEADS, HG_KDIM)
    v = i.reshape(B, T, HG_HEADS, HG_VDIM)
    block = REC_BLOCK if T % REC_BLOCK == 0 else T
    o, S = hgrn_recurrence(S0.astype(F32), q, k, v, logf, block)
    o = rms_norm(o, norm_g) * jax.nn.silu(g).reshape(B, T, HG_HEADS, HG_VDIM)
    out = o.reshape(B, T, D_MODEL).astype(h.dtype) @ w_out
    return out, S.astype(h.dtype)

def dsa_attention(q, k_all, v_all, qi, ki_all, w_idx, q_pos, n_sel):
    B, T = q.shape[:2]
    L = k_all.shape[1]
    blk = Q_BLOCK if T % Q_BLOCK == 0 else T
    n = T // blk
    key_chunk = jnp.arange(L) // CHUNK
    scale = HEAD_DIM ** -0.5

    def blocks(a):
        return a.reshape((B, n, blk) + a.shape[2:]).swapaxes(0, 1)

    def one_block(xs):
        qb, qib, wb, pb = xs
        admissible = key_chunk[None, :] <= (pb // CHUNK)[:, None]
        dots = jnp.einsum('bthd,bsd->bths', qib, ki_all, preferred_element_type=F32)
        score = jnp.einsum('bth,bths->bts', wb.astype(F32), jax.nn.relu(dots))
        score = jnp.where(admissible[None], score, -jnp.inf)
        sel_val, sel_idx = lax.top_k(score, n_sel)
        valid = sel_val > -jnp.inf
        kg = jax.vmap(lambda kb, ib: kb[ib])(k_all, sel_idx)
        vg = jax.vmap(lambda vb, ib: vb[ib])(v_all, sel_idx)
        qg = qb.reshape(B, blk, N_KV_HEADS, N_GROUPS, HEAD_DIM)
        logits = jnp.einsum('btkgd,btskd->btkgs', qg, kg, preferred_element_type=F32) * scale
        logits = jnp.where(valid[:, :, None, None, :], logits, -jnp.inf)
        p = jax.nn.softmax(logits, axis=-1).astype(vg.dtype)
        o = jnp.einsum('btkgs,btskd->btkgd', p, vg)
        return o.reshape(B, blk, N_HEADS * HEAD_DIM)

    out = lax.map(one_block, (blocks(q), blocks(qi), blocks(w_idx), q_pos.reshape(n, blk)))
    return out.swapaxes(0, 1).reshape(B, T, N_HEADS * HEAD_DIM)

def dsa_mixer(h, k_cache, v_cache, ki_cache, w_in, kln_w, kln_b, w_out):
    B, T, _ = h.shape
    past = k_cache.shape[1]
    pos = past + jnp.arange(T)
    o1 = N_HEADS * HEAD_DIM
    o2 = o1 + N_KV_HEADS * HEAD_DIM
    o3 = o2 + N_KV_HEADS * HEAD_DIM
    o4 = o3 + IDX_HEADS * IDX_DIM
    o5 = o4 + IDX_DIM
    proj = h @ w_in
    q = partial_rope(proj[..., :o1].reshape(B, T, N_HEADS, HEAD_DIM), pos)
    k = partial_rope(proj[..., o1:o2].reshape(B, T, N_KV_HEADS, HEAD_DIM), pos)
    v = proj[..., o2:o3].reshape(B, T, N_KV_HEADS, HEAD_DIM)
    qi = partial_rope(proj[..., o3:o4].reshape(B, T, IDX_HEADS, IDX_DIM), pos)
    ki = layer_norm(proj[..., o4:o5], kln_w, kln_b)
    ki = partial_rope(ki[:, :, None, :], pos)[:, :, 0, :]
    wi = proj[..., o5:] * (IDX_HEADS * IDX_DIM) ** -0.5
    k_all = jnp.concatenate([k_cache.astype(k.dtype), k], axis=1)
    v_all = jnp.concatenate([v_cache.astype(v.dtype), v], axis=1)
    ki_all = jnp.concatenate([ki_cache.astype(ki.dtype), ki], axis=1)
    n_sel = min(TOPK_MAX, (past + T) // 4)
    o = dsa_attention(q, k_all, v_all, qi, ki_all, wi, pos, n_sel)
    return o @ w_out, k, v, ki

def conv_ffn(h, state, w_in, conv_w, conv_b, w_down):
    T = h.shape[1]
    gu = h @ w_in
    a, u = gu[..., :D_FF], gu[..., D_FF:]
    a_ext = jnp.concatenate([state.astype(a.dtype), a], axis=1)
    c = conv_b
    for j in range(CONV_W):
        c = c + a_ext[:, j:j + T] * conv_w[j]
    y = (jax.nn.silu(c) * u) @ w_down
    return y, a_ext[:, -(CONV_W - 1):]

def trunk(x, hg_state, conv_state, k_cache, v_cache, ki_cache,
          norm_mix, norm_ffn, norm_final, hg_w_in, hg_lb, hg_norm, hg_w_out,
          ds_w_in, ds_kln_w, ds_kln_b, ds_w_out, ffn_w_in, ffn_conv_w, ffn_conv_b, ffn_w_down):
    lower_bounds = jnp.cumsum(jax.nn.softmax(hg_lb.astype(F32), axis=0), axis=0)
    new_hg, new_conv, new_k, new_v, new_ki = [], [], [], [], []
    for i in range(DEPTH):
        j = i // N_MIXERS
        h = rms_norm(x, norm_mix[i])
        if i % N_MIXERS == 0:
            out, S = hgrn_mixer(h, hg_state[j], hg_w_in[j], lower_bounds[j], hg_norm[j], hg_w_out[j])
            new_hg.append(S)
        else:
            out, k, v, ki = dsa_mixer(h, k_cache[j], v_cache[j], ki_cache[j],
                                      ds_w_in[j], ds_kln_w[j], ds_kln_b[j], ds_w_out[j])
            new_k.append(k)
            new_v.append(v)
            new_ki.append(ki)
        x = x + out
        h = rms_norm(x, norm_ffn[i])
        out, cs = conv_ffn(h, conv_state[i], ffn_w_in[i], ffn_conv_w[i], ffn_conv_b[i], ffn_w_down[i])
        new_conv.append(cs)
        x = x + out
    y = rms_norm(x, norm_final)
    return (y, jnp.stack(new_hg), jnp.stack(new_conv),
            jnp.stack(new_k), jnp.stack(new_v), jnp.stack(new_ki))

def setup_inputs(seed: int = 0) -> dict:
    key = jax.random.key(seed)
    ks = jax.random.split(key, 22)

    def nrm(k, shape, scale):
        return jax.random.normal(k, shape, F32) * scale

    return {
        'x_prompt': nrm(ks[0], (BATCH, SEQ, D_MODEL), 1.0),
        'x_sample': nrm(ks[1], (DEC_BATCH, DEC_SEQ, D_MODEL), 1.0),
        'cache_k': nrm(ks[2], (N_DSA_LAYERS, DEC_BATCH, PAST_LEN, N_KV_HEADS, HEAD_DIM), 1.0),
        'cache_v': nrm(ks[3], (N_DSA_LAYERS, DEC_BATCH, PAST_LEN, N_KV_HEADS, HEAD_DIM), 1.0),
        'cache_kidx': nrm(ks[4], (N_DSA_LAYERS, DEC_BATCH, PAST_LEN, IDX_DIM), 1.0),
        'state_hgrn': nrm(ks[5], (N_HGRN_LAYERS, DEC_BATCH, HG_HEADS, HG_KDIM, HG_VDIM), 0.5),
        'state_conv': nrm(ks[6], (DEPTH, DEC_BATCH, CONV_W - 1, D_FF), 1.0),
        'norm_mix': 1.0 + nrm(ks[7], (DEPTH, D_MODEL), 0.02),
        'norm_ffn': 1.0 + nrm(ks[8], (DEPTH, D_MODEL), 0.02),
        'norm_final': 1.0 + nrm(ks[9], (D_MODEL,), 0.02),
        'hg_w_in': nrm(ks[10], (N_HGRN_LAYERS, D_MODEL, HG_IN), D_MODEL ** -0.5),
        'hg_lb': nrm(ks[11], (N_HGRN_LAYERS + 1, HG_FDIM), 0.1),
        'hg_norm': 1.0 + nrm(ks[12], (N_HGRN_LAYERS, HG_VDIM), 0.02),
        'hg_w_out': nrm(ks[13], (N_HGRN_LAYERS, D_MODEL, D_MODEL), D_MODEL ** -0.5),
        'ds_w_in': nrm(ks[14], (N_DSA_LAYERS, D_MODEL, DSA_IN), D_MODEL ** -0.5),
        'ds_kln_w': 1.0 + nrm(ks[15], (N_DSA_LAYERS, IDX_DIM), 0.02),
        'ds_kln_b': nrm(ks[16], (N_DSA_LAYERS, IDX_DIM), 0.02),
        'ds_w_out': nrm(ks[17], (N_DSA_LAYERS, N_HEADS * HEAD_DIM, D_MODEL), (N_HEADS * HEAD_DIM) ** -0.5),
        'ffn_w_in': nrm(ks[18], (DEPTH, D_MODEL, 2 * D_FF), D_MODEL ** -0.5),
        'ffn_conv_w': nrm(ks[19], (DEPTH, CONV_W, D_FF), CONV_W ** -0.5),
        'ffn_conv_b': nrm(ks[20], (DEPTH, D_FF), 0.02),
        'ffn_w_down': nrm(ks[21], (DEPTH, D_FF, D_MODEL), D_FF ** -0.5),
    }

def reference(x_prompt, x_sample, cache_k, cache_v, cache_kidx, state_hgrn, state_conv,
              norm_mix, norm_ffn, norm_final, hg_w_in, hg_lb, hg_norm, hg_w_out,
              ds_w_in, ds_kln_w, ds_kln_b, ds_w_out, ffn_w_in, ffn_conv_w, ffn_conv_b, ffn_w_down):
    run = functools.partial(
        trunk, norm_mix=norm_mix, norm_ffn=norm_ffn, norm_final=norm_final,
        hg_w_in=hg_w_in, hg_lb=hg_lb, hg_norm=hg_norm, hg_w_out=hg_w_out,
        ds_w_in=ds_w_in, ds_kln_w=ds_kln_w, ds_kln_b=ds_kln_b, ds_w_out=ds_w_out,
        ffn_w_in=ffn_w_in, ffn_conv_w=ffn_conv_w, ffn_conv_b=ffn_conv_b, ffn_w_down=ffn_w_down)
    b = x_prompt.shape[0]
    dt = x_prompt.dtype
    hg0 = jnp.zeros((N_HGRN_LAYERS, b, HG_HEADS, HG_KDIM, HG_VDIM), dt)
    conv0 = jnp.zeros((DEPTH, b, CONV_W - 1, D_FF), dt)
    k0 = jnp.zeros((N_DSA_LAYERS, b, 0, N_KV_HEADS, HEAD_DIM), dt)
    v0 = jnp.zeros((N_DSA_LAYERS, b, 0, N_KV_HEADS, HEAD_DIM), dt)
    ki0 = jnp.zeros((N_DSA_LAYERS, b, 0, IDX_DIM), dt)
    y_prompt, hg_p, conv_p, k_p, v_p, ki_p = run(x_prompt, hg0, conv0, k0, v0, ki0)
    y_sample, hg_s, conv_s, k_s, v_s, ki_s = run(x_sample, state_hgrn, state_conv, cache_k, cache_v, cache_kidx)
    return (y_prompt, y_sample, k_p, v_p, ki_p, hg_p, conv_p, k_s, v_s, ki_s, hg_s, conv_s)


_drawn_inputs = setup_inputs


def setup_inputs(seed=0):
    import zlib

    import numpy as np

    out = dict(_drawn_inputs(seed))
    spreads = {}
    factors = {'norm_final': 23.023,
     'hg_norm': 10.926,
     'ds_kln_w': 26.891,
     'ffn_conv_b': 3.391,
     'norm_ffn': 2.706,
     'ds_kln_b': 21.051,
     'cache_k': 5.077,
     'cache_v': 3.984,
     'cache_kidx': 4.284,
     'ds_w_out': 3.069}
    for name, (base, spread) in spreads.items():
        noise = np.random.default_rng([zlib.crc32(name.encode()), seed]).standard_normal(out[name].shape)
        drawn = base * np.exp(spread * noise) if base else spread * noise
        out[name] = __import__('jax').numpy.asarray(drawn.astype(out[name].dtype))
    for name, factor in factors.items():
        out[name] = (out[name] * factor).astype(out[name].dtype)
    return out
```

```python
from contextlib import ExitStack

import numpy as np

import concourse.bass as bass
from concourse import mybir

ALU = mybir.AluOpType
ACT = mybir.ActivationFunctionType
AX = mybir.AxisListType
F32 = mybir.dt.float32
F32R = mybir.dt.float32r
BF16 = mybir.dt.bfloat16

P = 128
EPS = 1e-6
D = 1024
KB = D // P
T_PROMPT = 1024
DEC_B = 8
DEC_T = 16
T_SAMPLE = DEC_B * DEC_T
T = T_PROMPT + T_SAMPLE
NT = T // P
PT = NT - 1
G = 3
GT = T // G
SLAB = KB * P
PAST = 2048
HEADS = 8
CH = 64
NC = T_PROMPT // CH
SB = 16
NS = CH // SB
NCH = NC + DEC_B
CLAMP = 1e18
D_FF = 2816
FB = D_FF // P
CONV_W = 3
BANK = 512
NEG = -1e30


def hold(eng, sem, value, tick):
    if isinstance(value, int):
        if value > 0:
            eng.wait_ge(sem, value)
    else:
        eng.wait_ge(sem, value)
        eng.sem_inc(tick, 1)


class Space:

    def __init__(self, nc, at, end):
        self.nc, self.at, self.end = nc, at, end

    def take(self, name, shape, dtype=F32, at=None):
        size = int(np.prod(shape[1:])) * (2 if dtype == BF16 else 4)
        size = (size + 31) // 32 * 32
        if at is None:
            at = self.at
            self.at += size
            assert self.at <= self.end, (name, self.at - self.end)
        t = self.nc.alloc_sbuf_tensor_at(name, list(shape), dtype, offset=at)
        t_at[name] = at
        return t


t_at = {}


class Norm:

    R = 3

    def __init__(self, env, nth, x, gain, ones, h_hi, h_lo, sq, std, t, banks):
        self.x, self.gain, self.ones, self.h_hi, self.h_lo = x, gain, ones, h_hi, h_lo
        self.sq, self.std, self.t, self.banks = sq, std, t, banks
        self.squared, self.summed, self.rooted, self.scaled, self.hi_done, self.lo_done = env["norm_sems"]
        self.blocks, self.groups = nth * G * KB, nth * G

    def squares(self, act, g):
        for kb in range(KB):
            u = g * KB + kb
            if u >= self.R:
                act.wait_ge(self.summed, self.blocks + u - self.R + 1)
            act.activation(self.sq[:, u % self.R], self.x[:, kb, g * GT:(g + 1) * GT], ACT.Square).then_inc(self.squared, 1)

    def roots(self, act, g):
        act.wait_ge(self.summed, self.blocks + (g + 1) * KB)
        act.activation(self.std[:, g], self.banks[g][:, 0:GT], ACT.Sqrt, bias=EPS).then_inc(self.rooted, 1)

    def his(self, act, g):
        for kb in range(KB):
            u = g * KB + kb
            act.wait_ge(self.scaled, self.blocks + u + 1)
            act.activation(self.h_hi[:, kb, g * GT:(g + 1) * GT], self.t[:, u % self.R], ACT.Copy).then_inc(self.hi_done, 1)

    def wait_group(self, eng, g):
        eng.wait_ge(self.lo_done, self.blocks + (g + 1) * KB)

    def on_scalar(self, act):
        self.squares(act, 0)
        self.squares(act, 1)
        self.roots(act, 0)
        self.his(act, 0)
        self.squares(act, 2)
        self.roots(act, 1)
        self.his(act, 1)
        self.roots(act, 2)
        self.his(act, 2)

    def on_tensor(self, pe):
        for u in range(G * KB):
            pe.wait_ge(self.squared, self.blocks + u + 1)
            pe.matmul(self.banks[u // KB][:, 0:GT], self.ones[:, :], self.sq[:, u % self.R], start=u % KB == 0,
                      stop=u % KB == KB - 1).then_inc(self.summed, 1)

    def on_vector(self, dve):
        def low(u):
            g, kb = divmod(u, KB)
            dve.wait_ge(self.hi_done, self.blocks + u + 1)
            dve.tensor_tensor(self.h_lo[:, kb, g * GT:(g + 1) * GT], self.t[:, u % self.R],
                              self.h_hi[:, kb, g * GT:(g + 1) * GT].bitcast(F32), ALU.subtract).then_inc(self.lo_done, 1)

        for g in range(G):
            dve.wait_ge(self.rooted, self.groups + g + 1)
            dve.reciprocal(self.std[:, g], self.std[:, g])
            dve.drain()
            for kb in range(KB):
                u = g * KB + kb
                if u >= 2:
                    low(u - 2)
                if u >= self.R:
                    dve.wait_ge(self.lo_done, self.blocks + u - self.R + 1)
                dve.scalar_tensor_tensor(self.t[:, u % self.R], self.x[:, kb, g * GT:(g + 1) * GT], self.gain[:, kb:kb + 1],
                                         self.std[:, g], ALU.mult, ALU.mult).then_inc(self.scaled, 1)
        low(G * KB - 2)
        low(G * KB - 1)


class Slabs:

    def __init__(self, nc, sem, tag, weights, first, n, ring, raw, hi, lo, tick):
        self.weights, self.first, self.n, self.ring = weights, first, n, ring
        self.raw, self.hi, self.lo, self.tick = raw, hi, lo, tick
        self.loaded = [sem(f"{tag}_loaded{k}") for k in range(2)]
        self.hi_done = sem(tag + "_w_hi")
        self.lo_done = sem(tag + "_w_lo")
        self.units = sem(tag + "_units")

    def load_all(self, sp):
        for s in range(2):
            sp.dma_start(self.raw[:, s], self.weights[self.first + s]).then_inc(self.loaded[s], 16)
        with sp.Fori(1, self.n // 2) as m:
            for par in range(2):
                hold(sp, self.lo_done, m * 2 + par - 1, self.tick["sp"])
                sp.dma_start(self.raw[:, par], self.weights[m * 2 + (self.first + par)]).then_inc(self.loaded[par], 16)
        if self.n % 2:
            s = self.n - 1
            sp.wait_ge(self.lo_done, s - 1)
            sp.dma_start(self.raw[:, 0], self.weights[self.first + s]).then_inc(self.loaded[0], 16)

    def split_hi(self, act, s, half, slot, par, used):
        hold(act, self.loaded[par], (half + 1) * 16, self.tick["act"])
        hold(act, self.units, used, self.tick["act"])
        act.activation(self.hi[:, slot], self.raw[:, par], ACT.Copy).then_inc(self.hi_done, 1)

    def split_lo(self, dve, s, slot, par):
        hold(dve, self.hi_done, s + 1, self.tick["dve"])
        dve.tensor_tensor(self.lo[:, slot], self.raw[:, par], self.hi[:, slot].bitcast(F32),
                          ALU.subtract).then_inc(self.lo_done, 1)

    def product(self, pe, out, slot, col, x_hi, x_lo, start, stop):
        w_hi, w_lo = self.hi[:, slot, col:col + P], self.lo[:, slot, col:col + P]
        pe.matmul(out, w_hi, x_hi, start=start, stop=False)
        pe.matmul(out, w_hi, x_lo, start=False, stop=False)
        return pe.matmul(out, w_lo, x_hi, start=False, stop=stop)

    def block(self, pe, out, slot, h_hi, h_lo, g):
        for kb in range(KB):
            last = self.product(pe, out, slot, kb * P, h_hi[:, kb, g * GT:(g + 1) * GT], h_lo[:, kb, g * GT:(g + 1) * GT],
                                kb == 0, kb == KB - 1)
        return last

    def tokens(self, pe, out, slot, cols, h_hi, h_lo, tile):
        for kb in range(KB):
            w_hi, w_lo = self.hi[:, slot, kb * P:kb * P + cols], self.lo[:, slot, kb * P:kb * P + cols]
            x_hi, x_lo = h_hi[:, kb, tile * P:(tile + 1) * P], h_lo[:, kb, tile * P:(tile + 1) * P]
            pe.matmul(out, x_hi, w_hi, start=kb == 0, stop=False)
            pe.matmul(out, x_lo, w_hi, start=False, stop=False)
            last = pe.matmul(out, x_hi, w_lo, start=False, stop=kb == KB - 1)
        return last


def pieces(n):
    return [(a, min(a + BANK, n)) for a in range(0, n, BANK)]


def spread(ap, shape):
    return ap.broadcast_to(shape)


def hgrn_phase(nc, env, x):
    io, const, sem, tick = env["io"], env["const"], env["sem"], env["tick"]
    sp_ = Space(nc, env["free"], env["end"])
    take = sp_.take
    h_hi, h_lo = take("hg_h_hi", [P, KB, T], F32R), take("hg_h_lo", [P, KB, T], F32R)
    raw = take("hg_raw", [P, 2, SLAB])
    w_hi, w_lo = take("hg_w_hi", [P, 2, SLAB], F32R), take("hg_w_lo", [P, 2, SLAB], F32R)
    decay = take("hg_G", [P, T])
    tmp1, tmp2 = take("hg_tmp1", [P, T]), take("hg_tmp2", [P, T])
    q_dec = take("hg_q_dec", [P, T])
    q_mid = take("hg_q_mid", [P, T])
    k_end = take("hg_k_end", [P, T])
    k_endT = take("hg_k_endT", [P, NT, P])
    vals = take("hg_v", [P, NT, P])
    gate = take("hg_gate", [P, T])
    attT = take("hg_attT", [P, PT * CH])
    attTs = take("hg_attTs", [P, P])
    k_mid = take("hg_k_mid", [P, NC * SB * NS * (NS + 1) // 2])
    states = take("hg_states", [P, NC, P], at=t_at["hg_k_mid"])
    k_mids = take("hg_k_mids", [P, T_SAMPLE])
    v_own = take("hg_v_own", [P, DEC_B, P])
    s_new = take("hg_s_new", [P, DEC_B, P], at=t_at["hg_v_own"])
    s_old = take("hg_s_old", [P, DEC_B, P])
    o_hi, o_lo = take("hg_o_hi", [P, T], F32R), take("hg_o_lo", [P, T], F32R)
    keep = take("hg_keep", [P, T], BF16)
    e_end = take("hg_e_end", [P, NCH])
    tri, own = take("hg_tri", [P, CH]), take("hg_own", [P, P])
    own_b = take("hg_own_b", [P, DEC_B])
    lbs = take("hg_lbs", [P, 2, HEADS, 1])
    small = take("hg_small", [P, KB + 1])
    lb_t = take("hg_lb_t", [P, 2, HEADS, 1])
    sq = take("hg_sq", [P, Norm.R, GT], at=t_at["hg_k_endT"])
    std = take("hg_std", [P, G, GT], at=t_at["hg_o_hi"])
    nt = take("hg_nt", [P, Norm.R, GT], at=t_at["hg_o_lo"])

    with ExitStack() as ctx:
        lin = [ctx.enter_context(nc.psum_tensor(f"hg_lin{g}", [P, BANK], F32)) for g in range(G)]
        rb = [ctx.enter_context(nc.psum_tensor(f"hg_rec{g}", [P, BANK], F32)) for g in range(5)]
        W = Slabs(nc, sem, "hg", io["weights"], 0, 40, 2, raw, w_hi, w_lo, tick)
        N = Norm(env, 0, x, small, const["ones"], h_hi, h_lo, sq, std, nt, lin)
        consts_in, x_in = sem("hg_consts_in"), env["x_in"]
        lb_ready = sem("hg_lb_ready")
        act_evac, dve_evac = sem("hg_act_evac"), sem("hg_dve_evac")
        f_act, f_dve = sem("hg_f_act"), sem("hg_f_dve")
        q_act, q_dve = sem("hg_q_act"), sem("hg_q_dve")
        turned, turned_out = sem("hg_turned"), sem("hg_turned_out")
        att_done, att_masked = sem("hg_att_done"), sem("hg_att_masked")
        v_spread = sem("hg_v_spread")
        ds_done, chained = sem("hg_ds_done"), sem("hg_chained")
        o_done, ss_done = sem("hg_o_done"), sem("hg_ss_done")
        n_act, n_dve = sem("hg_n_act"), sem("hg_n_dve")
        s_in, sp_out, ss_out = sem("hg_s_in"), sem("hg_sp_out"), sem("hg_ss_out")
        gated = sem("hg_gated")
        block = ctx.enter_context(nc.Block())

        def k_at(i):
            return NC * SB * i * (i + 1) // 2

        def ds_at(c):
            return rb[c % 2 * 2 + c // 8][:, c // 2 % 4 * P:(c // 2 % 4 + 1) * P]

        def o_parts(buf):
            chunks = buf[:, 0:T_PROMPT].rearrange("p (c two t) -> p c two t", two=2, t=CH)
            banks = [(chunks[:, :, n], rb[1 + n][:, :].rearrange("p (c t) -> p c t", t=CH)) for n in range(2)]
            return banks + [(buf[:, T_PROMPT:T], rb[3][:, 0:T_SAMPLE])]

        def units_before(h):
            if isinstance(h, int) and h == HEADS + 1:
                return units_before(HEADS) + 24
            return 12 * h if isinstance(h, int) and h < 2 else (h - 2) * 36 + 24

        def slab_base(h):
            if isinstance(h, int) and h == HEADS + 1:
                return slab_base(HEADS) + 1
            return 4 * h if isinstance(h, int) and h < 2 else (h - 2) * 5 + 8

        def body_slabs(h):
            out_p = isinstance(h, int) and h < 2
            return 0 if out_p else 1

        @block.sync
        def _(sp):
            sp.dma_start(tri[:, :], io["tri"]).then_inc(consts_in, 16)
            sp.dma_start(own[:, :], io["own"]).then_inc(consts_in, 16)
            sp.dma_start(own_b[:, :], io["own_b"]).then_inc(consts_in, 16)
            sp.dma_start(keep[:, :], io["keep"]).then_inc(consts_in, 16)
            sp.dma_start(lbs[:, :, :, :], io["hg_lb"]).then_inc(consts_in, 16)
            sp.dma_start(small[:, 0:KB], io["gains"][0]).then_inc(consts_in, 16)
            sp.dma_start(small[:, KB:KB + 1], io["hg_norm"]).then_inc(consts_in, 16)
            W.load_all(sp)

        @block.gpsimd
        def _(pool):
            pool.dma_start(s_old[:, :, :], io["state_hgrn"][0]).then_inc(s_in, 16)

            def states_out(r):
                hold(pool, chained, r * 2 + 1, tick["pool"])
                pool.dma_start(io["hgrn_p"][r], states[:, NC - 1]).then_inc(sp_out, 16)
                hold(pool, chained, r * 2 + 2, tick["pool"])
                pool.dma_start(io["hgrn_s"][r], s_new[:, :, :]).then_inc(ss_out, 16)

            with pool.Fori(0, HEADS - 1) as r:
                states_out(r)
                hold(pool, o_done, r + 1, tick["pool"])
                pool.dma_start(s_old[:, :, :], io["state_hgrn"][r + 1]).then_inc(s_in, 16)
            states_out(HEADS - 1)
            pool.wait_ge(sp_out, 16 * HEADS)
            pool.wait_ge(ss_out, 16 * HEADS)

        def split_used(h, k):
            first = units_before(h)
            outp = 24 if body_slabs(h) else 0
            if k == 0:
                return first
            if k == 1:
                return first + outp
            return first + outp + 3 * (k - 1)

        def slab_no(h, k):
            return slab_base(h) + body_slabs(h) + k

        def pars(first_par, h, k):
            return (first_par + body_slabs(h) + k) % 2

        def half(h, par0, k):
            off = body_slabs(h) + k
            if isinstance(h, int):
                return (slab_base(h) + off) // 2
            m, odd = loop_m[0]
            return m * 5 + ((13 if odd else 8) + off) // 2

        loop_m = [None]

        def over_bodies(eng, body):
            body(0, 0)
            body(1, 0)
            with eng.Fori(0, 3) as m:
                loop_m[0] = (m, 0)
                body(m * 2 + 2, 0)
                loop_m[0] = (m, 1)
                body(m * 2 + 3, 1)
            body(8, 0)
            body(9, 1)

        def has(h, low, high):
            return not isinstance(h, int) or low <= h < high

        @block.scalar
        def _(act):
            act.wait_ge(x_in, 16)
            act.wait_ge(consts_in, 16 * 7)
            N.on_scalar(act)
            act.activation(lb_t[:, :, :, :], lbs[:, :, :, :], ACT.Exp).then_inc(lb_ready, 1)
            tk = tick["act"]

            def hi(h, par0, k):
                s, par = slab_no(h, k), pars(par0, h, k)
                W.split_hi(act, s, half(h, par0, k), par, par, split_used(h, k))

            def body(h, par0):
                r = h - 1
                if has(h, 1, 9):
                    hold(act, turned, r + 1, tk)
                    for n, (a, b) in enumerate(pieces(T)):
                        i = act.activation(k_endT[:, a // P:b // P, :], rb[n][:, 0:b - a], ACT.Copy)
                    i.then_inc(turned_out, 1)
                if isinstance(h, int) and h == 8:
                    W.split_hi(act, 39, 19, 1, 1, units_before(8))
                if has(h, 0, 8):
                    if body_slabs(h):
                        hi(h, par0, 0)
                    hi(h, par0, 1)
                    base = units_before(h) + (24 if body_slabs(h) else 0)
                    hold(act, gated, h, tk)
                    for g in range(G):
                        hold(act, W.units, base + g + 1, tk)
                        act.activation(tmp1[:, g * GT:(g + 1) * GT], lin[g][:, 0:GT], ACT.Exp, scale=-1.0).then_inc(act_evac, 1)
                    hold(act, f_dve, h * 4 + 1, tk)
                    act.activation(tmp1[:, :], tmp2[:, :], ACT.Ln).then_inc(f_act, 1)
                    hi(h, par0, 2)
                    hold(act, f_dve, h * 4 + 2, tk)
                    act.activation(e_end[:, 0:NC], decay[:, CH - 1:T_PROMPT:CH], ACT.Exp)
                    act.activation(e_end[:, NC:NCH], decay[:, T_PROMPT + DEC_T - 1:T:DEC_T], ACT.Exp)
                    hold(act, f_dve, h * 4 + 3, tk)
                    act.activation(k_mid[:, :], k_mid[:, :], ACT.Exp)
                    act.activation(k_mids[:, :], k_mids[:, :], ACT.Exp).then_inc(f_act, 1)
                    act.activation(k_end[:, :], k_end[:, :], ACT.Exp).then_inc(f_act, 1)
                if has(h, 1, 9):
                    if has(h, 1, 8):
                        hold(act, f_dve, h * 4 + 4, tk)
                    hold(act, o_done, r + 1, tk)
                    for dst, src in o_parts(tmp1):
                        i = act.activation(dst, src, ACT.Square)
                    i.then_inc(n_act, 1)
                if has(h, 0, 8):
                    for g in range(G):
                        hold(act, W.units, base + 3 + g + 1, tk)
                        act.activation(vals[:, 3 * g:3 * g + 3, :], lin[g][:, 0:GT], ACT.Copy).then_inc(act_evac, 1)
                    hi(h, par0, 3)
                if has(h, 1, 9):
                    hold(act, ss_done, r + 1, tk)
                    for (a, b), src in zip(pieces(T), (rb[0][:, :], rb[4][:, :], rb[3][:, P:2 * P])):
                        i = act.activation(tmp2[:, a:b], src, ACT.Sqrt, bias=EPS)
                    i.then_inc(n_act, 1)
                    hold(act, n_dve, r * 2 + 1, tk)
                    if has(h, 2, 9):
                        hold(act, W.units, units_before(h) + 24, tk)
                    act.activation(o_hi[:, :], tmp1[:, :], ACT.Copy).then_inc(n_act, 1)
                if has(h, 0, 8):
                    hold(act, f_dve, h * 4 + 4, tk)
                    for g in range(G):
                        hold(act, W.units, base + 6 + g + 1, tk)
                        act.activation(q_dec[:, g * GT:(g + 1) * GT], lin[g][:, 0:GT], ACT.Copy)
                        act.activation(q_mid[:, g * GT:(g + 1) * GT], lin[g][:, 0:GT], ACT.Exp, scale=-1.0).then_inc(act_evac, 1)
                    hi(h, par0, 4)
                    hold(act, q_dve, h * 2 + 1, tk)
                    act.activation(tmp1[:, :], tmp1[:, :], ACT.Exp)
                    act.activation(tmp2[:, :], decay[:, :], ACT.Exp).then_inc(q_act, 1)
                    hold(act, q_dve, h * 2 + 2, tk)
                    for g in range(G):
                        hold(act, W.units, base + 9 + g + 1, tk)
                        act.activation(gate[:, g * GT:(g + 1) * GT], lin[g][:, 0:GT], ACT.Copy)
                        act.activation(tmp1[:, g * GT:(g + 1) * GT], lin[g][:, 0:GT], ACT.Exp, scale=-1.0).then_inc(act_evac, 1)
            W.split_hi(act, 0, 0, 0, 0, 0)
            over_bodies(act, body)

        @block.vector
        def _(dve):
            tk = tick["dve"]
            dve.wait_ge(x_in, 16)
            dve.wait_ge(consts_in, 16 * 7)
            N.on_vector(dve)
            dve.wait_ge(lb_ready, 1)
            dve.tensor_tensor(lbs[:, 0], lb_t[:, 0], lb_t[:, 1], ALU.add)
            dve.drain()
            dve.reciprocal(lbs[:, 1], lbs[:, 0])
            dve.drain()
            dve.tensor_tensor(lbs[:, 0], lb_t[:, 0], lbs[:, 1], ALU.mult)
            dve.drain()
            dve.tensor_scalar(lbs[:, 1], lbs[:, 0], -1.0, 1.0, ALU.mult, ALU.add)
            dve.memset(attT[:, :], 0.0)
            dve.drain()

            def lo(h, par0, k):
                par = pars(par0, h, k)
                W.split_lo(dve, slab_no(h, k), par, par)

            def body(h, par0):
                r = h - 1
                if has(h, 1, 9):
                    hold(dve, att_done, r + 1, tk)
                    for half_ in range(2):
                        for i in range(NS):
                            rows = slice(half_ * CH, half_ * CH + SB * (i + 1))
                            dst = attT[rows, :].rearrange("p (c t) -> p c t", t=CH)[:, :, i * SB:(i + 1) * SB]
                            src = rb[3][rows, :].rearrange("p (c t) -> p c t", t=CH)[:, :, i * SB:(i + 1) * SB]
                            dve.tensor_tensor(dst, src, spread(tri[rows, i * SB:(i + 1) * SB].unsqueeze(1), dst.shape), ALU.mult)
                    dve.tensor_tensor(attTs[:, :], rb[4][:, 0:P], own[:, :], ALU.mult).then_inc(att_masked, 1)
                    hold(dve, ss_out, r * 16, tk)
                    dve.tensor_tensor(v_own[:, :, :], spread(vals[:, NT - 1, :].unsqueeze(1), [P, DEC_B, P]),
                                      spread(own_b[:, :].unsqueeze(2), [P, DEC_B, P]), ALU.mult).then_inc(v_spread, 1)
                if has(h, 0, 8) and body_slabs(h):
                    lo(h, par0, 0)
                if isinstance(h, int) and h == 8:
                    W.split_lo(dve, 39, 1, 1)
                if has(h, 2, 10):
                    dve.drain()
                    for nb in range(KB):
                        for g in range(G):
                            hold(dve, W.units, units_before(h) + nb * G + g + 1, tk)
                            xs = x[:, nb, g * GT:(g + 1) * GT]
                            dve.tensor_tensor(xs, xs, lin[g][:, 0:GT], ALU.add).then_inc(dve_evac, 1)
                if has(h, 1, 9):
                    hold(dve, ds_done, r * 3 + 1, tk)
                    dve.tensor_copy(states[:, 0], rb[0][:, 0:P])
                    for c in range(1, NC):
                        dve.drain()
                        i = dve.scalar_tensor_tensor(states[:, c], states[:, c - 1], e_end[:, c:c + 1],
                                                     ds_at(c), ALU.mult, ALU.add)
                    i.then_inc(chained, 1)
                    hold(dve, ds_done, r * 3 + 3, tk)
                    hold(dve, s_in, (r + 1) * 16, tk)
                    for b in range(DEC_B):
                        i = dve.scalar_tensor_tensor(s_new[:, b], s_old[:, b], e_end[:, NC + b:NC + b + 1],
                                                     (rb[4] if b < 4 else rb[0])[:, b % 4 * P:(b % 4 + 1) * P], ALU.mult, ALU.add)
                    i.then_inc(chained, 1)
                if has(h, 0, 8):
                    lo(h, par0, 1)
                    hold(dve, act_evac, h * 12 + 3, tk)
                    dve.tensor_scalar(tmp1[:, :], tmp1[:, :], 1.0, None, ALU.add)
                    dve.drain()
                    dve.reciprocal(tmp1[:, :], tmp1[:, :])
                    dve.drain()
                    dve.tensor_scalar(tmp2[:, :], tmp1[:, :], lb_col(1), lb_col(0), ALU.mult, ALU.add).then_inc(f_dve, 1)
                    dve.drain()
                    dve.tensor_scalar(q_mid[:, :], tmp2[:, :], -1.0, 1.0, ALU.mult, ALU.add)
                    lo(h, par0, 2)
                    hold(dve, f_act, h * 3 + 1, tk)
                    dve.tensor_tensor_scan(decay[:, :], keep[:, :], tmp1[:, :], 0.0, ALU.mult, ALU.add).then_inc(f_dve, 1)
                    dve.drain()
                    if has(h, 1, 8):
                        hold(dve, o_done, r + 1, tk)
                        hold(dve, sp_out, (r + 1) * 16, tk)
                    gp = decay[:, 0:T_PROMPT].rearrange("p (c t) -> p c t", t=CH)
                    for i in range(NS):
                        n = SB * (i + 1)
                        km = k_mid[:, k_at(i):k_at(i + 1)].rearrange("p (c t) -> p c t", t=n)
                        mid = i * SB + SB // 2 - 1
                        dve.tensor_tensor(km, spread(gp[:, :, mid:mid + 1], [P, NC, n]), gp[:, :, 0:n], ALU.subtract)
                    gs = decay[:, T_PROMPT:T].rearrange("p (b t) -> p b t", t=DEC_T)
                    mid = SB // 2 - 1
                    kms = k_mids[:, :].rearrange("p (b t) -> p b t", t=DEC_T)
                    dve.tensor_tensor(kms, spread(gs[:, :, mid:mid + 1], [P, DEC_B, DEC_T]), gs, ALU.subtract)
                    ke = k_end[:, 0:T_PROMPT].rearrange("p (c t) -> p c t", t=CH)
                    dve.tensor_tensor(ke, spread(gp[:, :, CH - 1:CH], [P, NC, CH]), gp, ALU.subtract)
                    kes = k_end[:, T_PROMPT:T].rearrange("p (b t) -> p b t", t=DEC_T)
                    dve.tensor_tensor(kes, spread(gs[:, :, DEC_T - 1:DEC_T], [P, DEC_B, DEC_T]), gs, ALU.subtract).then_inc(f_dve, 1)
                    hold(dve, f_act, h * 3 + 2, tk)
                    kp = q_mid[:, 0:T_PROMPT].rearrange("p (c t) -> p c t", t=CH)
                    for i in range(NS):
                        n = SB * (i + 1)
                        km = k_mid[:, k_at(i):k_at(i + 1)].rearrange("p (c t) -> p c t", t=n)
                        dve.scalar_tensor_tensor(km, km, CLAMP, kp[:, :, 0:n], ALU.min, ALU.mult)
                    dve.scalar_tensor_tensor(k_mids[:, :], k_mids[:, :], CLAMP, q_mid[:, T_PROMPT:T], ALU.min, ALU.mult)
                    hold(dve, f_act, h * 3 + 3, tk)
                    dve.tensor_tensor(k_end[:, :], k_end[:, :], q_mid[:, :], ALU.mult).then_inc(f_dve, 1)
                    lo(h, par0, 3)
                if has(h, 1, 9):
                    hold(dve, n_act, r * 3 + 2, tk)
                    dve.reciprocal(tmp2[:, :], tmp2[:, :])
                    dve.drain()
                    for (dst, src), (scale, _) in zip(o_parts(tmp1), o_parts(tmp2)):
                        dve.scalar_tensor_tensor(dst, src, small[:, KB:KB + 1], scale, ALU.mult, ALU.mult)
                    dve.drain()
                    dve.tensor_tensor(tmp1[:, :], tmp1[:, :], gate[:, :], ALU.mult).then_inc(n_dve, 1)
                    hold(dve, n_act, r * 3 + 3, tk)
                    dve.tensor_tensor(o_lo[:, :], tmp1[:, :], o_hi[:, :].bitcast(F32), ALU.subtract).then_inc(n_dve, 1)
                if has(h, 0, 8):
                    hold(dve, act_evac, h * 12 + 9, tk)
                    dve.tensor_scalar(q_mid[:, :], q_mid[:, :], 1.0, None, ALU.add)
                    dve.drain()
                    dve.reciprocal(q_mid[:, :], q_mid[:, :])
                    dve.drain()
                    dve.tensor_tensor(q_dec[:, :], q_dec[:, :], q_mid[:, :], ALU.mult)
                    g16 = decay[:, :].rearrange("p (n t) -> p n t", t=SB)
                    dve.tensor_tensor(tmp1[:, :].rearrange("p (n t) -> p n t", t=SB), g16,
                                      spread(g16[:, :, SB // 2 - 1:SB // 2], [P, T // SB, SB]), ALU.subtract).then_inc(q_dve, 1)
                    lo(h, par0, 4)
                    hold(dve, q_act, h + 1, tk)
                    dve.scalar_tensor_tensor(q_mid[:, :], tmp1[:, :], CLAMP, q_dec[:, :], ALU.min, ALU.mult)
                    dve.drain()
                    dve.tensor_tensor(q_dec[:, :], q_dec[:, :], tmp2[:, :], ALU.mult).then_inc(q_dve, 1)
                    hold(dve, act_evac, h * 12 + 12, tk)
                    dve.tensor_scalar(tmp1[:, :], tmp1[:, :], 1.0, None, ALU.add)
                    dve.drain()
                    dve.reciprocal(tmp1[:, :], tmp1[:, :])
                    dve.drain()
                    dve.tensor_tensor(gate[:, :], gate[:, :], tmp1[:, :], ALU.mult).then_inc(gated, 1)

            def lb_col(which):
                h = cur[0]
                return lbs[:, which, h]

            cur = [0]

            def body_(h, par0):
                cur[0] = h
                body(h, par0)

            W.split_lo(dve, 0, 0, 0)
            over_bodies(dve, body_)
            dve.drain()

        @block.tensor
        def _(pe):
            tk = tick["pe"]
            ident = const["ident"]
            N.on_tensor(pe)

            def body(h, par0):
                r = h - 1
                has_out = body_slabs(h)
                first = units_before(h)
                if has(h, 1, 9):
                    hold(pe, f_dve, r * 4 + 4, tk)
                    hold(pe, q_dve, r * 2 + 2, tk)
                    for t in range(NT):
                        i = pe.transpose(rb[t // 4][:, t % 4 * P:(t % 4 + 1) * P], k_end[:, t * P:(t + 1) * P], ident[:, :])
                    i.then_inc(turned, 1)
                    for c in range(NC):
                        rows, col = c % 2 * CH, c // 2 * CH
                        for i_ in range(NS):
                            n = SB * (i_ + 1)
                            at = k_at(i_) + c * n
                            pe.matmul(rb[3][rows:rows + n, col + i_ * SB:col + (i_ + 1) * SB], k_mid[:, at:at + n],
                                      q_mid[:, c * CH + i_ * SB:c * CH + (i_ + 1) * SB], start=True, stop=True)
                    pe.matmul(rb[4][:, 0:P], k_mids[:, :], q_mid[:, T_PROMPT:T], start=True, stop=True).then_inc(att_done, 1)
                if has_out and has(h, 2, 10):
                    hold(pe, n_dve, (h - 2) * 2 + 2, tk)
                    hold(pe, W.lo_done, slab_base(h) + 1, tk)
                    for nb in range(KB):
                        for g in range(G):
                            n = nb * G + g
                            if n < G and has(h, 2, 9):
                                hold(pe, act_evac, h * 12 - 2 + n, tk)
                            else:
                                hold(pe, dve_evac, (h - 2) * 24 + n - 2, tk)
                            W.product(pe, lin[g][:, 0:GT], par0, nb * P, o_hi[:, g * GT:(g + 1) * GT],
                                      o_lo[:, g * GT:(g + 1) * GT], True, True).then_inc(W.units, 1)
                if has(h, 1, 9):
                    hold(pe, turned_out, r + 1, tk)
                    hold(pe, att_masked, r + 1, tk)
                    for c in range(NC):
                        rows = slice(c % 2 * CH, (c % 2 + 1) * CH)
                        i = pe.matmul(ds_at(c), k_endT[rows, c // 2, :], vals[rows, c // 2, :],
                                      start=True, stop=True)
                    i.then_inc(ds_done, 1)
                    hold(pe, v_spread, r + 1, tk)
                    pe.matmul(rb[4][:, :], k_endT[:, NT - 1, :], v_own[:, 0:4, :].rearrange("p b v -> p (b v)"),
                              start=True, stop=True).then_inc(ds_done, 1)
                if has(h, 0, 8):
                    hold(pe, W.lo_done, slab_no(h, 0) + 1, tk)
                    for g in range(G):
                        if isinstance(h, int) and h == 0:
                            N.wait_group(pe, g)
                        elif isinstance(h, int) and h == 1:
                            pe.wait_ge(act_evac, 12 - 2 + g)
                        else:
                            hold(pe, dve_evac, (h - 1) * 24 - 2 + g, tk)
                        W.block(pe, lin[g][:, 0:GT], pars(par0, h, 0), h_hi, h_lo, g).then_inc(W.units, 1)
                if has(h, 1, 9):
                    hold(pe, chained, r * 2 + 1, tk)
                    pe.matmul(rb[0][:, :], k_endT[:, NT - 1, :], v_own[:, 4:8, :].rearrange("p b v -> p (b v)"),
                              start=True, stop=True).then_inc(ds_done, 1)
                    for c in range(NC):
                        rows = slice(c % 2 * CH, (c % 2 + 1) * CH)
                        out = rb[1 + c % 2][:, c // 2 * CH:(c // 2 + 1) * CH]
                        pe.matmul(out, vals[rows, c // 2, :], attT[rows, c // 2 * CH:(c // 2 + 1) * CH], start=True, stop=c == 0)
                        if c:
                            pe.matmul(out, states[:, c - 1, :], q_dec[:, c * CH:(c + 1) * CH], start=False, stop=True)
                    pe.matmul(rb[3][:, 0:P], vals[:, NT - 1, :], attTs[:, :], start=True, stop=False)
                    hold(pe, s_in, (r + 1) * 16, tk)
                    for b in range(DEC_B):
                        i = pe.matmul(rb[3][:, b * DEC_T:(b + 1) * DEC_T], s_old[:, b, :],
                                      q_dec[:, T_PROMPT + b * DEC_T:T_PROMPT + (b + 1) * DEC_T], start=False, stop=b == DEC_B - 1)
                    i.then_inc(o_done, 1)
                if has(h, 0, 8):
                    hold(pe, W.lo_done, slab_no(h, 1) + 1, tk)
                    for g in range(G):
                        hold(pe, act_evac, h * 12 + g + 1, tk)
                        for tile in range(3):
                            i = W.tokens(pe, lin[g][:, tile * P:(tile + 1) * P], pars(par0, h, 1), P, h_hi, h_lo, 3 * g + tile)
                        i.then_inc(W.units, 1)
                if has(h, 1, 9):
                    hold(pe, n_act, r * 3 + 1, tk)
                    hold(pe, chained, r * 2 + 2, tk)
                    pe.matmul(rb[0][:, :], const["ones_v"][:, :], tmp1[:, 0:512], start=True, stop=True)
                    pe.matmul(rb[4][:, :], const["ones_v"][:, :], tmp1[:, 512:1024], start=True, stop=True)
                    pe.matmul(rb[3][:, P:2 * P], const["ones_v"][:, :], tmp1[:, 1024:T], start=True, stop=True).then_inc(ss_done, 1)
                for k in (2, 3):
                    if has(h, 0, 8):
                        hold(pe, W.lo_done, slab_no(h, k) + 1, tk)
                        for g in range(G):
                            hold(pe, act_evac, h * 12 + 3 * (k - 1) + g + 1, tk)
                            W.block(pe, lin[g][:, 0:GT], pars(par0, h, k), h_hi, h_lo, g).then_inc(W.units, 1)

            over_bodies(pe, body)


def in_slabs(w):
    k, n = w.shape
    return w.reshape(KB, P, n // P, P).transpose(2, 1, 0, 3).reshape(n // P, P, SLAB)


def down_slabs(w):
    return w.reshape(-1, P, SLAB)


def ffn_phase(nc, env, x, layer):
    io, const, sem, tick = env["io"], env["const"], env["sem"], env["tick"]
    tag = f"ff{layer}"
    sp_ = Space(nc, env["free"], env["end"])

    def take(name, shape, dtype=F32, at=None):
        return sp_.take(tag + name, shape, dtype, None if at is None else t_at[tag + at])

    RING = 3
    h_hi, h_lo = take("h_hi", [P, KB, T], F32R), take("h_lo", [P, KB, T], F32R)
    raw = take("raw", [P, 2, SLAB])
    w_hi, w_lo = take("w_hi", [P, RING, SLAB], F32R), take("w_lo", [P, RING, SLAB], F32R)
    W_EXT = CONV_W - 1
    SEQ_EXT = DEC_T + W_EXT
    ext_cols = W_EXT + T_PROMPT + DEC_B * SEQ_EXT
    a_ext = take("a_ext", [P, 2, ext_cols])
    conv = take("conv", [P, 2, T])
    y = take("y", [P, T])
    y_hi, y_lo = take("y_hi", [P, 4, T], F32R), take("y_lo", [P, 4, T], F32R)
    state = take("state", [P, FB, DEC_B, W_EXT])
    ends = take("ends", [P, FB, (1 + DEC_B) * W_EXT])
    conv_p = take("conv_p", [P, FB, CONV_W + 1])
    gain = take("gain", [P, KB])
    sq = take("sq", [P, Norm.R, GT], at="a_ext")
    std = take("std", [P, G, GT], at="conv")
    nt = take("nt", [P, Norm.R, GT], at="y")
    CHUNKS = FB // 2
    SLABS = 2 * FB + FB

    with ExitStack() as ctx:
        lin = [ctx.enter_context(nc.psum_tensor(f"{tag}lin{g}", [P, BANK], F32)) for g in range(2 * G)]
        W = Slabs(nc, sem, tag, io["weights"], env["ffn_first"][layer], SLABS, RING, raw, w_hi, w_lo, tick)
        N = Norm(env, 1 + 2 * layer, x, gain, const["ones"], h_hi, h_lo, sq, std, nt, lin)
        consts_in = sem(tag + "_consts_in")
        a_out = sem(tag + "_a_out")
        state_set = sem(tag + "_state_set")
        conv_done = sem(tag + "_conv_done")
        silu_done = sem(tag + "_silu_done")
        u_out = sem(tag + "_u_out")
        y_split = sem(tag + "_y_split")
        y_done = sem(tag + "_y_done")
        down_out = sem(tag + "_down_out")
        ends_taken = sem(tag + "_ends_taken")
        out_done = sem(tag + "_out_done")
        block = ctx.enter_context(nc.Block())

        def units_before(c):
            return 0 if isinstance(c, int) and c == 0 else c * 36 - 24

        def slab_base(c):
            return 0 if isinstance(c, int) and c == 0 else c * 6 - 2

        def over_chunks(eng, body):
            for c in range(3):
                body(c, c % 2)
            with eng.Fori(1, (CHUNKS - 1) // 2) as m:
                body(m * 2 + 1, 1)
                body(m * 2 + 2, 0)
            body(CHUNKS, CHUNKS % 2)

        def slot(c, k):
            return (k if isinstance(c, int) and c == 0 else k + 1) % RING

        def half(c, k):
            return k // 2 if isinstance(c, int) and c == 0 else c * 3 + (k // 2 - 1)

        def used_for(c, k):
            first = units_before(c)
            if isinstance(c, int) and c == 0:
                return max(0, 3 * (k - 2))
            if isinstance(c, int) and c == 1 and k < 3:
                return 3 * (k + 2)
            if k < 3:
                return first - 24 if k == 0 else first
            return first + 3 * (k - 2)

        @block.sync
        def _(sp):
            sp.dma_start(state[:, :, :, :], io["state_conv"][layer]).then_inc(consts_in, 16)
            sp.dma_start(conv_p[:, :, :], io["conv_p"][layer]).then_inc(consts_in, 16)
            sp.dma_start(gain[:, :], io["gains"][env["ffn_gain"][layer]]).then_inc(consts_in, 16)
            W.load_all(sp)
            sp.wait_ge(ends_taken, FB)
            sp.dma_start(io["conv_out"][layer], ends[:, :, :]).then_inc(out_done, 16)
            sp.wait_ge(out_done, 16)

        @block.gpsimd
        def _(pool):
            tk = tick["pool"]
            pool.wait_ge(consts_in, 48)
            pool.wait_ge(N.squared, N.blocks + G * KB)
            pool.wait_ge(N.summed, N.blocks + G * KB)
            for i in range(2):
                pool.memset(a_ext[:, i, 0:W_EXT], 0.0)

            def put_state(b, i):
                if not isinstance(b, int) or b >= 2:
                    hold(pool, conv_done, b - 1, tk)
                pool.tensor_copy(a_ext[:, i, W_EXT + T_PROMPT:].rearrange("p (b t) -> p b t", t=SEQ_EXT)[:, :, 0:W_EXT],
                                 state[:, b]).then_inc(state_set, 1)

            def take_ends(b, i):
                hold(pool, a_out, b * 3 + 3, tk)
                pool.tensor_copy(ends[:, b, 0:W_EXT], a_ext[:, i, T_PROMPT:T_PROMPT + W_EXT])
                pool.tensor_copy(ends[:, b, W_EXT:].rearrange("p (b t) -> p b t", t=W_EXT),
                                 a_ext[:, i, W_EXT + T_PROMPT:].rearrange("p (b t) -> p b t", t=SEQ_EXT)[:, :, DEC_T:SEQ_EXT])\
                    .then_inc(ends_taken, 1)

            put_state(0, 0)
            put_state(1, 1)
            with pool.Fori(0, CHUNKS - 1) as m:
                for i in range(2):
                    take_ends(m * 2 + i, i)
                    put_state(m * 2 + (i + 2), i)
            for i in range(2):
                take_ends(FB - 2 + i, i)

        @block.scalar
        def _(act):
            tk = tick["act"]
            act.wait_ge(consts_in, 48)
            N.on_scalar(act)

            def hi(c, k):
                W.split_hi(act, slab_base(c) + k, half(c, k), slot(c, k), k % 2, used_for(c, k))

            def gate_rows(c, j):
                blk = c * 2 + j
                hold(act, ends_taken, blk - 1, tk)
                hold(act, conv_done, blk - 1, tk)
                hold(act, state_set, blk + 1, tk)
                for g in range(G):
                    hold(act, W.units, units_before(c) + 6 * j + g + 1, tk)
                    a, b = g * GT, min((g + 1) * GT, T_PROMPT)
                    last = act.activation(a_ext[:, j, W_EXT + a:W_EXT + b], lin[g][:, 0:b - a], ACT.Copy)
                    if g == G - 1:
                        last = act.activation(
                            a_ext[:, j, W_EXT + T_PROMPT:].rearrange("p (b t) -> p b t", t=SEQ_EXT)[:, :, W_EXT:],
                            lin[g][:, b - a:GT].rearrange("p (b t) -> p b t", t=DEC_T), ACT.Copy)
                    last.then_inc(a_out, 1)

            def silu(c, j):
                hold(act, conv_done, c * 2 + j + 1, tk)
                act.activation(conv[:, j], conv[:, j], ACT.Silu).then_inc(silu_done, 1)

            def y_high(c, par, j):
                hold(act, u_out, (c * 2 + j) * 3 + 3, tk)
                act.activation(y_hi[:, 2 * par + j], y[:, :], ACT.Copy).then_inc(y_split, 1)

            def body(c, par):
                if isinstance(c, int) and c == CHUNKS:
                    hi(c, 1)
                    return
                hi(c, 1)
                gate_rows(c, 0)
                hi(c, 2)
                silu(c, 0)
                hi(c, 3)
                y_high(c, par, 0)
                gate_rows(c, 1)
                if not (isinstance(c, int) and c == 0):
                    hi(c, 4)
                    hi(c, 5)
                silu(c, 1)
                y_high(c, par, 1)
                hi(c + 1, 0)

            W.split_hi(act, 0, 0, 0, 0, 0)
            over_chunks(act, body)

        @block.vector
        def _(dve):
            tk = tick["dve"]
            dve.wait_ge(consts_in, 48)
            N.on_vector(dve)

            def lo(c, k):
                W.split_lo(dve, slab_base(c) + k, slot(c, k), k % 2)

            def seqs(ap, t):
                return ap.rearrange("p (b t) -> p b t", t=t)

            def convolve(c, j):
                blk = c * 2 + j
                hold(dve, a_out, blk * 3 + 3, tk)
                if not (isinstance(c, int) and c == 0):
                    hold(dve, u_out, (blk - 1) * 3, tk)
                rows = a_ext[:, j, W_EXT + T_PROMPT:]
                for tap in range(CONV_W):
                    w = conv_p[:, blk, tap:tap + 1]
                    src_p, src_s = a_ext[:, j, tap:tap + T_PROMPT], seqs(rows, SEQ_EXT)[:, :, tap:tap + DEC_T]
                    dst_p, dst_s = conv[:, j, 0:T_PROMPT], seqs(conv[:, j, T_PROMPT:], DEC_T)
                    if tap == 0:
                        b = conv_p[:, blk, CONV_W:CONV_W + 1]
                        dve.tensor_scalar(dst_p, src_p, w, b, ALU.mult, ALU.add)
                        last = dve.tensor_scalar(dst_s, src_s, w, b, ALU.mult, ALU.add)
                    else:
                        dve.drain()
                        dve.scalar_tensor_tensor(dst_p, src_p, w, dst_p, ALU.mult, ALU.add)
                        last = dve.scalar_tensor_tensor(dst_s, src_s, w, dst_s, ALU.mult, ALU.add)
                last.then_inc(conv_done, 1)

            def up_rows(c, j):
                blk = c * 2 + j
                hold(dve, silu_done, blk + 1, tk)
                hold(dve, y_split, blk, tk)
                hold(dve, y_done, blk, tk)
                for g in range(G):
                    hold(dve, W.units, units_before(c) + 6 * j + 3 + g + 1, tk)
                    dve.tensor_tensor(y[:, g * GT:(g + 1) * GT], lin[G + g][:, 0:GT], conv[:, j, g * GT:(g + 1) * GT],
                                      ALU.mult).then_inc(u_out, 1)

            def y_low(c, par, j):
                hold(dve, y_split, c * 2 + j + 1, tk)
                dve.tensor_tensor(y_lo[:, 2 * par + j], y[:, :], y_hi[:, 2 * par + j].bitcast(F32), ALU.subtract).then_inc(y_done, 1)

            def body(c, par):
                end = isinstance(c, int) and c == CHUNKS
                lo(c, 1)
                if not end:
                    convolve(c, 0)
                    lo(c, 2)
                    up_rows(c, 0)
                    lo(c, 3)
                    y_low(c, par, 0)
                    convolve(c, 1)
                    if not (isinstance(c, int) and c == 0):
                        lo(c, 4)
                        lo(c, 5)
                    up_rows(c, 1)
                    y_low(c, par, 1)
                    lo(c + 1, 0)
                if not (isinstance(c, int) and c == 0):
                    first = units_before(c) + (0 if end else 12)
                    dve.drain()
                    for n in range(KB * G):
                        nb, g = divmod(n, G)
                        hold(dve, W.units, first + n + 1, tk)
                        xs = x[:, nb, g * GT:(g + 1) * GT]
                        dve.tensor_tensor(xs, xs, lin[n % 6][:, 0:GT], ALU.add).then_inc(down_out, 1)

            W.split_lo(dve, 0, 0, 0)
            over_chunks(dve, body)
            dve.drain()

        @block.tensor
        def _(pe):
            tk = tick["pe"]
            N.on_tensor(pe)

            def body(c, par):
                start, end = (isinstance(c, int) and c == v for v in (0, CHUNKS))
                if not end:
                    for k in range(4):
                        j, up = divmod(k, 2)
                        hold(pe, W.lo_done, slab_base(c) + k + 1, tk)
                        for g in range(G):
                            if k == 0 and start:
                                N.wait_group(pe, g)
                            elif k >= 2 or (isinstance(c, int) and c == 1):
                                hold(pe, u_out if up else a_out, (c * 2 + j - 1) * 3 + g + 1, tk)
                            elif not start:
                                hold(pe, down_out, (c - 2) * 24 + 19 + 3 * up + g, tk)
                            W.block(pe, lin[3 * up + g][:, 0:GT], slot(c, k), h_hi, h_lo, g).then_inc(W.units, 1)
                if not start:
                    k0 = 0 if end else 4
                    hold(pe, W.lo_done, slab_base(c) + k0 + 2, tk)
                    hold(pe, y_done, c * 2, tk)
                    for n in range(KB * G):
                        nb, g = divmod(n, G)
                        if n < 6 and not end:
                            hold(pe, u_out if n >= 3 else a_out, c * 6 + 3 + n % 3 + 1, tk)
                        else:
                            hold(pe, down_out, (c - 1) * 24 + n - 5, tk)
                        for j in range(2):
                            src = 2 * (1 - par) + j
                            i = W.product(pe, lin[n % 6][:, 0:GT], slot(c, k0 + j), nb * P, y_hi[:, src, g * GT:(g + 1) * GT],
                                          y_lo[:, src, g * GT:(g + 1) * GT], j == 0, j == 1)
                        i.then_inc(W.units, 1)

            over_chunks(pe, body)


HEAD_D = 64
N_HEADS = 16
N_KV = 4
GROUP = N_HEADS // N_KV
QB = N_HEADS // 2
IDX_H = 8
IDX_B = IDX_H // 2
ROT = HEAD_D // 4
TOPK = 256
CHUNK = 64
THETA = 500000.0
S_KEYS = PAST + DEC_T
A_KEYS = PAST + T_SAMPLE
TAKEN = -3e38
BARRED = -1e38
DSA_PROJ = IDX_B + 1 + 1 + 2 + 2 + QB
KI_SLAB, WI_SLAB, K_SLAB, V_SLAB, Q_SLAB = IDX_B, IDX_B + 1, IDX_B + 2, IDX_B + 4, IDX_B + 6


def head_order():
    heads = [(2 * p + half) * GROUP + g for p in range(2) for g in range(GROUP) for half in range(2)]
    return np.concatenate([np.arange(h * HEAD_D, (h + 1) * HEAD_D) for h in heads])


def dsa_slabs(i):
    w = i["ds_w_in"][0]
    o1 = N_HEADS * HEAD_D
    o2 = o1 + N_KV * HEAD_D
    o3 = o2 + N_KV * HEAD_D
    o4 = o3 + IDX_H * HEAD_D
    o5 = o4 + HEAD_D
    wi = np.concatenate([w[:, o5:], np.zeros((D, P - IDX_H), w.dtype)], axis=1)
    cols = [w[:, o3:o4], w[:, o4:o5], w[:, o4:o5], wi, w[:, o1:o2], w[:, o2:o3], w[:, :o1][:, head_order()]]
    out = in_slabs(i["ds_w_out"][0][head_order()])
    return np.concatenate([in_slabs(np.concatenate(cols, axis=1)), out])


def dsa_layout(i):
    ck = i["cache_k"][0].reshape(DEC_B, PAST, 2, P).transpose(0, 2, 3, 1)
    cv = i["cache_v"][0].reshape(DEC_B, PAST // P, P, N_KV * HEAD_D).transpose(0, 2, 1, 3)
    ci = i["cache_kidx"][0].transpose(0, 2, 1)
    ln = np.stack([i["ds_kln_w"][0], i["ds_kln_b"][0]], axis=1)
    return {"cache_k": ck, "cache_v": cv, "cache_ki": np.concatenate([ci, ci], axis=1), "ki_ln": np.concatenate([ln, ln])}


def dsa_constants():
    pos = np.concatenate([np.arange(T_PROMPT), np.tile(PAST + np.arange(DEC_T), DEC_B)]).astype(np.float32)
    half = ROT // 2
    freq = np.power(np.float32(THETA), -np.arange(half, dtype=np.float32) / np.float32(half)).astype(np.float32)
    ang = pos[None, :] * freq[:, None]
    cos, sin = np.ones((HEAD_D, T), np.float32), np.zeros((HEAD_D, T), np.float32)
    cos[:half] = cos[half:ROT] = np.cos(ang)
    sin[:half], sin[half:ROT] = -np.sin(ang), np.sin(ang)
    rows = np.arange(P)
    t_row = rows % DEC_T
    same_t = (t_row[:, None] == np.arange(DEC_T)[None, :]).astype(np.float32)
    b_row = rows // DEC_T
    spread_b = ((b_row[:, None, None] == np.arange(DEC_B)[None, :, None]) & (t_row[:, None, None] == t_row[None, None, :]))
    other = np.where(b_row[:, None] == np.arange(DEC_B)[None, :], 0.0, NEG)
    bf = mybir.dt.np(BF16)
    return {"cos": np.concatenate([cos, cos]), "sin": np.concatenate([sin, sin]), "same_t": same_t,
            "spread_b": spread_b.astype(bf), "other": other.astype(np.float32)}


def dsa_space(nc, env):
    sp_ = Space(nc, env["free"], env["end"])
    env["k"] = sp_.take("at_k", [P, 2, T])
    env["v"] = sp_.take("at_v", [P, NT, N_KV * HEAD_D])
    env["ki"] = sp_.take("at_ki", [P, T])
    env["wi"] = sp_.take("at_wi", [P, NT, IDX_H])
    env["at_free"] = sp_.at


def project_phase(nc, env, x):
    dsa_space(nc, env)
    io, const, sem, tick = env["io"], env["const"], env["sem"], env["tick"]
    k_sb, v_sb, ki, wi = env["k"], env["v"], env["ki"], env["wi"]
    take = Space(nc, env["at_free"], env["end"]).take
    h_hi, h_lo = take("pj_h_hi", [P, KB, T], F32R), take("pj_h_lo", [P, KB, T], F32R)
    raw = take("pj_raw", [P, 2, SLAB])
    w_hi, w_lo = take("pj_w_hi", [P, 2, SLAB], F32R), take("pj_w_lo", [P, 2, SLAB], F32R)
    rows = take("pj_rows", [P, 2, T])
    swapped = take("pj_swapped", [P, T])
    roped = take("pj_roped", [P, 2, T])
    cos, sin = take("pj_cos", [P, T]), take("pj_sin", [P, T])
    ln = take("pj_ln", [P, 2])
    gain = take("pj_gain", [P, KB])
    sq = take("pj_sq", [P, Norm.R, GT], at=t_at["pj_roped"])
    std = take("pj_std", [P, G, GT], at=t_at["pj_swapped"])
    nt = take("pj_nt", [P, Norm.R, GT], at=t_at["pj_roped"] + 4 * T)
    WI_SCALE = float(np.float32((IDX_H * HEAD_D) ** -0.5))
    SWAP = list(range(ROT // 2, ROT)) + list(range(ROT // 2)) + list(range(ROT, 32))

    with ExitStack() as ctx:
        lin = [ctx.enter_context(nc.psum_tensor(f"pj_lin{g}", [P, BANK], F32)) for g in range(G)]
        lnb = [ctx.enter_context(nc.psum_tensor(f"pj_ln{g}", [P, BANK], F32)) for g in range(G)]
        W = Slabs(nc, sem, "pj", io["weights"], HG_SLABS + FFN_SLABS, DSA_PROJ, 2, raw, w_hi, w_lo, tick)
        N = Norm(env, 2, x, gain, const["ones"], h_hi, h_lo, sq, std, nt, lin)
        consts_in = sem("pj_consts_in")
        evac = sem("pj_evac")
        rope_done = sem("pj_rope_done")
        ln_pe, ln_dve, ln_act = sem("pj_ln_pe"), sem("pj_ln_dve"), sem("pj_ln_act")
        q_out = [sem(f"pj_q_out{k}") for k in range(2)]
        kv_out = sem("pj_kv_out")
        block = ctx.enter_context(nc.Block())
        FIRST_Q = IDX_B + 3

        @block.sync
        def _(sp):
            for dst, src in ((cos[:, :], io["cos"]), (sin[:, :], io["sin"]), (ln[:, :], io["ki_ln"]), (gain[:, :], io["gains"][2])):
                sp.dma_start(dst, src).then_inc(consts_in, 16)
            W.load_all(sp)

        @block.gpsimd
        def _(pool):
            tk = tick["pool"]
            for n in range(IDX_B):
                pool.wait_ge(rope_done, n + 1)
                pool.dma_start(io["qi_t"][n], roped[:, n % 2, :]).then_inc(q_out[n % 2], 16)
            pool.wait_ge(rope_done, IDX_B + 1)
            pool.dma_start(io["ki_out"], ki[0:HEAD_D, :]).then_inc(kv_out, 16)
            pool.wait_ge(rope_done, IDX_B + 3)
            pool.dma_start(io["k_out"], k_sb[:, :, :]).then_inc(kv_out, 16)
            pool.wait_ge(evac, 3 * (V_SLAB + 2))
            pool.dma_start(io["v_out"], v_sb[:, :, :]).then_inc(kv_out, 16)
            with pool.Fori(0, QB // 2) as m:
                for par in range(2):
                    hold(pool, rope_done, m * 2 + (FIRST_Q + par + 1), tk)
                    pool.dma_start(io["q_t"][m * 2 + par], roped[:, par, :]).then_inc(q_out[par], 16)
            pool.wait_ge(kv_out, 48)
            for par in range(2):
                pool.wait_ge(q_out[par], 16 * (IDX_B + QB) // 2)

        @block.scalar
        def _(act):
            tk = tick["act"]
            act.wait_ge(consts_in, 64)
            N.on_scalar(act)

            def hi(s, par, half):
                W.split_hi(act, s, half, par, par, (s - 1) * 3)

            def copy_rows(s, n, buf, scale=1.0):
                hold(act, rope_done, n - 1, tk)
                for g in range(G):
                    hold(act, W.units, s * 3 + g + 1, tk)
                    act.activation(rows[:, buf, g * GT:(g + 1) * GT], lin[g][:, 0:GT], ACT.Copy, scale=scale).then_inc(evac, 1)

            W.split_hi(act, 0, 0, 0, 0, 0)
            for s in range(Q_SLAB):
                hi(s + 1, (s + 1) % 2, (s + 1) // 2)
                if s <= KI_SLAB:
                    copy_rows(s, s, s % 2)
                elif s == WI_SLAB:
                    for g in range(G):
                        act.wait_ge(W.units, 3 * s + g + 1)
                        act.activation(wi[:, 3 * g:3 * g + 3, :], lin[g][:, 0:3 * IDX_H], ACT.Copy, scale=WI_SCALE).then_inc(evac, 1)
                    act.wait_ge(ln_dve, 1)
                    act.activation(swapped[:, :], rows[:, 0, :], ACT.Square).then_inc(ln_act, 1)
                    act.wait_ge(ln_pe, 2)
                    for g in range(G):
                        i = act.activation(swapped[:, g * GT:(g + 1) * GT], lnb[g][:, 0:GT], ACT.Sqrt, bias=EPS)
                    i.then_inc(ln_act, 1)
                elif s < V_SLAB:
                    copy_rows(s, s - 1, (s - 1) % 2)
                else:
                    for g in range(G):
                        act.wait_ge(W.units, 3 * s + g + 1)
                        act.activation(v_sb[:, 3 * g:3 * g + 3, (s - V_SLAB) * P:(s - V_SLAB + 1) * P],
                                       lin[g][:, 0:GT].rearrange("p (t c) -> p t c", c=P), ACT.Copy).then_inc(evac, 1)
            with act.Fori(0, QB // 2 - 1) as m:
                for par in range(2):
                    hi(m * 2 + (Q_SLAB + par + 1), 1 - par, m + (Q_SLAB + par + 1) // 2)
                    copy_rows(m * 2 + (Q_SLAB + par), m * 2 + (FIRST_Q + par), 1 - par, HEAD_D ** -0.5)
            last = Q_SLAB + QB - 2
            hi(last + 1, 1, (last + 1) // 2)
            copy_rows(last, FIRST_Q + QB - 2, 1, HEAD_D ** -0.5)
            copy_rows(last + 1, FIRST_Q + QB - 1, 0, HEAD_D ** -0.5)

        @block.vector
        def _(dve):
            tk = tick["dve"]
            dve.wait_ge(consts_in, 64)
            N.on_vector(dve)

            def lo(s, par):
                W.split_lo(dve, s, par, par)

            def rope(src, dst):
                dve.drain()
                dve.stream_shuffle(swapped[:, :], src, SWAP)
                dve.tensor_tensor(dst, src, cos[:, :], ALU.mult)
                dve.drain()
                dve.tensor_tensor(swapped[:, :], swapped[:, :], sin[:, :], ALU.mult)
                dve.drain()
                dve.tensor_tensor(dst, dst, swapped[:, :], ALU.add).then_inc(rope_done, 1)

            def rope_rows(s, n, buf, dst, out_par=None, outs=0):
                hold(dve, evac, s * 3 + 3, tk)
                if out_par is not None:
                    hold(dve, q_out[out_par], outs, tk)
                rope(rows[:, buf, :], dst)

            W.split_lo(dve, 0, 0, 0)
            for s in range(Q_SLAB):
                lo(s + 1, (s + 1) % 2)
                if s < KI_SLAB:
                    rope_rows(s, s, s % 2, roped[:, s % 2, :], s % 2, 16 * (s // 2))
                elif s == KI_SLAB:
                    dve.wait_ge(ln_pe, 1)
                    dve.drain()
                    for g in range(G):
                        cols = slice(g * GT, (g + 1) * GT)
                        i = dve.tensor_tensor(rows[:, 0, cols], rows[:, 0, cols], lnb[g][:, 0:GT], ALU.subtract)
                    i.then_inc(ln_dve, 1)
                elif s == WI_SLAB:
                    dve.wait_ge(ln_act, 2)
                    dve.reciprocal(swapped[:, :], swapped[:, :])
                    dve.drain()
                    dve.tensor_tensor(rows[:, 0, :], rows[:, 0, :], swapped[:, :], ALU.mult)
                    dve.drain()
                    dve.tensor_scalar(rows[:, 0, :], rows[:, 0, :], ln[:, 0:1], ln[:, 1:2], ALU.mult, ALU.add)
                    rope(rows[:, 0, :], ki[:, :])
                elif s < V_SLAB:
                    rope_rows(s, s - 1, (s - 1) % 2, k_sb[:, s - K_SLAB, :])
            with dve.Fori(0, QB // 2 - 1) as m:
                for par in range(2):
                    lo(m * 2 + (Q_SLAB + par + 1), 1 - par)
                    rope_rows(m * 2 + (Q_SLAB + par), 0, 1 - par, roped[:, par, :], par, m * 16 + 16 * IDX_B // 2)
            last = Q_SLAB + QB - 2
            lo(last + 1, 1)
            for par in range(2):
                rope_rows(last + par, 0, 1 - par, roped[:, par, :], par, 16 * (IDX_B + QB - 2) // 2)
            dve.drain()

        @block.tensor
        def _(pe):
            tk = tick["pe"]
            N.on_tensor(pe)

            def project(s, par):
                hold(pe, W.lo_done, s + 1, tk)
                for g in range(G):
                    if isinstance(s, int) and s == 0:
                        N.wait_group(pe, g)
                    hold(pe, evac, (s - 1) * 3 + g + 1, tk)
                    W.block(pe, lin[g][:, 0:GT], par, h_hi, h_lo, g).then_inc(W.units, 1)

            def project_tokens(s, par, cols):
                pe.wait_ge(W.lo_done, s + 1)
                for g in range(G):
                    pe.wait_ge(evac, (s - 1) * 3 + g + 1)
                    for tile in range(3):
                        i = W.tokens(pe, lin[g][:, tile * cols:(tile + 1) * cols], par, cols, h_hi, h_lo, 3 * g + tile)
                    i.then_inc(W.units, 1)

            def ln_mean(src, step):
                for g in range(G):
                    i = pe.matmul(lnb[g][:, 0:GT], const["ones_v"][:, :], src[:, g * GT:(g + 1) * GT], start=True, stop=True)
                i.then_inc(ln_pe, 1)

            for s in range(Q_SLAB):
                if s == WI_SLAB:
                    pe.wait_ge(evac, 3 * (KI_SLAB + 1))
                    ln_mean(rows[:, 0, :], 0)
                    project_tokens(s, s % 2, IDX_H)
                    pe.wait_ge(ln_act, 1)
                    ln_mean(swapped[:, :], 1)
                elif s < V_SLAB:
                    project(s, s % 2)
                else:
                    project_tokens(s, s % 2, P)
            with pe.Fori(0, QB // 2) as m:
                for par in range(2):
                    project(m * 2 + (Q_SLAB + par), par)


def mask_at(tile):
    return P * tile * (tile + 1) // 2


def select_phase(nc, env, x):
    io, sem, tick = env["io"], env["sem"], env["tick"]
    ki, wi = env["ki"], env["wi"]
    sp_ = Space(nc, env["at_free"], env["end"])
    take = sp_.take
    mask_p, mask_s = take("mask_p", [P, mask_at(PT)], BF16), take("mask_s", [P, A_KEYS], BF16)
    env["mask_p"], env["mask_s"], env["masks_end"] = mask_p, mask_s, sp_.at
    FIRST = TOPK // P
    qi = take("se_qi", [P, IDX_B, T])
    qi_b = take("se_qi_b", [P, DEC_B, IDX_B, DEC_T])
    keys = take("se_keys", [P, 2, PAST])
    relu_s, relu_p = take("se_relu_s", [P, 3, BANK]), take("se_relu_p", [P, 2, T_PROMPT])
    score_s, score_p = take("se_score_s", [P, S_KEYS]), take("se_score_p", [P, 2, T_PROMPT])
    top = take("se_top", [P, 8])
    same_t, own_b, other = take("se_same_t", [P, DEC_T]), take("se_own_b", [P, DEC_B]), take("se_other", [P, DEC_B])
    w_by_row = take("se_w_by_row", [P, P])
    w_col = take("se_w_col", [P, DEC_B])
    w_sel = take("se_w_sel", [P, DEC_B, P])
    tail = take("se_tail", [P, DEC_T])
    tiles = list(range(FIRST, PT))
    chunks = pieces(PAST) + [(PAST, S_KEYS)]
    NCHK = len(chunks)
    units = [(b, c) for b in range(DEC_B) for c in range(NCHK)]

    with ExitStack() as ctx:
        bank = [ctx.enter_context(nc.psum_tensor(f"se_bank{n}", [P, BANK], F32)) for n in range(8)]
        acc, dots = bank[0:NCHK], bank[NCHK:8]
        pair = ((bank[5], bank[6]), (bank[7], bank[0]))
        consts_in, qi_in = sem("se_consts_in"), sem("se_qi_in")
        keys_in = [sem(f"se_keys_in{n}") for n in range(2)]
        qi_sorted, w_rows_set, w_turned, w_sel_set = (sem("se_" + n) for n in ("qi_sorted", "w_rows_set", "w_turned", "w_sel_set"))
        dots_done, relu_done, summed = sem("se_dots_done"), sem("se_relu_done"), sem("se_summed")
        scores_out = sem("se_scores_out")
        p_dots, p_relu, p_added = sem("se_p_dots"), sem("se_p_relu"), sem("se_p_added")
        block = ctx.enter_context(nc.Block())

        @block.sync
        def _(sp):
            for dst, src in ((same_t[:, :], io["same_t"]), (own_b[:, :], io["own_b"]), (other[:, :], io["other"])):
                sp.dma_start(dst, src).then_inc(consts_in, 16)
            sp.dma_start(qi[:, :, :], io["qi_t"].rearrange("b p t -> p b t")).then_inc(qi_in, 16)
            for b in range(DEC_B):
                if b >= 2:
                    sp.wait_ge(dots_done, NCHK * (b - 1))
                sp.dma_start(keys[:, b % 2, :], io["cache_ki"][b]).then_inc(keys_in[b % 2], 16)

        @block.tensor
        def _(pe):
            pe.wait_ge(w_rows_set, 1)
            pe.wait_ge(consts_in, 48)
            pe.matmul(dots[0][:, 0:DEC_B], w_by_row[:, :], own_b[:, :], start=True, stop=True).then_inc(w_turned, 1)
            pe.wait_ge(w_sel_set, 1)
            pe.wait_ge(qi_sorted, 1)

            def head_sum(u):
                b, c = units[u]
                n = chunks[c][1] - chunks[c][0]
                pe.wait_ge(relu_done, u + 1)
                pe.matmul(acc[c][:, 0:n], w_sel[:, b, :], relu_s[:, u % 3, 0:n], start=b == 0, stop=b == DEC_B - 1)\
                    .then_inc(summed, 1)

            for u, (b, c) in enumerate(units):
                a, e = chunks[c]
                if c == 0:
                    pe.wait_ge(keys_in[b % 2], 16 * (b // 2 + 1))
                if u >= 3:
                    pe.wait_ge(relu_done, u - 2)
                for half in range(2):
                    rows = slice(half * HEAD_D, (half + 1) * HEAD_D)
                    rhs = keys[rows, b % 2, a:e] if c < NCHK - 1 else ki[rows, T_PROMPT + b * DEC_T:T_PROMPT + (b + 1) * DEC_T]
                    i = pe.matmul(dots[u % 3][rows, 0:e - a], qi_b[rows, b].rearrange("p h t -> p (h t)"), rhs, start=True, stop=True)
                i.then_inc(dots_done, 1)
                if u >= 2:
                    head_sum(u - 2)
            head_sum(len(units) - 2)
            head_sum(len(units) - 1)

            pe.wait_ge(scores_out, 1)
            n = 0
            for t in tiles:
                for h in range(IDX_H):
                    rows = slice(h % 2 * HEAD_D, (h % 2 + 1) * HEAD_D)
                    if n >= 2:
                        pe.wait_ge(p_relu, n - 1)
                    for k, (a, e) in enumerate(pieces((t + 1) * P)):
                        i = pe.matmul(pair[h % 2][k][:, 0:e - a], qi[rows, h // 2, t * P:(t + 1) * P], ki[rows, a:e], start=True, stop=True)
                    i.then_inc(p_dots, 1)
                    n += 1

        @block.scalar
        def _(act):
            for u, (b, c) in enumerate(units):
                n = chunks[c][1] - chunks[c][0]
                act.wait_ge(dots_done, u + 1)
                if u >= 3:
                    act.wait_ge(summed, u - 2)
                act.activation(relu_s[:, u % 3, 0:n], dots[u % 3][:, 0:n], ACT.Relu).then_inc(relu_done, 1)
            act.wait_ge(summed, len(units))
            for c, (a, e) in enumerate(chunks):
                i = act.activation(score_s[:, a:e], acc[c][:, 0:e - a], ACT.Copy)
            i.then_inc(scores_out, 1)
            n = 0
            for t in tiles:
                for h in range(IDX_H):
                    act.wait_ge(p_dots, n + 1)
                    if n >= 2:
                        act.wait_ge(p_added, n - 1)
                    for k, (a, e) in enumerate(pieces((t + 1) * P)):
                        i = act.activation(relu_p[:, n % 2, a:e], pair[h % 2][k][:, 0:e - a], ACT.Relu)
                    i.then_inc(p_relu, 1)
                    n += 1

        @block.vector
        def _(dve):
            dve.wait_ge(consts_in, 48)
            for half in range(2):
                dst = w_by_row[:, half * HEAD_D:(half + 1) * HEAD_D].rearrange("p (h t) -> p h t", t=DEC_T)
                src = wi[:, NT - 1, :].rearrange("p (h two) -> p two h", two=2)[:, half]
                i = dve.tensor_tensor(dst, spread(src.unsqueeze(2), dst.shape), spread(same_t[:, :].unsqueeze(1), dst.shape), ALU.mult)
            i.then_inc(w_rows_set, 1)
            dve.memset(w_sel[:, :, :], 0.0)
            dve.wait_ge(qi_in, 16)
            dve.tensor_copy(qi_b[:, :, :, :], qi[:, :, T_PROMPT:T].rearrange("p h (b t) -> p b h t", t=DEC_T)).then_inc(qi_sorted, 1)
            dve.wait_ge(w_turned, 1)
            dve.tensor_copy(w_col[:, :], dots[0][:, 0:DEC_B])
            dve.drain()
            for b in range(DEC_B):
                i = dve.tensor_scalar(w_sel[:, b, b * DEC_T:(b + 1) * DEC_T], same_t[:, :], w_col[:, b:b + 1], None, ALU.mult)
            i.then_inc(w_sel_set, 1)

            def take_top(score):
                with dve.Fori(0, 4) as _:
                    for _ in range(TOPK // 8 // 4):
                        dve.max(top[:, :], score)
                        dve.drain()
                        dve.match_replace(score, top[:, :], score, TAKEN)
                        dve.drain()

            dve.memset(mask_p[:, 0:mask_at(FIRST)], 0.0)
            dve.drain()
            for t in range(FIRST):
                dve.memset(mask_p[0:CHUNK, mask_at(t + 1) - CHUNK:mask_at(t + 1)], NEG)
            dve.wait_ge(scores_out, 1)
            take_top(score_s[:, :])
            dve.tensor_scalar(mask_s[:, 0:PAST], score_s[:, 0:PAST], TAKEN * 0.7, NEG, ALU.is_gt, ALU.mult)
            dve.tensor_scalar(tail[:, :], score_s[:, PAST:S_KEYS], TAKEN * 0.7, NEG, ALU.is_gt, ALU.mult)
            dve.drain()
            dst = mask_s[:, PAST:A_KEYS].rearrange("p (b t) -> p b t", t=DEC_T)
            dve.tensor_tensor(dst, spread(tail[:, :].unsqueeze(1), dst.shape), spread(other[:, :].unsqueeze(2), dst.shape), ALU.add)
            n = 0
            for t in tiles:
                keys_n = (t + 1) * P
                score = score_p[:, t % 2, 0:keys_n]
                for h in range(IDX_H):
                    w = wi[:, t, h:h + 1]
                    dve.wait_ge(p_relu, n + 1)
                    dve.drain()
                    if h == 0:
                        dve.tensor_scalar(score, relu_p[:, n % 2, 0:keys_n], w, None, ALU.mult).then_inc(p_added, 1)
                    else:
                        dve.scalar_tensor_tensor(score, relu_p[:, n % 2, 0:keys_n], w, score, ALU.mult, ALU.add).then_inc(p_added, 1)
                    n += 1
                dve.drain()
                dve.memset(score_p[0:CHUNK, t % 2, keys_n - CHUNK:keys_n], BARRED)
                dve.drain()
                take_top(score)
                dve.tensor_scalar(mask_p[:, mask_at(t):mask_at(t + 1)], score, TAKEN * 0.7, NEG, ALU.is_gt, ALU.mult)
            dve.drain()


def attend_prompt_phase(nc, env, x):
    io, const, sem, tick = env["io"], env["const"], env["sem"], env["tick"]
    k_sb, v_sb, mask_p = env["k"], env["v"], env["mask_p"]
    sp_ = Space(nc, env["masks_end"], env["end"])
    env["o_t"] = o_t = sp_.take("o_t", [P, QB, T])
    env["o_end"] = sp_.at
    take = sp_.take
    probs, probs_t = take("ap_probs", [P, 2, T_PROMPT]), take("ap_probs_t", [P, 2, T_PROMPT])
    q = take("ap_q", [P, 2, QB, P])
    part_max, neg_max = take("ap_part_max", [P, 2, 2]), take("ap_neg_max", [P, 2, 1])
    total, inv = take("ap_total", [P, 2, 1]), take("ap_inv", [P, 2, 1])
    o = take("ap_o", [P, P])
    blocks = [(t, j) for t in range(PT) for j in range(QB)]

    with ExitStack() as ctx:
        bank = [ctx.enter_context(nc.psum_tensor(f"ap_bank{n}", [P, BANK], F32)) for n in range(8)]
        qk, tr, ob = (bank[0:2], bank[2:4]), bank[4:6], bank[6:8]
        q_in = [sem(f"ap_q_in{n}") for n in range(2)]
        qk_done, maxed, exped, turned, turned_out, pv_done, o_out = (
            sem("ap_" + n) for n in ("qk_done", "maxed", "exped", "turned", "turned_out", "pv_done", "o_out"))
        o_turned, o_copied = sem("ap_o_turned"), sem("ap_o_copied")
        block = ctx.enter_context(nc.Block())

        @block.sync
        def _(sp):
            for t in range(PT):
                if t >= 2:
                    sp.wait_ge(qk_done, 2 * QB * (t - 1))
                sp.dma_start(q[:, t % 2], io["q_t"][:, :, t * P:(t + 1) * P].rearrange("j p t -> p j t")).then_inc(q_in[t % 2], 16)

        @block.tensor
        def _(pe):
            def scores(n, half):
                t, j = blocks[n]
                rows = slice(half * HEAD_D, (half + 1) * HEAD_D)
                if j == 0:
                    pe.wait_ge(q_in[t % 2], 16 * (t // 2 + 1))
                if n:
                    pe.wait_ge(maxed, 2 * n + half - 1)
                for c, (a, e) in enumerate(pieces((t + 1) * P)):
                    i = pe.matmul(qk[half][c][:, 0:e - a], q[rows, t % 2, j, :], k_sb[rows, j // GROUP, a:e], start=True, stop=True)
                i.then_inc(qk_done, 1)

            def turn(n, half):
                t, j = blocks[n]
                pe.wait_ge(exped, 2 * n + half + 1)
                if n or half:
                    pe.wait_ge(turned_out, 2 * n + half)
                for c in range(t + 1):
                    i = pe.transpose(tr[c // 4][:, c % 4 * P:(c % 4 + 1) * P], probs[:, half, c * P:(c + 1) * P], const["ident"][:, :])
                i.then_inc(turned, 1)

            def values(n, half):
                t, j = blocks[n]
                pe.wait_ge(turned_out, 2 * n + half + 1)
                if n:
                    pe.wait_ge(o_out, 2 * n + half - 1)
                    pe.wait_ge(o_copied, n)
                col = (j // GROUP * 2 + half) * HEAD_D
                for c in range(t + 1):
                    i = pe.matmul(ob[half][:, 0:HEAD_D], probs_t[:, half, c * P:(c + 1) * P], v_sb[:, c, col:col + HEAD_D],
                                  start=c == 0, stop=c == t)
                i.then_inc(pv_done, 1)

            for n in range(len(blocks) + 1):
                for half in range(2):
                    if n:
                        turn(n - 1, half)
                    if n < len(blocks):
                        scores(n, half)
                    if n:
                        values(n - 1, half)
                if n:
                    pe.wait_ge(o_out, 2 * n)
                    pe.transpose(ob[1][:, P:2 * P], o[:, :], const["ident"][:, :]).then_inc(o_turned, 1)

        @block.scalar
        def _(act):
            for n in range(len(blocks) + 1):
                for half in range(2):
                    if n:
                        t = blocks[n - 1][0]
                        act.wait_ge(turned, 2 * (n - 1) + half + 1)
                        if n > 1:
                            act.wait_ge(pv_done, 2 * (n - 1) + half - 1)
                        for c, (a, e) in enumerate(pieces((t + 1) * P)):
                            i = act.activation(probs_t[:, half, a:e], tr[c][:, 0:e - a], ACT.Copy)
                        i.then_inc(turned_out, 1)
                    if n < len(blocks):
                        keys = (blocks[n][0] + 1) * P
                        act.wait_ge(maxed, 2 * n + half + 1)
                        act.activation(probs[:, half, 0:keys], probs[:, half, 0:keys], ACT.Exp, bias=neg_max[:, half],
                                       accum_out=total[:, half]).then_inc(exped, 1)

        @block.vector
        def _(dve):
            for n in range(len(blocks) + 1):
                for half in range(2):
                    if n < len(blocks):
                        t = blocks[n][0]
                        dve.wait_ge(qk_done, 2 * n + half + 1)
                        if n:
                            dve.wait_ge(turned, 2 * n + half - 1)
                        parts = pieces((t + 1) * P)
                        for c, (a, e) in enumerate(parts):
                            dve.tensor_tensor_reduce(out=probs[:, half, a:e], in0=qk[half][c][:, 0:e - a],
                                                     in1=mask_p[:, mask_at(t) + a:mask_at(t) + e], scale=1.0, scalar=-3e38,
                                                     op0=ALU.add, op1=ALU.max, accum_out=part_max[:, half, c:c + 1])
                        dve.drain()
                        if len(parts) == 2:
                            dve.tensor_tensor(part_max[:, half, 0:1], part_max[:, half, 0:1], part_max[:, half, 1:2], ALU.max)
                            dve.drain()
                        dve.tensor_scalar(neg_max[:, half], part_max[:, half, 0:1], -1.0, None, ALU.mult).then_inc(maxed, 1)
                    if n:
                        m = n - 1
                        dve.wait_ge(pv_done, 2 * m + half + 1)
                        if half == 0 and m:
                            dve.wait_ge(o_turned, m)
                        dve.tensor_scalar(o[:, half * HEAD_D:(half + 1) * HEAD_D], ob[half][:, 0:HEAD_D], inv[:, half], None, ALU.mult)\
                            .then_inc(o_out, 1)
                    if n < len(blocks):
                        dve.wait_ge(exped, 2 * n + half + 1)
                        dve.drain()
                        dve.reciprocal(inv[:, half], total[:, half])
                if n:
                    t, j = blocks[n - 1]
                    dve.wait_ge(o_turned, n)
                    dve.tensor_copy(o_t[:, j, t * P:(t + 1) * P], ob[1][:, P:2 * P]).then_inc(o_copied, 1)
            dve.drain()


def attend_sample_phase(nc, env, x):
    io, const, sem, tick = env["io"], env["const"], env["sem"], env["tick"]
    k_sb, v_sb, mask_s, o_t = env["k"], env["v"], env["mask_s"], env["o_t"]
    take = Space(nc, env["o_end"], env["end"]).take
    keys, vals = take("as_keys", [P, 2, PAST]), take("as_vals", [P, 2, PAST // P, N_KV * HEAD_D])
    probs, probs_t = take("as_probs", [P, 2, A_KEYS]), take("as_probs_t", [P, A_KEYS])
    q = take("as_q", [P, QB, T_SAMPLE])
    q_u = take("as_q_u", [P, 2, GROUP, DEC_T])
    rows_of = take("as_rows_of", [P, DEC_B, P], BF16)
    chunks = pieces(A_KEYS)
    NCHK = len(chunks)
    part_max, neg_max = take("as_part_max", [P, 2, NCHK]), take("as_neg_max", [P, 2, 1])
    total, inv = take("as_total", [P, 2, 1]), take("as_inv", [P, 2, 1])
    o = take("as_o", [P, P])
    tiles = [(a // P, e // P) for a, e in chunks]
    UNITS = 2 * DEC_B

    with ExitStack() as ctx:
        bank = [ctx.enter_context(nc.psum_tensor(f"as_bank{n}", [P, BANK], F32)) for n in range(8)]
        qk, tr, ob = bank[0:NCHK], bank[5:7], bank[7]
        consts_in = sem("as_consts_in")
        keys_in = [sem(f"as_keys_in{n}") for n in range(2)]
        vals_in = [sem(f"as_vals_in{n}") for n in range(2)]
        q_set, qk_done, read, exped, turned, turned_out, pv_done, o_out, o_turned, o_copied = (
            sem("as_" + n) for n in ("q_set", "qk_done", "read", "exped", "turned", "turned_out", "pv_done", "o_out", "o_turned", "o_copied"))
        maxed = sem("as_maxed")
        block = ctx.enter_context(nc.Block())

        @block.sync
        def _(sp):
            tk = tick["sp"]
            sp.dma_start(q[:, :, :], io["q_t"][:, :, T_PROMPT:T].rearrange("j p t -> p j t")).then_inc(consts_in, 16)
            sp.dma_start(rows_of[:, :, :], io["spread_b"]).then_inc(consts_in, 16)

            def load(b, par):
                for p in range(2):
                    if not isinstance(b, int):
                        hold(sp, qk_done, (b * 2 + (p - 1)) * NCHK, tk)
                    elif b:
                        sp.wait_ge(qk_done, (b * 2 + p - 1) * NCHK)
                    sp.dma_start(keys[:, p], io["cache_k"][b, p]).then_inc(keys_in[p], 16)
                if not (isinstance(b, int) and b < 2):
                    hold(sp, pv_done, b * 2 - 2, tk)
                sp.dma_start(vals[:, par], io["cache_v"][b]).then_inc(vals_in[par], 16)

            load(0, 0)
            load(1, 1)
            with sp.Fori(1, DEC_B // 2) as m:
                load(m * 2, 0)
                load(m * 2 + 1, 1)

        @block.gpsimd
        def _(pool):
            pool.wait_ge(consts_in, 32)

            def put_q(b):
                for p in range(2):
                    hold(pool, qk_done, (b * 2 + (p - 1)) * NCHK, tick["pool"])
                    pool.tensor_copy(q_u[:, p], q[:, GROUP * p:GROUP * (p + 1), :].rearrange("p g (b t) -> p g b t", t=DEC_T)[:, :, b, :])\
                        .then_inc(q_set, 1)

            put_q(0)
            with pool.Fori(1, DEC_B) as b:
                put_q(b)

        @block.tensor
        def _(pe):
            tk = tick["pe"]
            pe.wait_ge(consts_in, 32)

            def scores(u, b, p, half_b, c):
                a, e = chunks[c]
                if c == 0:
                    hold(pe, q_set, u + 1, tk)
                    hold(pe, keys_in[p], (b + 1) * 16, tk)
                hold(pe, read, (u - 1) * NCHK + c + 1, tk)
                out = qk[c]
                pe.matmul(out[:, 0:e - a], rows_of[:, b, :], mask_s[:, a:e], start=True, stop=False)
                for half in range(2):
                    rows = slice(half * HEAD_D, (half + 1) * HEAD_D)
                    rhs = keys[rows, p, a:e] if c < NCHK - 1 else k_sb[rows, p, T_PROMPT:T]
                    i = pe.matmul(out[rows, 0:e - a], q_u[rows, p].rearrange("p g t -> p (g t)"), rhs, start=False, stop=True)
                i.then_inc(qk_done, 1)

            def turn(u, p, c):
                if c == 0:
                    hold(pe, exped, u + 1, tk)
                hold(pe, turned_out, u * NCHK + c - 1, tk)
                lo, hi = tiles[c]
                for n in range(lo, hi):
                    i = pe.transpose(tr[(c + p * NCHK) % 2][:, (n - lo) * P:(n - lo + 1) * P], probs[:, p, n * P:(n + 1) * P], const["ident"][:, :])
                i.then_inc(turned, 1)

            def values(u, b, p, par, half_b):
                hold(pe, turned_out, (u + 1) * NCHK, tk)
                if p == 0:
                    hold(pe, vals_in[par], (half_b + 1) * 16, tk)
                hold(pe, o_copied, u, tk)
                n = PAST // P
                for c in range(n + 1):
                    rhs = vals[:, par, c, p * P:(p + 1) * P] if c < n else v_sb[:, NT - 1, p * P:(p + 1) * P]
                    i = pe.matmul(ob[:, 0:P], probs_t[:, c * P:(c + 1) * P], rhs, start=c == 0, stop=c == n)
                i.then_inc(pv_done, 1)

            def turn_o(u):
                hold(pe, o_out, u + 1, tk)
                pe.transpose(ob[:, P:2 * P], o[:, :], const["ident"][:, :]).then_inc(o_turned, 1)

            def body(b, par, half_b, first=False):
                for p in range(2):
                    u = b * 2 + p
                    for c in range(NCHK):
                        scores(u, b, p, half_b, c)
                        if not (first and p == 0):
                            turn(u - 1, 1 - p, c)
                    if not (first and p == 0):
                        if p == 0:
                            values(u - 1, b - 1, 1, 1 - par, None)
                        else:
                            values(u - 1, b, 0, par, half_b)
                        turn_o(u - 1)

            body(0, 0, 0, True)
            body(1, 1, 0)
            with pe.Fori(1, DEC_B // 2) as m:
                body(m * 2, 0, m)
                body(m * 2 + 1, 1, m)
            for c in range(NCHK):
                turn(UNITS - 1, 1, c)
            values(UNITS - 1, DEC_B - 1, 1, 1, None)
            turn_o(UNITS - 1)

        @block.scalar
        def _(act):
            tk = tick["act"]

            def softmax(u, p):
                hold(act, maxed, u + 1, tk)
                act.activation(probs[:, p], probs[:, p], ACT.Exp, bias=neg_max[:, p], accum_out=total[:, p]).then_inc(exped, 1)

            def copy(u, p, c):
                a, e = chunks[c]
                hold(act, turned, u * NCHK + c + 1, tk)
                if c == 0:
                    hold(act, pv_done, u, tk)
                act.activation(probs_t[:, a:e], tr[(c + p * NCHK) % 2][:, 0:e - a], ACT.Copy).then_inc(turned_out, 1)

            def body(b, first=False):
                for p in range(2):
                    u = b * 2 + p
                    if not (first and p == 0):
                        for c in range(NCHK):
                            copy(u - 1, 1 - p, c)
                    softmax(u, p)

            body(0, True)
            with act.Fori(1, DEC_B) as b:
                body(b)
            for c in range(NCHK):
                copy(UNITS - 1, 1, c)

        @block.vector
        def _(dve):
            tk = tick["dve"]

            def maxima(u, p):
                for c, (a, e) in enumerate(chunks):
                    hold(dve, qk_done, u * NCHK + c + 1, tk)
                    if c == 0:
                        hold(dve, turned, (u - 1) * NCHK, tk)
                    dve.tensor_scalar(probs[:, p, a:e], qk[c][:, 0:e - a], 0.0, None, ALU.add, ALU.max,
                                      accum_out=part_max[:, p, c:c + 1]).then_inc(read, 1)
                dve.drain()
                dve.reduce_max(neg_max[:, p], part_max[:, p, :], AX.X)
                dve.drain()
                dve.tensor_scalar(neg_max[:, p], neg_max[:, p], -1.0, None, ALU.mult).then_inc(maxed, 1)

            def outputs(u, b, p):
                hold(dve, exped, u + 1, tk)
                dve.reciprocal(inv[:, p], total[:, p])
                hold(dve, pv_done, u + 1, tk)
                hold(dve, o_turned, u, tk)
                dve.drain()
                dve.tensor_scalar(o[:, :], ob[:, 0:P], inv[:, p], None, ALU.mult).then_inc(o_out, 1)
                hold(dve, o_turned, u + 1, tk)
                for half in range(2):
                    rows = slice(half * HEAD_D, (half + 1) * HEAD_D)
                    dst = o_t[rows, GROUP * p:GROUP * (p + 1), T_PROMPT:T].rearrange("p g (b t) -> p g b t", t=DEC_T)[:, :, b, :]
                    src = ob[rows, P + half * HEAD_D:P + (half + 1) * HEAD_D].rearrange("p (g t) -> p g t", t=DEC_T)
                    i = dve.tensor_copy(dst, src)
                i.then_inc(o_copied, 1)

            def body(b, first=False):
                for p in range(2):
                    maxima(b * 2 + p, p)
                    if not (first and p == 0):
                        outputs(b * 2 + p - 1, b - (1 - p), 1 - p)

            body(0, True)
            with dve.Fori(1, DEC_B) as b:
                body(b)
            outputs(UNITS - 1, DEC_B - 1, 1)
            dve.drain()


def attend_out_phase(nc, env, x):
    io, sem, tick, o_t = env["io"], env["sem"], env["tick"], env["o_t"]
    take = Space(nc, env["o_end"], env["end"]).take
    o_hi = take("ao_o_hi", [P, QB, T], F32R)
    o_lo = take("ao_o_lo", [P, QB, T], F32R, at=env["free"])
    assert 4 * QB * T <= t_at["o_t"] - env["free"]
    raw = take("ao_raw", [P, 2, SLAB])
    w_hi, w_lo = take("ao_w_hi", [P, 2, SLAB], F32R), take("ao_w_lo", [P, 2, SLAB], F32R)

    with ExitStack() as ctx:
        lin = [ctx.enter_context(nc.psum_tensor(f"ao_lin{g}", [P, BANK], F32)) for g in range(G)]
        W = Slabs(nc, sem, "ao", io["weights"], HG_SLABS + FFN_SLABS + DSA_PROJ, KB, 2, raw, w_hi, w_lo, tick)
        hi_set, lo_set, added = sem("ao_hi_set"), sem("ao_lo_set"), sem("ao_added")
        block = ctx.enter_context(nc.Block())

        @block.sync
        def _(sp):
            W.load_all(sp)

        @block.scalar
        def _(act):
            for kb in range(QB):
                act.activation(o_hi[:, kb], o_t[:, kb], ACT.Copy).then_inc(hi_set, 1)
                if kb == 0:
                    W.split_hi(act, 0, 0, 0, 0, 0)
            for s in range(1, KB):
                W.split_hi(act, s, s // 2, s % 2, s % 2, 3 * (s - 1))

        @block.vector
        def _(dve):
            for kb in range(QB):
                dve.wait_ge(hi_set, kb + 1)
                dve.tensor_tensor(o_lo[:, kb], o_t[:, kb], o_hi[:, kb].bitcast(F32), ALU.subtract).then_inc(lo_set, 1)
                if kb == 0:
                    W.split_lo(dve, 0, 0, 0)
            for s in range(KB):
                if s + 1 < KB:
                    W.split_lo(dve, s + 1, (s + 1) % 2, (s + 1) % 2)
                for g in range(G):
                    dve.wait_ge(W.units, 3 * s + g + 1)
                    xs = x[:, s, g * GT:(g + 1) * GT]
                    dve.tensor_tensor(xs, xs, lin[g][:, 0:GT], ALU.add).then_inc(added, 1)
            dve.drain()

        @block.tensor
        def _(pe):
            pe.wait_ge(lo_set, QB)
            for s in range(KB):
                pe.wait_ge(W.lo_done, s + 1)
                for g in range(G):
                    if s:
                        pe.wait_ge(added, 3 * (s - 1) + g + 1)
                    W.block(pe, lin[g][:, 0:GT], s % 2, o_hi, o_lo, g).then_inc(W.units, 1)


def final_phase(nc, env, x):
    io, const, sem, tick = env["io"], env["const"], env["sem"], env["tick"]
    take = Space(nc, env["free"], env["end"]).take
    sq = take("fn_sq", [P, KB, GT])
    std = take("fn_std", [P, G, GT])
    y = take("fn_y", [P, 2, KB, GT])
    gain = take("fn_gain", [P, KB])
    with ExitStack() as ctx:
        bank = [ctx.enter_context(nc.psum_tensor(f"fn_bank{g}", [P, BANK], F32)) for g in range(G)]
        gain_in, squared, summed, rooted, scaled = (sem("fn_" + n) for n in ("gain_in", "squared", "summed", "rooted", "scaled"))
        y_out = [sem(f"fn_y_out{n}") for n in range(2)]
        block = ctx.enter_context(nc.Block())

        @block.sync
        def _(sp):
            sp.dma_start(gain[:, :], io["gains"][4]).then_inc(gain_in, 16)
            for g in range(G):
                sp.wait_ge(scaled, g + 1)
                sp.dma_start(io["y"][:, :, g * GT:(g + 1) * GT], y[:, g % 2]).then_inc(y_out[g % 2], 16)
            sp.wait_ge(y_out[0], 32)
            sp.wait_ge(y_out[1], 16)

        @block.scalar
        def _(act):
            for g in range(G):
                for kb in range(KB):
                    if g:
                        act.wait_ge(summed, (g - 1) * KB + kb + 1)
                    act.activation(sq[:, kb], x[:, kb, g * GT:(g + 1) * GT], ACT.Square).then_inc(squared, 1)
                act.wait_ge(summed, (g + 1) * KB)
                act.activation(std[:, g], bank[g][:, 0:GT], ACT.Sqrt, bias=EPS).then_inc(rooted, 1)

        @block.tensor
        def _(pe):
            for u in range(G * KB):
                pe.wait_ge(squared, u + 1)
                pe.matmul(bank[u // KB][:, 0:GT], const["ones"][:, :], sq[:, u % KB], start=u % KB == 0,
                          stop=u % KB == KB - 1).then_inc(summed, 1)

        @block.vector
        def _(dve):
            dve.wait_ge(gain_in, 16)
            for g in range(G):
                dve.wait_ge(rooted, g + 1)
                dve.reciprocal(std[:, g], std[:, g])
                dve.drain()
                if g >= 2:
                    dve.wait_ge(y_out[g % 2], 16)
                for kb in range(KB):
                    i = dve.scalar_tensor_tensor(y[:, g % 2, kb], x[:, kb, g * GT:(g + 1) * GT], gain[:, kb:kb + 1], std[:, g],
                                                 ALU.mult, ALU.mult)
                i.then_inc(scaled, 1)


FFN_SLABS = 3 * FB
HG_SLABS = 5 * HEADS


def constants():
    s, t = np.arange(P)[:, None], np.arange(P)[None, :]
    tri = (s % CH <= np.arange(CH)[None, :]).astype(np.float32)
    own = ((s // DEC_T == t // DEC_T) & (s <= t)).astype(np.float32)
    own_b = (s // DEC_T == np.arange(DEC_B)[None, :]).astype(np.float32)
    pos = np.arange(T)
    start = np.where(pos < T_PROMPT, pos % CH == 0, pos % DEC_T == 0)
    keep = np.broadcast_to(1.0 - start, (P, T)).astype(mybir.dt.np(BF16))
    return {"tri": tri, "own": own, "own_b": own_b, "keep": keep, "ident": np.eye(P, dtype=np.float32),
            **dsa_constants(),
            "ones": np.full((P, P), 1.0 / D, np.float32), "ones_v": np.full((P, P), 1.0 / P, np.float32)}


def layout(i):
    x = np.concatenate([i["x_prompt"].reshape(T_PROMPT, D), i["x_sample"].reshape(T_SAMPLE, D)])
    w = i["hg_w_in"][0]
    q, f, v, g = (in_slabs(w[:, n * D:(n + 1) * D]) for n in range(4))
    out = down_slabs(i["hg_w_out"][0])
    order = []
    for h in range(HEADS + 2):
        if h >= 2:
            order.append(out[h - 2])
        if h < HEADS:
            order += [f[h], v[h], q[h], g[h]]
    slabs = [np.stack(order)]

    def ffn(layer):
        gate, up = in_slabs(i["ffn_w_in"][layer][:, :D_FF]), in_slabs(i["ffn_w_in"][layer][:, D_FF:])
        down = down_slabs(i["ffn_w_down"][layer])
        order = []
        for c in range(FB // 2 + 1):
            if c < FB // 2:
                order += [gate[2 * c], up[2 * c], gate[2 * c + 1], up[2 * c + 1]]
            if c:
                order += [down[2 * c - 2], down[2 * c - 1]]
        return np.stack(order)

    slabs.append(ffn(0))
    slabs.append(dsa_slabs(i))
    slabs.append(ffn(1))
    gains = np.stack([i["norm_mix"][0], i["norm_ffn"][0], i["norm_mix"][1], i["norm_ffn"][1], i["norm_final"]])
    a = {
        "x": x.T.reshape(KB, P, T).transpose(1, 0, 2),
        "weights": np.concatenate(slabs),
        "gains": gains.reshape(5, KB, P).transpose(0, 2, 1),
        "hg_lb": i["hg_lb"].reshape(2, HEADS, P, 1).transpose(2, 0, 1, 3),
        "hg_norm": i["hg_norm"][0].reshape(P, 1),
        "state_hgrn": i["state_hgrn"][0].transpose(1, 2, 0, 3),
        "state_conv": i["state_conv"].reshape(2, DEC_B, 2, FB, P).transpose(0, 4, 3, 1, 2),
        "conv_p": np.concatenate([i["ffn_conv_w"], i["ffn_conv_b"][:, None]], axis=1).reshape(2, 4, FB, P).transpose(0, 3, 2, 1),
    }
    a.update(dsa_layout(i))
    return {k: np.ascontiguousarray(v) for k, v in {**a, **constants()}.items()}


OUTS = {
    "ki_out": (HEAD_D, T),
    "k_out": (P, 2, T),
    "v_out": (P, NT, N_KV * HEAD_D),
    "y": (P, KB, T),
    "hgrn_p": (HEADS, P, P),
    "hgrn_s": (HEADS, P, DEC_B, P),
    "conv_out": (2, P, FB, (1 + DEC_B) * (CONV_W - 1)),
}


def program(nc, io, phases=None):
    io["q_t"] = nc.dram_tensor("q_t", (QB, P, T), F32, kind="Internal").ap()
    io["qi_t"] = nc.dram_tensor("qi_t", (IDX_B, P, T), F32, kind="Internal").ap()
    with ExitStack() as ctx:
        sem = lambda name: ctx.enter_context(nc.semaphore(name))
        tick = {e: sem("tick_" + e) for e in ("pe", "act", "dve", "pool", "sp")}

        end = nc.sbuf_usable_end // 32 * 32
        free = (nc.sbuf_base + 31) // 32 * 32
        arena = ctx.enter_context(nc.sbuf_tensor("arena", [P, (end - free) // 4 - 16], F32))
        sp_ = Space(nc, free, end)
        x = sp_.take("x", [P, KB, T])
        const = {n: sp_.take("c_" + n, [P, P]) for n in ("ident", "ones", "ones_v")}
        env = {"io": io, "const": const, "sem": sem, "tick": tick, "free": sp_.at, "end": end,
               "x_in": sem("x_in"), "ffn_first": FFN_FIRST, "ffn_gain": (1, 3),
               "norm_sems": [sem("norm_" + n) for n in ("squared", "summed", "rooted", "scaled", "hi_done", "lo_done")]}
        consts_in, x_out = sem("consts_in"), sem("x_out")
        with nc.Block() as block:
            @block.sync
            def _(sp):
                sp.dma_start(x[:, :, :], io["x"]).then_inc(env["x_in"], 16)
                for n in const:
                    sp.dma_start(const[n][:, :], io[n]).then_inc(consts_in, 16)
                sp.wait_ge(consts_in, 16 * len(const))
        for name, phase in PHASES:
            if phases is None or name in phases:
                phase(nc, env, x)


PHASES = [("hgrn", hgrn_phase), ("ffn0", lambda nc, env, x: ffn_phase(nc, env, x, 0)), ("proj", project_phase),
          ("select", select_phase), ("attp", attend_prompt_phase), ("atts", attend_sample_phase), ("ato", attend_out_phase),
          ("ffn1", lambda nc, env, x: ffn_phase(nc, env, x, 1)), ("final", final_phase)]
FFN_FIRST = (HG_SLABS, HG_SLABS + FFN_SLABS + DSA_PROJ + KB)


def kernel(**inputs):
    import concourse.bacc as bacc
    from concourse.bass_utils import run_bass_kernel_spmd

    nc = bacc.Bacc("TRN2", target_bir_lowering=False, num_devices=1)
    arrays = layout({name: np.asarray(a) for name, a in inputs.items()})
    io = {name: nc.dram_tensor("in_" + name, a.shape, mybir.dt.from_np(a.dtype), kind="ExternalInput").ap()
          for name, a in arrays.items()}
    for name, shape in OUTS.items():
        io[name] = nc.dram_tensor("out_" + name, shape, F32, kind="ExternalOutput").ap()
    program(nc, io)
    r = run_bass_kernel_spmd(nc, [{"in_" + name: a for name, a in arrays.items()}], core_ids=[0]).results[0]
    out = {name: r["out_" + name] for name in OUTS}

    def frames(a, tail):
        return a[:T_PROMPT].reshape((1, T_PROMPT) + tail), a[T_PROMPT:].reshape((DEC_B, DEC_T) + tail)

    y_p, y_s = frames(out["y"].transpose(2, 1, 0).reshape(T, D), (D,))
    k_p, k_s = frames(out["k_out"].transpose(2, 1, 0).reshape(T, N_KV * HEAD_D), (N_KV, HEAD_D))
    v_p, v_s = frames(out["v_out"].transpose(1, 0, 2).reshape(T, N_KV * HEAD_D), (N_KV, HEAD_D))
    ki_p, ki_s = frames(out["ki_out"].T, (HEAD_D,))
    conv = out["conv_out"].transpose(0, 3, 2, 1).reshape(2, 1 + DEC_B, CONV_W - 1, D_FF)
    return (y_p, y_s, k_p[None], v_p[None], ki_p[None], out["hgrn_p"][None, None], conv[:, :1],
            k_s[None], v_s[None], ki_s[None], out["hgrn_s"].transpose(2, 0, 1, 3)[None], conv[:, 1:])
```

```python
from contextlib import ExitStack

import numpy as np

import concourse.bass as bass
from concourse import mybir

ALU = mybir.AluOpType
ACT = mybir.ActivationFunctionType
AX = mybir.AxisListType
F32 = mybir.dt.float32
F32R = mybir.dt.float32r
BF16 = mybir.dt.bfloat16

P = 128
EPS = 1e-6
D = 1024
KB = D // P
T_PROMPT = 1024
DEC_B = 8
DEC_T = 16
T_SAMPLE = DEC_B * DEC_T
T = T_PROMPT + T_SAMPLE
NT = T // P
PT = NT - 1
G = 3
GT = T // G
SLAB = KB * P
PAST = 2048
HEADS = 8
CH = 64
NC = T_PROMPT // CH
SB = 16
NS = CH // SB
NCH = NC + DEC_B
CLAMP = 1e18
D_FF = 2816
FB = D_FF // P
CONV_W = 3
BANK = 512
NEG = -1e30


def hold(eng, sem, value, tick):
    if isinstance(value, int):
        if value > 0:
            eng.wait_ge(sem, value)
    else:
        eng.wait_ge(sem, value)
        eng.sem_inc(tick, 1)


class Space:

    def __init__(self, nc, at, end):
        self.nc, self.at, self.end = nc, at, end

    def take(self, name, shape, dtype=F32, at=None):
        size = int(np.prod(shape[1:])) * (2 if dtype == BF16 else 4)
        size = (size + 31) // 32 * 32
        if at is None:
            at = self.at
            self.at += size
            assert self.at <= self.end, (name, self.at - self.end)
        t = self.nc.alloc_sbuf_tensor_at(name, list(shape), dtype, offset=at)
        t_at[name] = at
        return t


t_at = {}


class Norm:

    R = 3

    def __init__(self, env, x, gain, ones, h_hi, h_lo, sq, std, t, banks, x_in=None):
        self.x, self.gain, self.ones, self.h_hi, self.h_lo = x, gain, ones, h_hi, h_lo
        self.x_in = x_in
        self.sq, self.std, self.t, self.banks = sq, std, t, banks
        self.squared, self.summed, self.rooted, self.scaled, self.hi_done, self.lo_done = env["norm_sems"]
        self.blocks, self.groups = env["norms"] * G * KB, env["norms"] * G
        env["norms"] += 1

    def square(self, act, g, kb):
        u = g * KB + kb
        if self.x_in and kb == 0:
            act.wait_ge(self.x_in[g], 16)
        if u >= self.R:
            act.wait_ge(self.summed, self.blocks + u - self.R + 1)
        act.activation(self.sq[:, u % self.R], self.x[:, kb, g * GT:(g + 1) * GT], ACT.Square).then_inc(self.squared, 1)

    def root(self, act, g):
        act.wait_ge(self.summed, self.blocks + (g + 1) * KB)
        act.activation(self.std[:, g], self.banks[g][:, 0:GT], ACT.Sqrt, bias=EPS).then_inc(self.rooted, 1)

    def high(self, act, g, kb):
        u = g * KB + kb
        act.wait_ge(self.scaled, self.blocks + u + 1)
        act.activation(self.h_hi[:, kb, g * GT:(g + 1) * GT], self.t[:, u % self.R], ACT.Copy).then_inc(self.hi_done, 1)

    def wait_group(self, eng, g):
        eng.wait_ge(self.lo_done, self.blocks + (g + 1) * KB)

    def on_scalar(self, act, between):
        for kb in range(KB):
            self.square(act, 0, kb)
        for g in range(G):
            self.root(act, g)
            for kb in range(KB):
                self.high(act, g, kb)
                if g + 1 < G:
                    self.square(act, g + 1, kb)
            if g == 0:
                between()

    def on_tensor(self, pe, g):
        for kb in range(KB):
            u = g * KB + kb
            pe.wait_ge(self.squared, self.blocks + u + 1)
            pe.matmul(self.banks[g][:, 0:GT], self.ones[:, :], self.sq[:, u % self.R], start=kb == 0,
                      stop=kb == KB - 1).then_inc(self.summed, 1)

    def on_vector(self, dve, between):
        for g in range(G):
            dve.wait_ge(self.rooted, self.groups + g + 1)
            dve.reciprocal(self.std[:, g], self.std[:, g])
            dve.drain()
            for kb in range(KB):
                u = g * KB + kb
                if u >= self.R:
                    dve.wait_ge(self.lo_done, self.blocks + u - self.R + 1)
                dve.scalar_tensor_tensor(self.t[:, u % self.R], self.x[:, kb, g * GT:(g + 1) * GT], self.gain[:, kb:kb + 1],
                                         self.std[:, g], ALU.mult, ALU.mult).then_inc(self.scaled, 1)
            if g == 0:
                between()

    def on_pool(self, pool):
        for u in range(G * KB):
            g, kb = divmod(u, KB)
            pool.wait_ge(self.hi_done, self.blocks + u + 1)
            pool.tensor_tensor(self.h_lo[:, kb, g * GT:(g + 1) * GT], self.t[:, u % self.R],
                               self.h_hi[:, kb, g * GT:(g + 1) * GT].bitcast(F32), ALU.subtract).then_inc(self.lo_done, 1)


class Slabs:

    def __init__(self, nc, sem, tag, weights, first, n, ring, raw, hi, lo, tick):
        self.weights, self.first, self.n, self.ring = weights, first, n, ring
        self.raw, self.hi, self.lo, self.tick = raw, hi, lo, tick
        self.loaded = [sem(f"{tag}_loaded{k}") for k in range(2)]
        self.hi_done = sem(tag + "_w_hi")
        self.lo_done = sem(tag + "_w_lo")
        self.units = sem(tag + "_units")

    def load_all(self, sp):
        for s in range(2):
            sp.dma_start(self.raw[:, s], self.weights[self.first + s]).then_inc(self.loaded[s], 16)
        with sp.Fori(1, self.n // 2) as m:
            for par in range(2):
                hold(sp, self.lo_done, m * 2 + par - 1, self.tick["sp"])
                sp.dma_start(self.raw[:, par], self.weights[m * 2 + (self.first + par)]).then_inc(self.loaded[par], 16)
        if self.n % 2:
            s = self.n - 1
            sp.wait_ge(self.lo_done, s - 1)
            sp.dma_start(self.raw[:, 0], self.weights[self.first + s]).then_inc(self.loaded[0], 16)

    def split_hi(self, act, s, half, slot, par, used):
        hold(act, self.loaded[par], (half + 1) * 16, self.tick["act"])
        hold(act, self.units, used, self.tick["act"])
        act.activation(self.hi[:, slot], self.raw[:, par], ACT.Copy).then_inc(self.hi_done, 1)

    def split_lo(self, dve, s, slot, par):
        hold(dve, self.hi_done, s + 1, self.tick["dve"])
        dve.tensor_tensor(self.lo[:, slot], self.raw[:, par], self.hi[:, slot].bitcast(F32),
                          ALU.subtract).then_inc(self.lo_done, 1)

    def product(self, pe, out, slot, col, x_hi, x_lo, start, stop):
        w_hi, w_lo = self.hi[:, slot, col:col + P], self.lo[:, slot, col:col + P]
        pe.matmul(out, w_hi, x_hi, start=start, stop=False)
        pe.matmul(out, w_hi, x_lo, start=False, stop=False)
        return pe.matmul(out, w_lo, x_hi, start=False, stop=stop)

    def block(self, pe, out, slot, h_hi, h_lo, g):
        for kb in range(KB):
            last = self.product(pe, out, slot, kb * P, h_hi[:, kb, g * GT:(g + 1) * GT], h_lo[:, kb, g * GT:(g + 1) * GT],
                                kb == 0, kb == KB - 1)
        return last


def pieces(n):
    return [(a, min(a + BANK, n)) for a in range(0, n, BANK)]


def spread(ap, shape):
    return ap.broadcast_to(shape)


def hgrn_phase(nc, env, x):
    io, const, sem, tick = env["io"], env["const"], env["sem"], env["tick"]
    sp_ = Space(nc, env["free"], env["end"])
    take = sp_.take
    h_hi, h_lo = take("hg_h_hi", [P, KB, T], F32R), take("hg_h_lo", [P, KB, T], F32R)
    raw = take("hg_raw", [P, 2, SLAB])
    w_hi, w_lo = take("hg_w_hi", [P, 2, SLAB], F32R), take("hg_w_lo", [P, 2, SLAB], F32R)
    decay = take("hg_G", [P, T])
    tmp1, tmp2 = take("hg_tmp1", [P, T]), take("hg_tmp2", [P, T])
    q_dec = take("hg_q_dec", [P, T])
    q_mid = take("hg_q_mid", [P, T])
    k_end = take("hg_k_end", [P, T])
    k_endT = take("hg_k_endT", [P, NT, P])
    turn_rows = k_endT[:, :, :].rearrange("p t c -> p (t c)")
    vals = take("hg_v", [P, NT, P])
    gate = take("hg_gate", [P, T])
    attT = take("hg_attT", [P, PT * CH])
    attTs = take("hg_attTs", [P, P])
    k_mid = take("hg_k_mid", [P, NC * SB * NS * (NS + 1) // 2])
    states = take("hg_states", [P, NC, P], at=t_at["hg_k_mid"])
    k_mids = take("hg_k_mids", [P, T_SAMPLE])
    v_own = take("hg_v_own", [P, DEC_B, P])
    s_new = take("hg_s_new", [P, DEC_B, P], at=t_at["hg_v_own"])
    s_old = take("hg_s_old", [P, DEC_B, P])
    o_hi, o_lo = take("hg_o_hi", [P, T], F32R), take("hg_o_lo", [P, T], F32R)
    o_work = take("hg_o_work", [P, T], at=t_at["hg_o_lo"])[:, :]
    keep = take("hg_keep", [P, T], BF16)
    e_end = take("hg_e_end", [P, NCH])
    tri, own = take("hg_tri", [P, CH]), take("hg_own", [P, P])
    own_b = take("hg_own_b", [P, DEC_B])
    lbs = take("hg_lbs", [P, 2, HEADS, 1])
    small = take("hg_small", [P, KB + 1])
    lb_t = take("hg_lb_t", [P, 2, HEADS, 1])
    sq = take("hg_sq", [P, Norm.R, GT], at=t_at["hg_k_endT"])
    std = take("hg_std", [P, G, GT], at=t_at["hg_o_hi"])
    nt = take("hg_nt", [P, Norm.R, GT], at=t_at["hg_o_lo"])

    with ExitStack() as ctx:
        lin = [ctx.enter_context(nc.psum_tensor(f"hg_lin{g}", [P, BANK], F32)) for g in range(G)]
        rb = [ctx.enter_context(nc.psum_tensor(f"hg_rec{g}", [P, BANK], F32)) for g in range(5)]
        W = Slabs(nc, sem, "hg", io["weights"], 0, 40, 2, raw, w_hi, w_lo, tick)
        N = Norm(env, x, small, const["ones"], h_hi, h_lo, sq, std, nt, lin, env["x_in"])
        consts_in = sem("hg_consts_in")
        lb_ready = sem("hg_lb_ready")
        act_evac, dve_evac = sem("hg_act_evac"), sem("hg_dve_evac")
        f_act, f_dve = sem("hg_f_act"), sem("hg_f_dve")
        q_act, q_dve = sem("hg_q_act"), sem("hg_q_dve")
        turned, turned_out = sem("hg_turned"), sem("hg_turned_out")
        att_done, att_masked = sem("hg_att_done"), sem("hg_att_masked")
        v_rows_set, v_turned = sem("hg_v_rows_set"), sem("hg_v_turned")
        v_spread = sem("hg_v_spread")
        ds_done, chained = sem("hg_ds_done"), sem("hg_chained")
        o_done, ss_done = sem("hg_o_done"), sem("hg_ss_done")
        n_act, n_dve = sem("hg_n_act"), sem("hg_n_dve")
        s_in, sp_out, ss_out = sem("hg_s_in"), sem("hg_sp_out"), sem("hg_ss_out")
        gated = sem("hg_gated")
        block = ctx.enter_context(nc.Block())

        def k_at(i):
            return NC * SB * i * (i + 1) // 2

        def ds_at(c):
            return rb[c % 2 * 2 + c // 8][:, c // 2 % 4 * P:(c // 2 % 4 + 1) * P]

        def o_parts(buf):
            chunks = buf[:, 0:T_PROMPT].rearrange("p (c two t) -> p c two t", two=2, t=CH)
            banks = [(chunks[:, :, n], rb[1 + n][:, :].rearrange("p (c t) -> p c t", t=CH)) for n in range(2)]
            return banks + [(buf[:, T_PROMPT:T], rb[3][:, 0:T_SAMPLE])]

        def units_before(h):
            if isinstance(h, int) and h == HEADS + 1:
                return units_before(HEADS) + 24
            return 12 * h if isinstance(h, int) and h < 2 else (h - 2) * 36 + 24

        def slab_base(h):
            if isinstance(h, int) and h == HEADS + 1:
                return slab_base(HEADS) + 1
            return 4 * h if isinstance(h, int) and h < 2 else (h - 2) * 5 + 8

        def body_slabs(h):
            out_p = isinstance(h, int) and h < 2
            return 0 if out_p else 1

        @block.sync
        def _(sp):
            sp.dma_start(tri[:, :], io["tri"]).then_inc(consts_in, 16)
            sp.dma_start(own[:, :], io["own"]).then_inc(consts_in, 16)
            sp.dma_start(own_b[:, :], io["own_b"]).then_inc(consts_in, 16)
            sp.dma_start(keep[:, :], io["keep"]).then_inc(consts_in, 16)
            sp.dma_start(lbs[:, :, :, :], io["hg_lb"]).then_inc(consts_in, 16)
            sp.dma_start(small[:, 0:KB], io["gains"][0]).then_inc(consts_in, 16)
            sp.dma_start(small[:, KB:KB + 1], io["hg_norm"]).then_inc(consts_in, 16)
            for g in range(1, G):
                load_x(sp, io, x, env["x_in"], g)
            W.load_all(sp)

        @block.gpsimd
        def _(pool):
            pool.dma_start(s_old[:, :, :], io["state_hgrn"][0]).then_inc(s_in, 16)

            N.on_pool(pool)

            def states_out(r):
                hold(pool, chained, r * 2 + 1, tick["pool"])
                pool.dma_start(io["hgrn_p"][r], states[:, NC - 1]).then_inc(sp_out, 16)
                hold(pool, chained, r * 2 + 2, tick["pool"])
                pool.dma_start(io["hgrn_s"][r], s_new[:, :, :]).then_inc(ss_out, 16)

            with pool.Fori(0, HEADS - 1) as r:
                states_out(r)
                hold(pool, o_done, r + 1, tick["pool"])
                pool.dma_start(s_old[:, :, :], io["state_hgrn"][r + 1]).then_inc(s_in, 16)
            states_out(HEADS - 1)
            pool.wait_ge(sp_out, 16 * HEADS)
            pool.wait_ge(ss_out, 16 * HEADS)

        def split_used(h, k):
            first = units_before(h)
            outp = 24 if body_slabs(h) else 0
            if k == 0:
                return first
            if k == 1:
                return first + outp
            return first + outp + 3 * (k - 1)

        def slab_no(h, k):
            return slab_base(h) + body_slabs(h) + k

        def pars(first_par, h, k):
            return (first_par + body_slabs(h) + k) % 2

        def half(h, par0, k):
            off = body_slabs(h) + k
            if isinstance(h, int):
                return (slab_base(h) + off) // 2
            m, odd = loop_m[0]
            return m * 5 + ((13 if odd else 8) + off) // 2

        loop_m = [None]

        def over_bodies(eng, body):
            body(0, 0)
            body(1, 0)
            with eng.Fori(0, 3) as m:
                loop_m[0] = (m, 0)
                body(m * 2 + 2, 0)
                loop_m[0] = (m, 1)
                body(m * 2 + 3, 1)
            body(8, 0)
            body(9, 1)

        def has(h, low, high):
            return not isinstance(h, int) or low <= h < high

        @block.scalar
        def _(act):
            N.on_scalar(act, lambda: W.split_hi(act, 0, 0, 0, 0, 0))
            act.wait_ge(consts_in, 16 * 7)
            act.activation(lb_t[:, :, :, :], lbs[:, :, :, :], ACT.Exp).then_inc(lb_ready, 1)
            tk = tick["act"]

            def hi(h, par0, k):
                s, par = slab_no(h, k), pars(par0, h, k)
                W.split_hi(act, s, half(h, par0, k), par, par, split_used(h, k))

            def body(h, par0):
                r = h - 1
                if has(h, 1, 9):
                    hold(act, turned, r + 1, tk)
                    hold(act, gated, h, tk)
                    for n, (a, b) in enumerate(pieces(T)):
                        i = act.activation(k_endT[:, a // P:b // P, :], rb[n][:, 0:b - a], ACT.Copy)
                    i.then_inc(turned_out, 1)
                if isinstance(h, int) and h == 8:
                    W.split_hi(act, 39, 19, 1, 1, units_before(8))
                if has(h, 0, 8):
                    if body_slabs(h):
                        hi(h, par0, 0)
                    hi(h, par0, 1)
                    base = units_before(h) + (24 if body_slabs(h) else 0)
                    for g in range(G):
                        hold(act, W.units, base + g + 1, tk)
                        act.activation(tmp1[:, g * GT:(g + 1) * GT], lin[g][:, 0:GT], ACT.Exp, scale=-1.0).then_inc(act_evac, 1)
                    hold(act, f_dve, h * 4 + 1, tk)
                    act.activation(tmp1[:, :], tmp2[:, :], ACT.Ln).then_inc(f_act, 1)
                    hi(h, par0, 2)
                    hold(act, f_dve, h * 4 + 2, tk)
                    act.activation(e_end[:, 0:NC], decay[:, CH - 1:T_PROMPT:CH], ACT.Exp)
                    act.activation(e_end[:, NC:NCH], decay[:, T_PROMPT + DEC_T - 1:T:DEC_T], ACT.Exp)
                if has(h, 1, 9):
                    hold(act, o_done, r + 1, tk)
                    for dst, src in o_parts(o_work):
                        i = act.activation(dst, src, ACT.Square)
                    i.then_inc(n_act, 1)
                if has(h, 0, 8):
                    for g in range(G):
                        hold(act, W.units, base + 3 + g + 1, tk)
                        act.activation(turn_rows[:, g * GT:(g + 1) * GT], lin[g][:, 0:GT], ACT.Copy).then_inc(v_rows_set, 1)
                    for g in range(G):
                        hold(act, v_turned, h * 3 + g + 1, tk)
                        act.activation(vals[:, 3 * g:3 * g + 3, :], lin[g][:, 0:GT], ACT.Copy).then_inc(act_evac, 1)
                    hi(h, par0, 3)
                    hold(act, f_dve, h * 4 + 3, tk)
                    act.activation(k_mid[:, :], k_mid[:, :], ACT.Exp)
                    act.activation(k_mids[:, :], k_mids[:, :], ACT.Exp).then_inc(f_act, 1)
                    act.activation(k_end[:, :], k_end[:, :], ACT.Exp).then_inc(f_act, 1)
                if has(h, 1, 9):
                    hold(act, ss_done, r + 1, tk)
                    for (a, b), src in zip(pieces(T), (rb[0][:, :], rb[4][:, :], rb[3][:, P:2 * P])):
                        act.activation(o_work[:, a:b], src, ACT.Ln, bias=EPS)
                    act.drain()
                    act.activation(o_work, o_work, ACT.Exp, scale=-0.5).then_inc(n_act, 1)
                if has(h, 0, 8):
                    hold(act, f_dve, h * 4 + 4, tk)
                    for g in range(G):
                        hold(act, W.units, base + 6 + g + 1, tk)
                        act.activation(q_dec[:, g * GT:(g + 1) * GT], lin[g][:, 0:GT], ACT.Copy, scale=0.5)
                        act.activation(q_mid[:, g * GT:(g + 1) * GT], lin[g][:, 0:GT], ACT.Tanh, scale=0.5).then_inc(act_evac, 1)
                    hi(h, par0, 4)
                if has(h, 1, 9):
                    hold(act, n_dve, r * 2 + 1, tk)
                    act.activation(o_hi[:, :], o_work, ACT.Copy).then_inc(n_act, 1)
                if has(h, 0, 8):
                    hold(act, q_dve, h * 2 + 1, tk)
                    act.activation(turn_rows, turn_rows, ACT.Exp)
                    act.activation(tmp2[:, :], decay[:, :], ACT.Exp).then_inc(q_act, 1)
                    hold(act, q_dve, h * 2 + 2, tk)
                    for g in range(G):
                        hold(act, W.units, base + 9 + g + 1, tk)
                        act.activation(gate[:, g * GT:(g + 1) * GT], lin[g][:, 0:GT], ACT.Copy, scale=0.5)
                        act.activation(turn_rows[:, g * GT:(g + 1) * GT], lin[g][:, 0:GT], ACT.Tanh, scale=0.5).then_inc(act_evac, 1)

            over_bodies(act, body)

        @block.vector
        def _(dve):
            tk = tick["dve"]
            dve.wait_ge(consts_in, 16 * 7)
            N.on_vector(dve, lambda: W.split_lo(dve, 0, 0, 0))
            dve.wait_ge(lb_ready, 1)
            dve.tensor_tensor(lbs[:, 0], lb_t[:, 0], lb_t[:, 1], ALU.add)
            dve.drain()
            dve.reciprocal(lbs[:, 1], lbs[:, 0])
            dve.drain()
            dve.tensor_tensor(lbs[:, 0], lb_t[:, 0], lbs[:, 1], ALU.mult)
            dve.drain()
            dve.tensor_scalar(lbs[:, 1], lbs[:, 0], -1.0, 1.0, ALU.mult, ALU.add)
            dve.memset(attT[:, :], 0.0)
            dve.drain()

            def lo(h, par0, k):
                par = pars(par0, h, k)
                W.split_lo(dve, slab_no(h, k), par, par)

            def body(h, par0):
                r = h - 1
                if has(h, 1, 9):
                    hold(dve, att_done, r + 1, tk)
                    for half_ in range(2):
                        for i in range(NS):
                            rows = slice(half_ * CH, half_ * CH + SB * (i + 1))
                            dst = attT[rows, :].rearrange("p (c t) -> p c t", t=CH)[:, :, i * SB:(i + 1) * SB]
                            src = rb[3][rows, :].rearrange("p (c t) -> p c t", t=CH)[:, :, i * SB:(i + 1) * SB]
                            dve.tensor_tensor(dst, src, spread(tri[rows, i * SB:(i + 1) * SB].unsqueeze(1), dst.shape), ALU.mult)
                    dve.tensor_tensor(attTs[:, :], rb[4][:, 0:P], own[:, :], ALU.mult).then_inc(att_masked, 1)
                    hold(dve, ss_out, r * 16, tk)
                    dve.tensor_tensor(v_own[:, :, :], spread(vals[:, NT - 1, :].unsqueeze(1), [P, DEC_B, P]),
                                      spread(own_b[:, :].unsqueeze(2), [P, DEC_B, P]), ALU.mult).then_inc(v_spread, 1)
                if has(h, 0, 8) and body_slabs(h):
                    lo(h, par0, 0)
                if isinstance(h, int) and h == 8:
                    W.split_lo(dve, 39, 1, 1)
                if has(h, 2, 10):
                    dve.drain()
                    for nb in range(KB):
                        for g in range(G):
                            hold(dve, W.units, units_before(h) + nb * G + g + 1, tk)
                            xs = x[:, nb, g * GT:(g + 1) * GT]
                            dve.tensor_tensor(xs, xs, lin[g][:, 0:GT], ALU.add).then_inc(dve_evac, 1)
                if has(h, 1, 9):
                    hold(dve, ds_done, r * 3 + 1, tk)
                    dve.tensor_copy(states[:, 0], rb[0][:, 0:P])
                    for c in range(1, NC):
                        dve.drain()
                        i = dve.scalar_tensor_tensor(states[:, c], states[:, c - 1], e_end[:, c:c + 1],
                                                     ds_at(c), ALU.mult, ALU.add)
                    i.then_inc(chained, 1)
                    hold(dve, ds_done, r * 3 + 3, tk)
                    hold(dve, s_in, (r + 1) * 16, tk)
                    for b in range(DEC_B):
                        i = dve.scalar_tensor_tensor(s_new[:, b], s_old[:, b], e_end[:, NC + b:NC + b + 1],
                                                     (rb[4] if b < 4 else rb[0])[:, b % 4 * P:(b % 4 + 1) * P], ALU.mult, ALU.add)
                    i.then_inc(chained, 1)
                if has(h, 0, 8):
                    lo(h, par0, 1)
                    hold(dve, act_evac, h * 12 + 3, tk)
                    dve.tensor_scalar(tmp1[:, :], tmp1[:, :], 1.0, None, ALU.add)
                    dve.drain()
                    dve.reciprocal(tmp1[:, :], tmp1[:, :])
                    dve.drain()
                    dve.tensor_scalar(tmp2[:, :], tmp1[:, :], lb_col(1), lb_col(0), ALU.mult, ALU.add).then_inc(f_dve, 1)
                    dve.drain()
                    dve.tensor_scalar(q_mid[:, :], tmp2[:, :], -1.0, 1.0, ALU.mult, ALU.add)
                    lo(h, par0, 2)
                    hold(dve, f_act, h * 3 + 1, tk)
                    dve.tensor_tensor_scan(decay[:, :], keep[:, :], tmp1[:, :], 0.0, ALU.mult, ALU.add).then_inc(f_dve, 1)
                    dve.drain()
                    if has(h, 1, 8):
                        hold(dve, o_done, r + 1, tk)
                        hold(dve, sp_out, (r + 1) * 16, tk)
                    gp = decay[:, 0:T_PROMPT].rearrange("p (c t) -> p c t", t=CH)
                    for i in range(NS):
                        n = SB * (i + 1)
                        km = k_mid[:, k_at(i):k_at(i + 1)].rearrange("p (c t) -> p c t", t=n)
                        mid = i * SB + SB // 2 - 1
                        dve.tensor_tensor(km, spread(gp[:, :, mid:mid + 1], [P, NC, n]), gp[:, :, 0:n], ALU.subtract)
                    gs = decay[:, T_PROMPT:T].rearrange("p (b t) -> p b t", t=DEC_T)
                    mid = SB // 2 - 1
                    kms = k_mids[:, :].rearrange("p (b t) -> p b t", t=DEC_T)
                    dve.tensor_tensor(kms, spread(gs[:, :, mid:mid + 1], [P, DEC_B, DEC_T]), gs, ALU.subtract)
                    ke = k_end[:, 0:T_PROMPT].rearrange("p (c t) -> p c t", t=CH)
                    dve.tensor_tensor(ke, spread(gp[:, :, CH - 1:CH], [P, NC, CH]), gp, ALU.subtract)
                    kes = k_end[:, T_PROMPT:T].rearrange("p (b t) -> p b t", t=DEC_T)
                    dve.tensor_tensor(kes, spread(gs[:, :, DEC_T - 1:DEC_T], [P, DEC_B, DEC_T]), gs, ALU.subtract).then_inc(f_dve, 1)
                    hold(dve, f_act, h * 3 + 2, tk)
                    kp = q_mid[:, 0:T_PROMPT].rearrange("p (c t) -> p c t", t=CH)
                    for i in range(NS):
                        n = SB * (i + 1)
                        km = k_mid[:, k_at(i):k_at(i + 1)].rearrange("p (c t) -> p c t", t=n)
                        dve.scalar_tensor_tensor(km, km, CLAMP, kp[:, :, 0:n], ALU.min, ALU.mult)
                    dve.scalar_tensor_tensor(k_mids[:, :], k_mids[:, :], CLAMP, q_mid[:, T_PROMPT:T], ALU.min, ALU.mult)
                    hold(dve, f_act, h * 3 + 3, tk)
                    dve.tensor_tensor(k_end[:, :], k_end[:, :], q_mid[:, :], ALU.mult).then_inc(f_dve, 1)
                    lo(h, par0, 3)
                if has(h, 1, 9):
                    hold(dve, n_act, r * 3 + 2, tk)
                    for (dst, src), (scale, _) in zip(o_parts(o_work), o_parts(o_work)):
                        dve.scalar_tensor_tensor(dst, src, small[:, KB:KB + 1], scale, ALU.mult, ALU.mult)
                    dve.drain()
                    dve.tensor_tensor(o_work, o_work, gate[:, :], ALU.mult).then_inc(n_dve, 1)
                if has(h, 0, 8):
                    hold(dve, act_evac, h * 12 + 9, tk)
                    dve.scalar_tensor_tensor(q_dec[:, :], q_mid[:, :], 1.0, q_dec[:, :], ALU.add, ALU.mult)
                    g16 = decay[:, :].rearrange("p (n t) -> p n t", t=SB)
                    dve.tensor_tensor(turn_rows.rearrange("p (n t) -> p n t", t=SB), g16,
                                      spread(g16[:, :, SB // 2 - 1:SB // 2], [P, T // SB, SB]), ALU.subtract).then_inc(q_dve, 1)
                    lo(h, par0, 4)
                if has(h, 1, 9):
                    hold(dve, n_act, r * 3 + 3, tk)
                    dve.tensor_tensor(o_lo[:, :], o_work, o_hi[:, :].bitcast(F32), ALU.subtract).then_inc(n_dve, 1)
                if has(h, 0, 8):
                    hold(dve, q_act, h + 1, tk)
                    dve.scalar_tensor_tensor(q_mid[:, :], turn_rows, CLAMP, q_dec[:, :], ALU.min, ALU.mult)
                    dve.drain()
                    dve.tensor_tensor(q_dec[:, :], q_dec[:, :], tmp2[:, :], ALU.mult).then_inc(q_dve, 1)
                    hold(dve, act_evac, h * 12 + 12, tk)
                    dve.scalar_tensor_tensor(gate[:, :], turn_rows, 1.0, gate[:, :], ALU.add, ALU.mult).then_inc(gated, 1)

            def lb_col(which):
                h = cur[0]
                return lbs[:, which, h]

            cur = [0]

            def body_(h, par0):
                cur[0] = h
                body(h, par0)

            over_bodies(dve, body_)
            dve.drain()

        @block.tensor
        def _(pe):
            tk = tick["pe"]
            ident = const["ident"]
            N.on_tensor(pe, 0)
            N.on_tensor(pe, 1)

            def body(h, par0):
                r = h - 1
                has_out = body_slabs(h)
                first = units_before(h)
                if has(h, 1, 9):
                    hold(pe, f_dve, r * 4 + 4, tk)
                    hold(pe, q_dve, r * 2 + 2, tk)
                    if has(h, 2, 9):
                        hold(pe, n_dve, r * 2 - 1, tk)
                    for t in range(NT):
                        i = pe.transpose(rb[t // 4][:, t % 4 * P:(t % 4 + 1) * P], k_end[:, t * P:(t + 1) * P], ident[:, :])
                    i.then_inc(turned, 1)
                    for c in range(NC):
                        rows, col = c % 2 * CH, c // 2 * CH
                        for i_ in range(NS):
                            n = SB * (i_ + 1)
                            at = k_at(i_) + c * n
                            pe.matmul(rb[3][rows:rows + n, col + i_ * SB:col + (i_ + 1) * SB], k_mid[:, at:at + n],
                                      q_mid[:, c * CH + i_ * SB:c * CH + (i_ + 1) * SB], start=True, stop=True)
                    pe.matmul(rb[4][:, 0:P], k_mids[:, :], q_mid[:, T_PROMPT:T], start=True, stop=True).then_inc(att_done, 1)
                if has_out and has(h, 2, 10):
                    hold(pe, n_dve, (h - 2) * 2 + 2, tk)
                    hold(pe, W.lo_done, slab_base(h) + 1, tk)
                    for nb in range(KB):
                        for g in range(G):
                            n = nb * G + g
                            if n < G and has(h, 2, 9):
                                hold(pe, act_evac, h * 12 - 2 + n, tk)
                            else:
                                hold(pe, dve_evac, (h - 2) * 24 + n - 2, tk)
                            W.product(pe, lin[g][:, 0:GT], par0, nb * P, o_hi[:, g * GT:(g + 1) * GT],
                                      o_lo[:, g * GT:(g + 1) * GT], True, True).then_inc(W.units, 1)
                if has(h, 1, 9):
                    hold(pe, turned_out, r + 1, tk)
                    hold(pe, att_masked, r + 1, tk)
                    for c in range(NC):
                        rows = slice(c % 2 * CH, (c % 2 + 1) * CH)
                        i = pe.matmul(ds_at(c), k_endT[rows, c // 2, :], vals[rows, c // 2, :],
                                      start=True, stop=True)
                    i.then_inc(ds_done, 1)
                    hold(pe, v_spread, r + 1, tk)
                    pe.matmul(rb[4][:, :], k_endT[:, NT - 1, :], v_own[:, 0:4, :].rearrange("p b v -> p (b v)"),
                              start=True, stop=True).then_inc(ds_done, 1)
                if has(h, 0, 8):
                    hold(pe, W.lo_done, slab_no(h, 0) + 1, tk)
                    for g in range(G):
                        if isinstance(h, int) and h == 0:
                            N.wait_group(pe, g)
                        elif isinstance(h, int) and h == 1:
                            pe.wait_ge(act_evac, 12 - 2 + g)
                        else:
                            hold(pe, dve_evac, (h - 1) * 24 - 2 + g, tk)
                        W.block(pe, lin[g][:, 0:GT], pars(par0, h, 0), h_hi, h_lo, g).then_inc(W.units, 1)
                        if isinstance(h, int) and h == 0 and g == 0:
                            N.on_tensor(pe, 2)
                if has(h, 1, 9):
                    hold(pe, chained, r * 2 + 1, tk)
                    pe.matmul(rb[0][:, :], k_endT[:, NT - 1, :], v_own[:, 4:8, :].rearrange("p b v -> p (b v)"),
                              start=True, stop=True).then_inc(ds_done, 1)
                    for c in range(NC):
                        rows = slice(c % 2 * CH, (c % 2 + 1) * CH)
                        out = rb[1 + c % 2][:, c // 2 * CH:(c // 2 + 1) * CH]
                        pe.matmul(out, vals[rows, c // 2, :], attT[rows, c // 2 * CH:(c // 2 + 1) * CH], start=True, stop=c == 0)
                        if c:
                            pe.matmul(out, states[:, c - 1, :], q_dec[:, c * CH:(c + 1) * CH], start=False, stop=True)
                    pe.matmul(rb[3][:, 0:P], vals[:, NT - 1, :], attTs[:, :], start=True, stop=False)
                    hold(pe, s_in, (r + 1) * 16, tk)
                    for b in range(DEC_B):
                        i = pe.matmul(rb[3][:, b * DEC_T:(b + 1) * DEC_T], s_old[:, b, :],
                                      q_dec[:, T_PROMPT + b * DEC_T:T_PROMPT + (b + 1) * DEC_T], start=False, stop=b == DEC_B - 1)
                    i.then_inc(o_done, 1)
                if has(h, 0, 8):
                    hold(pe, W.lo_done, slab_no(h, 1) + 1, tk)
                    for g in range(G):
                        hold(pe, act_evac, h * 12 + g + 1, tk)
                        W.block(pe, lin[g][:, 0:GT], pars(par0, h, 1), h_hi, h_lo, g).then_inc(W.units, 1)
                if has(h, 1, 9):
                    hold(pe, n_act, r * 3 + 1, tk)
                    hold(pe, chained, r * 2 + 2, tk)
                    pe.matmul(rb[0][:, :], const["ones_v"][:, :], o_work[:, 0:512], start=True, stop=True)
                    pe.matmul(rb[4][:, :], const["ones_v"][:, :], o_work[:, 512:1024], start=True, stop=True)
                    pe.matmul(rb[3][:, P:2 * P], const["ones_v"][:, :], o_work[:, 1024:T], start=True, stop=True).then_inc(ss_done, 1)
                if has(h, 0, 8):
                    for g in range(G):
                        hold(pe, v_rows_set, h * 3 + g + 1, tk)
                        for tile in range(3):
                            i = pe.transpose(lin[g][:, tile * P:(tile + 1) * P], k_endT[:, 3 * g + tile, :], ident[:, :])
                        i.then_inc(v_turned, 1)
                for k in (2, 3):
                    if has(h, 0, 8):
                        hold(pe, W.lo_done, slab_no(h, k) + 1, tk)
                        for g in range(G):
                            hold(pe, act_evac, h * 12 + 3 * (k - 1) + g + 1, tk)
                            W.block(pe, lin[g][:, 0:GT], pars(par0, h, k), h_hi, h_lo, g).then_inc(W.units, 1)

            over_bodies(pe, body)


def in_slabs(w):
    k, n = w.shape
    return w.reshape(KB, P, n // P, P).transpose(2, 1, 0, 3).reshape(n // P, P, SLAB)


def down_slabs(w):
    return w.reshape(-1, P, SLAB)


def ffn_phase(nc, env, x, layer):
    io, const, sem, tick = env["io"], env["const"], env["sem"], env["tick"]
    tag = f"ff{layer}"
    sp_ = Space(nc, env["free"], env["end"])

    def take(name, shape, dtype=F32, at=None):
        return sp_.take(tag + name, shape, dtype, None if at is None else t_at[tag + at])

    RING = 3
    h_hi, h_lo = take("h_hi", [P, KB, T], F32R), take("h_lo", [P, KB, T], F32R)
    raw = take("raw", [P, 2, SLAB])
    w_hi, w_lo = take("w_hi", [P, RING, SLAB], F32R), take("w_lo", [P, RING, SLAB], F32R)
    W_EXT = CONV_W - 1
    SEQ_EXT = DEC_T + W_EXT
    ext_cols = W_EXT + T_PROMPT + DEC_B * SEQ_EXT
    a_ext = take("a_ext", [P, 2, ext_cols])
    conv = take("conv", [P, 2, T])
    y = take("y", [P, T])
    y_hi, y_lo = take("y_hi", [P, 4, T], F32R), take("y_lo", [P, 4, T], F32R)
    state = take("state", [P, FB, DEC_B, W_EXT])
    ends = take("ends", [P, FB, (1 + DEC_B) * W_EXT])
    conv_p = take("conv_p", [P, FB, CONV_W + 1])
    gain = take("gain", [P, KB])
    sq = take("sq", [P, Norm.R, GT], at="a_ext")
    std = take("std", [P, G, GT], at="conv")
    nt = take("nt", [P, Norm.R, GT], at="y")
    CHUNKS = FB // 2
    SLABS = 2 * FB + FB

    with ExitStack() as ctx:
        lin = [ctx.enter_context(nc.psum_tensor(f"{tag}lin{g}", [P, BANK], F32)) for g in range(2 * G)]
        W = Slabs(nc, sem, tag, io["weights"], env["ffn_first"][layer], SLABS, RING, raw, w_hi, w_lo, tick)
        N = Norm(env, x, gain, const["ones"], h_hi, h_lo, sq, std, nt, lin)
        consts_in = sem(tag + "_consts_in")
        a_out = sem(tag + "_a_out")
        state_set = sem(tag + "_state_set")
        conv_done = sem(tag + "_conv_done")
        silu_done = sem(tag + "_silu_done")
        u_out = sem(tag + "_u_out")
        y_split = sem(tag + "_y_split")
        y_done = sem(tag + "_y_done")
        down_out = sem(tag + "_down_out")
        ends_taken = sem(tag + "_ends_taken")
        out_done = sem(tag + "_out_done")
        block = ctx.enter_context(nc.Block())

        def units_before(c):
            return 0 if isinstance(c, int) and c == 0 else c * 36 - 24

        def slab_base(c):
            return 0 if isinstance(c, int) and c == 0 else c * 6 - 2

        def over_chunks(eng, body):
            for c in range(3):
                body(c, c % 2)
            with eng.Fori(1, (CHUNKS - 1) // 2) as m:
                body(m * 2 + 1, 1)
                body(m * 2 + 2, 0)
            body(CHUNKS, CHUNKS % 2)

        def slot(c, k):
            return (k if isinstance(c, int) and c == 0 else k + 1) % RING

        def half(c, k):
            return k // 2 if isinstance(c, int) and c == 0 else c * 3 + (k // 2 - 1)

        def used_for(c, k):
            first = units_before(c)
            if isinstance(c, int) and c == 0:
                return max(0, 3 * (k - 2))
            if isinstance(c, int) and c == 1 and k < 3:
                return 3 * (k + 2)
            if k < 3:
                return first - 24 if k == 0 else first
            return first + 3 * (k - 2)

        @block.sync
        def _(sp):
            sp.dma_start(state[:, :, :, :], io["state_conv"][layer]).then_inc(consts_in, 16)
            sp.dma_start(conv_p[:, :, :], io["conv_p"][layer]).then_inc(consts_in, 16)
            sp.dma_start(gain[:, :], io["gains"][env["ffn_gain"][layer]]).then_inc(consts_in, 16)
            W.load_all(sp)
            sp.wait_ge(ends_taken, FB)
            sp.dma_start(io["conv_out"][layer], ends[:, :, :]).then_inc(out_done, 16)
            sp.wait_ge(out_done, 16)

        @block.gpsimd
        def _(pool):
            tk = tick["pool"]
            N.on_pool(pool)
            pool.wait_ge(consts_in, 48)
            pool.wait_ge(N.squared, N.blocks + G * KB)
            pool.wait_ge(N.summed, N.blocks + G * KB)
            for i in range(2):
                pool.memset(a_ext[:, i, 0:W_EXT], 0.0)

            def put_state(b, i):
                if not isinstance(b, int) or b >= 2:
                    hold(pool, conv_done, b - 1, tk)
                pool.tensor_copy(a_ext[:, i, W_EXT + T_PROMPT:].rearrange("p (b t) -> p b t", t=SEQ_EXT)[:, :, 0:W_EXT],
                                 state[:, b]).then_inc(state_set, 1)

            def take_ends(b, i):
                hold(pool, a_out, b * 3 + 3, tk)
                pool.tensor_copy(ends[:, b, 0:W_EXT], a_ext[:, i, T_PROMPT:T_PROMPT + W_EXT])
                pool.tensor_copy(ends[:, b, W_EXT:].rearrange("p (b t) -> p b t", t=W_EXT),
                                 a_ext[:, i, W_EXT + T_PROMPT:].rearrange("p (b t) -> p b t", t=SEQ_EXT)[:, :, DEC_T:SEQ_EXT])\
                    .then_inc(ends_taken, 1)

            put_state(0, 0)
            put_state(1, 1)
            with pool.Fori(0, CHUNKS - 1) as m:
                for i in range(2):
                    take_ends(m * 2 + i, i)
                    put_state(m * 2 + (i + 2), i)
            for i in range(2):
                take_ends(FB - 2 + i, i)

        @block.scalar
        def _(act):
            tk = tick["act"]
            N.on_scalar(act, lambda: W.split_hi(act, 0, 0, 0, 0, 0))

            def hi(c, k):
                W.split_hi(act, slab_base(c) + k, half(c, k), slot(c, k), k % 2, used_for(c, k))

            def gate_rows(c, j):
                blk = c * 2 + j
                hold(act, ends_taken, blk - 1, tk)
                hold(act, conv_done, blk - 1, tk)
                hold(act, state_set, blk + 1, tk)
                for g in range(G):
                    hold(act, W.units, units_before(c) + 6 * j + g + 1, tk)
                    a, b = g * GT, min((g + 1) * GT, T_PROMPT)
                    last = act.activation(a_ext[:, j, W_EXT + a:W_EXT + b], lin[g][:, 0:b - a], ACT.Copy)
                    if g == G - 1:
                        last = act.activation(
                            a_ext[:, j, W_EXT + T_PROMPT:].rearrange("p (b t) -> p b t", t=SEQ_EXT)[:, :, W_EXT:],
                            lin[g][:, b - a:GT].rearrange("p (b t) -> p b t", t=DEC_T), ACT.Copy)
                    last.then_inc(a_out, 1)

            def silu(c, j):
                hold(act, conv_done, c * 2 + j + 1, tk)
                act.activation(conv[:, j], conv[:, j], ACT.Silu).then_inc(silu_done, 1)

            def y_high(c, par, j):
                hold(act, u_out, (c * 2 + j) * 3 + 3, tk)
                act.activation(y_hi[:, 2 * par + j], y[:, :], ACT.Copy).then_inc(y_split, 1)

            def body(c, par):
                if isinstance(c, int) and c == CHUNKS:
                    hi(c, 1)
                    return
                hi(c, 1)
                gate_rows(c, 0)
                hi(c, 2)
                silu(c, 0)
                hi(c, 3)
                y_high(c, par, 0)
                gate_rows(c, 1)
                if not (isinstance(c, int) and c == 0):
                    hi(c, 4)
                    hi(c, 5)
                silu(c, 1)
                y_high(c, par, 1)
                hi(c + 1, 0)

            over_chunks(act, body)

        @block.vector
        def _(dve):
            tk = tick["dve"]
            dve.wait_ge(consts_in, 48)
            N.on_vector(dve, lambda: W.split_lo(dve, 0, 0, 0))

            def lo(c, k):
                W.split_lo(dve, slab_base(c) + k, slot(c, k), k % 2)

            def seqs(ap, t):
                return ap.rearrange("p (b t) -> p b t", t=t)

            def convolve(c, j):
                blk = c * 2 + j
                hold(dve, a_out, blk * 3 + 3, tk)
                if not (isinstance(c, int) and c == 0):
                    hold(dve, u_out, (blk - 1) * 3, tk)
                rows = a_ext[:, j, W_EXT + T_PROMPT:]
                for tap in range(CONV_W):
                    w = conv_p[:, blk, tap:tap + 1]
                    src_p, src_s = a_ext[:, j, tap:tap + T_PROMPT], seqs(rows, SEQ_EXT)[:, :, tap:tap + DEC_T]
                    dst_p, dst_s = conv[:, j, 0:T_PROMPT], seqs(conv[:, j, T_PROMPT:], DEC_T)
                    if tap == 0:
                        b = conv_p[:, blk, CONV_W:CONV_W + 1]
                        dve.tensor_scalar(dst_p, src_p, w, b, ALU.mult, ALU.add)
                        last = dve.tensor_scalar(dst_s, src_s, w, b, ALU.mult, ALU.add)
                    else:
                        dve.drain()
                        dve.scalar_tensor_tensor(dst_p, src_p, w, dst_p, ALU.mult, ALU.add)
                        last = dve.scalar_tensor_tensor(dst_s, src_s, w, dst_s, ALU.mult, ALU.add)
                last.then_inc(conv_done, 1)

            def up_rows(c, j):
                blk = c * 2 + j
                hold(dve, silu_done, blk + 1, tk)
                hold(dve, y_split, blk, tk)
                hold(dve, y_done, blk, tk)
                for g in range(G):
                    hold(dve, W.units, units_before(c) + 6 * j + 3 + g + 1, tk)
                    dve.tensor_tensor(y[:, g * GT:(g + 1) * GT], lin[G + g][:, 0:GT], conv[:, j, g * GT:(g + 1) * GT],
                                      ALU.mult).then_inc(u_out, 1)

            def y_low(c, par, j):
                hold(dve, y_split, c * 2 + j + 1, tk)
                dve.tensor_tensor(y_lo[:, 2 * par + j], y[:, :], y_hi[:, 2 * par + j].bitcast(F32), ALU.subtract).then_inc(y_done, 1)

            def body(c, par):
                end = isinstance(c, int) and c == CHUNKS
                lo(c, 1)
                if not end:
                    convolve(c, 0)
                    lo(c, 2)
                    up_rows(c, 0)
                    lo(c, 3)
                    y_low(c, par, 0)
                    convolve(c, 1)
                    if not (isinstance(c, int) and c == 0):
                        lo(c, 4)
                        lo(c, 5)
                    up_rows(c, 1)
                    y_low(c, par, 1)
                    lo(c + 1, 0)
                if not (isinstance(c, int) and c == 0):
                    first = units_before(c) + (0 if end else 12)
                    dve.drain()
                    for n in range(KB * G):
                        nb, g = divmod(n, G)
                        hold(dve, W.units, first + n + 1, tk)
                        xs = x[:, nb, g * GT:(g + 1) * GT]
                        dve.tensor_tensor(xs, xs, lin[n % 6][:, 0:GT], ALU.add).then_inc(down_out, 1)

            over_chunks(dve, body)
            dve.drain()

        @block.tensor
        def _(pe):
            tk = tick["pe"]
            N.on_tensor(pe, 0)
            N.on_tensor(pe, 1)

            def body(c, par):
                start, end = (isinstance(c, int) and c == v for v in (0, CHUNKS))
                if not end:
                    for k in range(4):
                        j, up = divmod(k, 2)
                        hold(pe, W.lo_done, slab_base(c) + k + 1, tk)
                        for g in range(G):
                            if k == 0 and start:
                                N.wait_group(pe, g)
                            elif k >= 2 or (isinstance(c, int) and c == 1):
                                hold(pe, u_out if up else a_out, (c * 2 + j - 1) * 3 + g + 1, tk)
                            elif not start:
                                hold(pe, down_out, (c - 2) * 24 + 19 + 3 * up + g, tk)
                            W.block(pe, lin[3 * up + g][:, 0:GT], slot(c, k), h_hi, h_lo, g).then_inc(W.units, 1)
                            if k == 0 and start and g == 0:
                                N.on_tensor(pe, 2)
                if not start:
                    k0 = 0 if end else 4
                    hold(pe, W.lo_done, slab_base(c) + k0 + 2, tk)
                    hold(pe, y_done, c * 2, tk)
                    for n in range(KB * G):
                        nb, g = divmod(n, G)
                        if n < 6 and not end:
                            hold(pe, u_out if n >= 3 else a_out, c * 6 + 3 + n % 3 + 1, tk)
                        else:
                            hold(pe, down_out, (c - 1) * 24 + n - 5, tk)
                        for j in range(2):
                            src = 2 * (1 - par) + j
                            i = W.product(pe, lin[n % 6][:, 0:GT], slot(c, k0 + j), nb * P, y_hi[:, src, g * GT:(g + 1) * GT],
                                          y_lo[:, src, g * GT:(g + 1) * GT], j == 0, j == 1)
                        i.then_inc(W.units, 1)

            over_chunks(pe, body)


HEAD_D = 64
N_HEADS = 16
N_KV = 4
GROUP = N_HEADS // N_KV
QB = N_HEADS // 2
IDX_H = 8
IDX_B = IDX_H // 2
ROT = HEAD_D // 4
TOPK = 256
CHUNK = 64
THETA = 500000.0
S_KEYS = PAST + DEC_T
A_KEYS = PAST + T_SAMPLE
TAKEN = -3e38
BARRED = -1e38
DSA_PROJ = IDX_B + 1 + 1 + 2 + 2 + QB
KI_SLAB, WI_SLAB, K_SLAB, V_SLAB, Q_SLAB = IDX_B, IDX_B + 1, IDX_B + 2, IDX_B + 4, IDX_B + 6


def head_order():
    heads = [(2 * p + half) * GROUP + g for p in range(2) for g in range(GROUP) for half in range(2)]
    return np.concatenate([np.arange(h * HEAD_D, (h + 1) * HEAD_D) for h in heads])


def dsa_slabs(i):
    w = i["ds_w_in"][0]
    o1 = N_HEADS * HEAD_D
    o2 = o1 + N_KV * HEAD_D
    o3 = o2 + N_KV * HEAD_D
    o4 = o3 + IDX_H * HEAD_D
    o5 = o4 + HEAD_D
    wi = np.concatenate([w[:, o5:], np.zeros((D, P - IDX_H), w.dtype)], axis=1)
    cols = [w[:, o3:o4], w[:, o4:o5], w[:, o4:o5], wi, w[:, o1:o2], w[:, o2:o3], w[:, :o1][:, head_order()]]
    out = in_slabs(i["ds_w_out"][0][head_order()])
    return np.concatenate([in_slabs(np.concatenate(cols, axis=1)), out])


def dsa_layout(i):
    ck = i["cache_k"][0].reshape(DEC_B, PAST, 2, P).transpose(0, 2, 3, 1)
    cv = i["cache_v"][0].reshape(DEC_B, PAST // P, P, N_KV * HEAD_D).transpose(0, 2, 1, 3)
    ci = i["cache_kidx"][0].transpose(0, 2, 1)
    ln = np.stack([i["ds_kln_w"][0], i["ds_kln_b"][0]], axis=1)
    return {"cache_k": ck, "cache_v": cv, "cache_ki": np.concatenate([ci, ci], axis=1), "ki_ln": np.concatenate([ln, ln])}


def dsa_constants():
    pos = np.concatenate([np.arange(T_PROMPT), np.tile(PAST + np.arange(DEC_T), DEC_B)]).astype(np.float32)
    half = ROT // 2
    freq = np.power(np.float32(THETA), -np.arange(half, dtype=np.float32) / np.float32(half)).astype(np.float32)
    ang = pos[None, :] * freq[:, None]
    cos, sin = np.ones((HEAD_D, T), np.float32), np.zeros((HEAD_D, T), np.float32)
    cos[:half] = cos[half:ROT] = np.cos(ang)
    sin[:half], sin[half:ROT] = -np.sin(ang), np.sin(ang)
    rows = np.arange(P)
    t_row = rows % DEC_T
    same_t = (t_row[:, None] == np.arange(DEC_T)[None, :]).astype(np.float32)
    b_row = rows // DEC_T
    spread_b = ((b_row[:, None, None] == np.arange(DEC_B)[None, :, None]) & (t_row[:, None, None] == t_row[None, None, :]))
    other = np.where(b_row[:, None] == np.arange(DEC_B)[None, :], 0.0, NEG)
    bf = mybir.dt.np(BF16)
    return {"cos": np.concatenate([cos, cos]), "sin": np.concatenate([sin, sin]), "same_t": same_t,
            "spread_b": spread_b.astype(bf), "other": other.astype(np.float32)}


def dsa_space(nc, env):
    sp_ = Space(nc, env["free"], env["end"])
    env["k"] = sp_.take("at_k", [P, 2, T])
    env["v"] = sp_.take("at_v", [P, NT, N_KV * HEAD_D])
    env["ki"] = sp_.take("at_ki", [P, T])
    env["wi"] = sp_.take("at_wi", [P, NT, IDX_H])
    env["at_free"] = sp_.at


def project_phase(nc, env, x):
    dsa_space(nc, env)
    io, const, sem, tick = env["io"], env["const"], env["sem"], env["tick"]
    k_sb, v_sb, ki, wi = env["k"], env["v"], env["ki"], env["wi"]
    take = Space(nc, env["at_free"], env["end"]).take
    h_hi, h_lo = take("pj_h_hi", [P, KB, T], F32R), take("pj_h_lo", [P, KB, T], F32R)
    raw = take("pj_raw", [P, 2, SLAB])
    w_hi, w_lo = take("pj_w_hi", [P, 2, SLAB], F32R), take("pj_w_lo", [P, 2, SLAB], F32R)
    rows = take("pj_rows", [P, 2, T])
    swapped = take("pj_swapped", [P, T])
    roped = take("pj_roped", [P, 2, T])
    cos, sin = take("pj_cos", [P, T]), take("pj_sin", [P, T])
    ln = take("pj_ln", [P, 2])
    gain = take("pj_gain", [P, KB])
    sq = take("pj_sq", [P, Norm.R, GT], at=t_at["pj_roped"])
    std = take("pj_std", [P, G, GT], at=t_at["pj_swapped"])
    nt = take("pj_nt", [P, Norm.R, GT], at=t_at["pj_roped"] + 4 * T)
    WI_SCALE = float(np.float32((IDX_H * HEAD_D) ** -0.5))
    SWAP = list(range(ROT // 2, ROT)) + list(range(ROT // 2)) + list(range(ROT, 32))

    with ExitStack() as ctx:
        lin = [ctx.enter_context(nc.psum_tensor(f"pj_lin{g}", [P, BANK], F32)) for g in range(G)]
        lnb = [ctx.enter_context(nc.psum_tensor(f"pj_ln{g}", [P, BANK], F32)) for g in range(G)]
        W = Slabs(nc, sem, "pj", io["weights"], HG_SLABS + FFN_SLABS, DSA_PROJ, 2, raw, w_hi, w_lo, tick)
        N = Norm(env, x, gain, const["ones"], h_hi, h_lo, sq, std, nt, lin)
        consts_in = sem("pj_consts_in")
        evac = sem("pj_evac")
        rope_done = sem("pj_rope_done")
        ln_pe, ln_dve, ln_act = sem("pj_ln_pe"), sem("pj_ln_dve"), sem("pj_ln_act")
        q_out = [sem(f"pj_q_out{k}") for k in range(2)]
        kv_out = sem("pj_kv_out")
        tok_set, tok_turned = sem("pj_tok_set"), sem("pj_tok_turned")
        block = ctx.enter_context(nc.Block())
        FIRST_Q = IDX_B + 3

        @block.sync
        def _(sp):
            for dst, src in ((cos[:, :], io["cos"]), (sin[:, :], io["sin"]), (ln[:, :], io["ki_ln"]), (gain[:, :], io["gains"][2])):
                sp.dma_start(dst, src).then_inc(consts_in, 16)
            W.load_all(sp)

        @block.gpsimd
        def _(pool):
            tk = tick["pool"]
            N.on_pool(pool)
            for n in range(IDX_B):
                pool.wait_ge(rope_done, n + 1)
                pool.dma_start(io["qi_t"][n], roped[:, n % 2, :]).then_inc(q_out[n % 2], 16)
            pool.wait_ge(rope_done, IDX_B + 1)
            pool.dma_start(io["ki_out"], ki[0:HEAD_D, :]).then_inc(kv_out, 16)
            pool.wait_ge(rope_done, IDX_B + 3)
            pool.dma_start(io["k_out"], k_sb[:, :, :]).then_inc(kv_out, 16)
            pool.wait_ge(evac, 3 * (V_SLAB + 2))
            pool.dma_start(io["v_out"], v_sb[:, :, :]).then_inc(kv_out, 16)
            with pool.Fori(0, QB // 2) as m:
                for par in range(2):
                    hold(pool, rope_done, m * 2 + (FIRST_Q + par + 1), tk)
                    pool.dma_start(io["q_t"][m * 2 + par], roped[:, par, :]).then_inc(q_out[par], 16)
            pool.wait_ge(kv_out, 48)
            for par in range(2):
                pool.wait_ge(q_out[par], 16 * (IDX_B + QB) // 2)

        @block.scalar
        def _(act):
            tk = tick["act"]
            N.on_scalar(act, lambda: W.split_hi(act, 0, 0, 0, 0, 0))

            def hi(s, par, half):
                W.split_hi(act, s, half, par, par, (s - 1) * 3)

            def copy_rows(s, n, buf, scale=1.0):
                hold(act, rope_done, n - 1, tk)
                for g in range(G):
                    hold(act, W.units, s * 3 + g + 1, tk)
                    act.activation(rows[:, buf, g * GT:(g + 1) * GT], lin[g][:, 0:GT], ACT.Copy, scale=scale).then_inc(evac, 1)

            def token_rows(s, buf, roped_before):
                act.wait_ge(rope_done, roped_before)
                for g in range(G):
                    act.wait_ge(W.units, 3 * s + g + 1)
                    act.activation(rows[:, buf, g * GT:(g + 1) * GT], lin[g][:, 0:GT], ACT.Copy).then_inc(tok_set, 1)

            for s in range(Q_SLAB):
                hi(s + 1, (s + 1) % 2, (s + 1) // 2)
                if s <= KI_SLAB:
                    copy_rows(s, s, s % 2)
                elif s == WI_SLAB:
                    token_rows(s, 1, IDX_B)
                    for g in range(G):
                        act.wait_ge(tok_turned, g + 1)
                        act.activation(wi[:, 3 * g:3 * g + 3, :], lin[g][:, 0:GT].rearrange("p (t c) -> p t c", c=P)[:, :, 0:IDX_H],
                                       ACT.Copy, scale=WI_SCALE).then_inc(evac, 1)
                    act.wait_ge(ln_dve, 1)
                    act.activation(swapped[:, :], rows[:, 0, :], ACT.Square).then_inc(ln_act, 1)
                    act.wait_ge(ln_pe, 2)
                    for g in range(G):
                        i = act.activation(swapped[:, g * GT:(g + 1) * GT], lnb[g][:, 0:GT], ACT.Sqrt, bias=EPS)
                    i.then_inc(ln_act, 1)
                elif s < V_SLAB:
                    copy_rows(s, s - 1, (s - 1) % 2)
                else:
                    n = s - V_SLAB
                    token_rows(s, 1 - n, IDX_B + 2 + n)
                    for g in range(G):
                        act.wait_ge(tok_turned, 3 * (n + 1) + g + 1)
                        act.activation(v_sb[:, 3 * g:3 * g + 3, (s - V_SLAB) * P:(s - V_SLAB + 1) * P],
                                       lin[g][:, 0:GT].rearrange("p (t c) -> p t c", c=P), ACT.Copy).then_inc(evac, 1)
            with act.Fori(0, QB // 2 - 1) as m:
                for par in range(2):
                    hi(m * 2 + (Q_SLAB + par + 1), 1 - par, m + (Q_SLAB + par + 1) // 2)
                    copy_rows(m * 2 + (Q_SLAB + par), m * 2 + (FIRST_Q + par), 1 - par, HEAD_D ** -0.5)
            last = Q_SLAB + QB - 2
            hi(last + 1, 1, (last + 1) // 2)
            copy_rows(last, FIRST_Q + QB - 2, 1, HEAD_D ** -0.5)
            copy_rows(last + 1, FIRST_Q + QB - 1, 0, HEAD_D ** -0.5)

        @block.vector
        def _(dve):
            tk = tick["dve"]
            dve.wait_ge(consts_in, 64)
            N.on_vector(dve, lambda: W.split_lo(dve, 0, 0, 0))

            def lo(s, par):
                W.split_lo(dve, s, par, par)

            def rope(src, dst):
                dve.drain()
                dve.stream_shuffle(swapped[:, :], src, SWAP)
                dve.tensor_tensor(dst, src, cos[:, :], ALU.mult)
                dve.drain()
                dve.tensor_tensor(swapped[:, :], swapped[:, :], sin[:, :], ALU.mult)
                dve.drain()
                dve.tensor_tensor(dst, dst, swapped[:, :], ALU.add).then_inc(rope_done, 1)

            def rope_rows(s, n, buf, dst, out_par=None, outs=0):
                hold(dve, evac, s * 3 + 3, tk)
                if out_par is not None:
                    hold(dve, q_out[out_par], outs, tk)
                rope(rows[:, buf, :], dst)

            for s in range(Q_SLAB):
                lo(s + 1, (s + 1) % 2)
                if s < KI_SLAB:
                    rope_rows(s, s, s % 2, roped[:, s % 2, :], s % 2, 16 * (s // 2))
                elif s == KI_SLAB:
                    dve.wait_ge(ln_pe, 1)
                    dve.drain()
                    for g in range(G):
                        cols = slice(g * GT, (g + 1) * GT)
                        i = dve.tensor_tensor(rows[:, 0, cols], rows[:, 0, cols], lnb[g][:, 0:GT], ALU.subtract)
                    i.then_inc(ln_dve, 1)
                elif s == WI_SLAB:
                    dve.wait_ge(ln_act, 2)
                    dve.reciprocal(swapped[:, :], swapped[:, :])
                    dve.drain()
                    dve.tensor_tensor(rows[:, 0, :], rows[:, 0, :], swapped[:, :], ALU.mult)
                    dve.drain()
                    dve.tensor_scalar(rows[:, 0, :], rows[:, 0, :], ln[:, 0:1], ln[:, 1:2], ALU.mult, ALU.add)
                    rope(rows[:, 0, :], ki[:, :])
                elif s < V_SLAB:
                    rope_rows(s, s - 1, (s - 1) % 2, k_sb[:, s - K_SLAB, :])
            with dve.Fori(0, QB // 2 - 1) as m:
                for par in range(2):
                    lo(m * 2 + (Q_SLAB + par + 1), 1 - par)
                    rope_rows(m * 2 + (Q_SLAB + par), 0, 1 - par, roped[:, par, :], par, m * 16 + 16 * IDX_B // 2)
            last = Q_SLAB + QB - 2
            lo(last + 1, 1)
            for par in range(2):
                rope_rows(last + par, 0, 1 - par, roped[:, par, :], par, 16 * (IDX_B + QB - 2) // 2)
            dve.drain()

        @block.tensor
        def _(pe):
            tk = tick["pe"]
            N.on_tensor(pe, 0)
            N.on_tensor(pe, 1)

            def project(s, par):
                hold(pe, W.lo_done, s + 1, tk)
                for g in range(G):
                    if isinstance(s, int) and s == 0:
                        N.wait_group(pe, g)
                    hold(pe, evac, (s - 1) * 3 + g + 1, tk)
                    W.block(pe, lin[g][:, 0:GT], par, h_hi, h_lo, g).then_inc(W.units, 1)
                    if isinstance(s, int) and s == 0 and g == 0:
                        N.on_tensor(pe, 2)

            def turn(n, buf):
                for g in range(G):
                    pe.wait_ge(tok_set, 3 * n + g + 1)
                    for tile in range(3 * g, 3 * g + 3):
                        i = pe.transpose(lin[g][:, (tile - 3 * g) * P:(tile - 3 * g + 1) * P], rows[:, buf, tile * P:(tile + 1) * P],
                                         const["ident"][:, :])
                    i.then_inc(tok_turned, 1)

            def ln_mean(src):
                for g in range(G):
                    i = pe.matmul(lnb[g][:, 0:GT], const["ones_v"][:, :], src[:, g * GT:(g + 1) * GT], start=True, stop=True)
                i.then_inc(ln_pe, 1)

            for s in range(Q_SLAB):
                if s == WI_SLAB:
                    pe.wait_ge(evac, 3 * (KI_SLAB + 1))
                    ln_mean(rows[:, 0, :])
                    project(s, s % 2)
                    turn(0, 1)
                    pe.wait_ge(ln_act, 1)
                    ln_mean(swapped[:, :])
                elif s < V_SLAB:
                    project(s, s % 2)
                else:
                    project(s, s % 2)
                    turn(s - V_SLAB + 1, V_SLAB + 1 - s)
            with pe.Fori(0, QB // 2) as m:
                for par in range(2):
                    project(m * 2 + (Q_SLAB + par), par)


def mask_at(tile):
    return P * tile * (tile + 1) // 2


FIRST_TOP = TOPK // P
EARLY_TOP = range(FIRST_TOP, FIRST_TOP + 2)
LATE_TOP = range(FIRST_TOP + 2, PT)
STEPS = 2 * TOPK // 8


def score_at(tile):
    return mask_at(tile) - mask_at(FIRST_TOP)


def top_step(dve, top, scores, taking):
    for n, score in enumerate(scores):
        if taking:
            dve.match_replace(score, top[:, n, :], score, TAKEN)
        else:
            dve.max(top[:, n, :], score)
    dve.drain()


def mask_from(dve, mask, score):
    return dve.tensor_scalar(mask, score, TAKEN * 0.7, NEG, ALU.is_gt, ALU.mult)


def select_phase(nc, env, x):
    io, sem, tick = env["io"], env["sem"], env["tick"]
    ki, wi = env["ki"], env["wi"]
    sp_ = Space(nc, env["at_free"], env["end"])
    take = sp_.take
    mask_p, mask_s = take("mask_p", [P, mask_at(PT)], BF16), take("mask_s", [P, A_KEYS], BF16)
    env["mask_p"], env["mask_s"] = mask_p, mask_s
    env["o_t"] = take("o_t", [P, QB, T])
    env["o_end"] = sp_.at
    score_p, score_s = take("score_p", [P, score_at(PT)]), take("score_s", [P, S_KEYS])
    top, tail, other = take("se_top", [P, 2, 8]), take("se_tail", [P, DEC_T]), take("se_other", [P, DEC_B])
    env["score_p"], env["score_s"], env["top"], env["tail"], env["other"] = score_p, score_s, top, tail, other
    env["scores_end"] = sp_.at
    qi = take("se_qi", [P, IDX_B, T])
    qi_b = take("se_qi_b", [P, DEC_B, IDX_B, DEC_T])
    keys = take("se_keys", [P, 2, PAST])
    relu_s, relu_p = take("se_relu_s", [P, 3, BANK]), take("se_relu_p", [P, 2, T_PROMPT])
    same_t, own_b = take("se_same_t", [P, DEC_T]), take("se_own_b", [P, DEC_B])
    w_by_row = take("se_w_by_row", [P, P])
    w_col = take("se_w_col", [P, DEC_B])
    w_sel = take("se_w_sel", [P, DEC_B, P])
    tiles = list(range(FIRST_TOP, PT))
    chunks = pieces(PAST) + [(PAST, S_KEYS)]
    NCHK = len(chunks)
    units = [(b, c) for b in range(DEC_B) for c in range(NCHK)]

    with ExitStack() as ctx:
        bank = [ctx.enter_context(nc.psum_tensor(f"se_bank{n}", [P, BANK], F32)) for n in range(8)]
        acc, dots = bank[0:NCHK], bank[NCHK:8]
        pair = ((bank[5], bank[6]), (bank[7], bank[0]))
        consts_in, qi_in = sem("se_consts_in"), sem("se_qi_in")
        keys_in = [sem(f"se_keys_in{n}") for n in range(2)]
        qi_sorted, w_rows_set, w_turned, w_sel_set = (sem("se_" + n) for n in ("qi_sorted", "w_rows_set", "w_turned", "w_sel_set"))
        dots_done, relu_done, summed = sem("se_dots_done"), sem("se_relu_done"), sem("se_summed")
        scores_out = sem("se_scores_out")
        p_dots, p_relu, p_added = sem("se_p_dots"), sem("se_p_relu"), sem("se_p_added")
        block = ctx.enter_context(nc.Block())

        @block.sync
        def _(sp):
            for dst, src in ((same_t[:, :], io["same_t"]), (own_b[:, :], io["own_b"]), (other[:, :], io["other"])):
                sp.dma_start(dst, src).then_inc(consts_in, 16)
            sp.dma_start(qi[:, :, :], io["qi_t"].rearrange("b p t -> p b t")).then_inc(qi_in, 16)
            for b in range(DEC_B):
                if b >= 2:
                    sp.wait_ge(dots_done, NCHK * (b - 1))
                sp.dma_start(keys[:, b % 2, :], io["cache_ki"][b]).then_inc(keys_in[b % 2], 16)

        @block.tensor
        def _(pe):
            pe.wait_ge(w_rows_set, 1)
            pe.wait_ge(consts_in, 48)
            pe.matmul(dots[0][:, 0:DEC_B], w_by_row[:, :], own_b[:, :], start=True, stop=True).then_inc(w_turned, 1)
            pe.wait_ge(w_sel_set, 1)
            pe.wait_ge(qi_sorted, 1)

            n = 0
            for t in tiles:
                for h in range(IDX_H):
                    rows = slice(h % 2 * HEAD_D, (h % 2 + 1) * HEAD_D)
                    if n >= 2:
                        pe.wait_ge(p_relu, n - 1)
                    for k, (a, e) in enumerate(pieces((t + 1) * P)):
                        i = pe.matmul(pair[h % 2][k][:, 0:e - a], qi[rows, h // 2, t * P:(t + 1) * P], ki[rows, a:e], start=True, stop=True)
                    i.then_inc(p_dots, 1)
                    n += 1

            pe.wait_ge(p_relu, n)

            def head_sum(u):
                b, c = units[u]
                n = chunks[c][1] - chunks[c][0]
                pe.wait_ge(relu_done, u + 1)
                pe.matmul(acc[c][:, 0:n], w_sel[:, b, :], relu_s[:, u % 3, 0:n], start=b == 0, stop=b == DEC_B - 1)\
                    .then_inc(summed, 1)

            for u, (b, c) in enumerate(units):
                a, e = chunks[c]
                if c == 0:
                    pe.wait_ge(keys_in[b % 2], 16 * (b // 2 + 1))
                if u >= 3:
                    pe.wait_ge(relu_done, u - 2)
                for half in range(2):
                    rows = slice(half * HEAD_D, (half + 1) * HEAD_D)
                    rhs = keys[rows, b % 2, a:e] if c < NCHK - 1 else ki[rows, T_PROMPT + b * DEC_T:T_PROMPT + (b + 1) * DEC_T]
                    i = pe.matmul(dots[u % 3][rows, 0:e - a], qi_b[rows, b].rearrange("p h t -> p (h t)"), rhs, start=True, stop=True)
                i.then_inc(dots_done, 1)
                if u >= 2:
                    head_sum(u - 2)
            head_sum(len(units) - 2)
            head_sum(len(units) - 1)

        @block.scalar
        def _(act):
            n = 0
            for t in tiles:
                for h in range(IDX_H):
                    act.wait_ge(p_dots, n + 1)
                    if n >= 2:
                        act.wait_ge(p_added, n - 1)
                    for k, (a, e) in enumerate(pieces((t + 1) * P)):
                        i = act.activation(relu_p[:, n % 2, a:e], pair[h % 2][k][:, 0:e - a], ACT.Relu)
                    i.then_inc(p_relu, 1)
                    n += 1
            for u, (b, c) in enumerate(units):
                n = chunks[c][1] - chunks[c][0]
                act.wait_ge(dots_done, u + 1)
                if u >= 3:
                    act.wait_ge(summed, u - 2)
                act.activation(relu_s[:, u % 3, 0:n], dots[u % 3][:, 0:n], ACT.Relu).then_inc(relu_done, 1)
            act.wait_ge(summed, len(units))
            for c, (a, e) in enumerate(chunks):
                i = act.activation(score_s[:, a:e], acc[c][:, 0:e - a], ACT.Copy)
            i.then_inc(scores_out, 1)

        @block.vector
        def _(dve):
            dve.wait_ge(consts_in, 48)
            for half in range(2):
                dst = w_by_row[:, half * HEAD_D:(half + 1) * HEAD_D].rearrange("p (h t) -> p h t", t=DEC_T)
                src = wi[:, NT - 1, :].rearrange("p (h two) -> p two h", two=2)[:, half]
                i = dve.tensor_tensor(dst, spread(src.unsqueeze(2), dst.shape), spread(same_t[:, :].unsqueeze(1), dst.shape), ALU.mult)
            i.then_inc(w_rows_set, 1)
            dve.memset(w_sel[:, :, :], 0.0)
            dve.wait_ge(qi_in, 16)
            dve.tensor_copy(qi_b[:, :, :, :], qi[:, :, T_PROMPT:T].rearrange("p h (b t) -> p b h t", t=DEC_T)).then_inc(qi_sorted, 1)
            dve.wait_ge(w_turned, 1)
            dve.tensor_copy(w_col[:, :], dots[0][:, 0:DEC_B])
            dve.drain()
            for b in range(DEC_B):
                i = dve.tensor_scalar(w_sel[:, b, b * DEC_T:(b + 1) * DEC_T], same_t[:, :], w_col[:, b:b + 1], None, ALU.mult)
            i.then_inc(w_sel_set, 1)

            dve.memset(mask_p[:, 0:mask_at(FIRST_TOP)], 0.0)
            dve.drain()
            for t in range(FIRST_TOP):
                dve.memset(mask_p[0:CHUNK, mask_at(t + 1) - CHUNK:mask_at(t + 1)], NEG)
            n = 0
            for t in tiles:
                keys_n = (t + 1) * P
                score = score_p[:, score_at(t):score_at(t + 1)]
                for h in range(IDX_H):
                    w = wi[:, t, h:h + 1]
                    dve.wait_ge(p_relu, n + 1)
                    dve.drain()
                    if h == 0:
                        dve.tensor_scalar(score, relu_p[:, n % 2, 0:keys_n], w, None, ALU.mult).then_inc(p_added, 1)
                    else:
                        dve.scalar_tensor_tensor(score, relu_p[:, n % 2, 0:keys_n], w, score, ALU.mult, ALU.add).then_inc(p_added, 1)
                    n += 1
                dve.drain()
                dve.memset(score_p[0:CHUNK, score_at(t + 1) - CHUNK:score_at(t + 1)], BARRED)
            dve.drain()
            scores = [score_p[:, score_at(t):score_at(t + 1)] for t in EARLY_TOP]
            with dve.Fori(0, 4) as _:
                for step in range(STEPS // 4):
                    top_step(dve, top, scores, step % 2)
            for t, score in zip(EARLY_TOP, scores):
                mask_from(dve, mask_p[:, mask_at(t):mask_at(t + 1)], score)
            dve.drain()


def attend_prompt_phase(nc, env, x):
    io, const, sem, tick = env["io"], env["const"], env["sem"], env["tick"]
    k_sb, v_sb, mask_p = env["k"], env["v"], env["mask_p"]
    mask_s, o_t, top, tail, other = env["mask_s"], env["o_t"], env["top"], env["tail"], env["other"]
    score_p, score_s = env["score_p"], env["score_s"]
    take = Space(nc, env["scores_end"], env["end"]).take
    probs, probs_t = take("ap_probs", [P, 2, T_PROMPT]), take("ap_probs_t", [P, 2, T_PROMPT])
    q, q_hi, q_lo = take("ap_q", [P, 2, QB, P]), take("ap_q_hi", [P, 2, QB, P], F32R), take("ap_q_lo", [P, 2, QB, P], F32R)
    k_hi, k_lo = take("ap_k_hi", [P, 2, T_PROMPT], F32R), take("ap_k_lo", [P, 2, T_PROMPT], F32R)
    part_max, neg_max = take("ap_part_max", [P, 2, 2]), take("ap_neg_max", [P, 2, 1])
    total, inv = take("ap_total", [P, 2, 1]), take("ap_inv", [P, 2, 2, 1])
    o = take("ap_o", [P, P])
    blocks = [(t, j) for t in range(PT) for j in range(QB)]
    tops = [tuple(LATE_TOP[n:n + 2]) for n in range(0, len(LATE_TOP), 2)] + [None]
    top_keys = [sum((t + 1) * P for t in ts) if ts else S_KEYS for ts in tops]
    weight = [t + 3 for t, _ in blocks]
    row_of = [k for k in range(len(tops)) for _ in range(STEPS)]
    cost = np.cumsum([top_keys[k] for k in row_of])
    share = np.cumsum(np.repeat(weight, 2)) / (2 * sum(weight))
    steps_by = np.searchsorted(cost, share * cost[-1] + 1, side="left").tolist()
    steps_by[-1] = len(row_of)
    for k, ts in enumerate(tops[:-1]):
        assert steps_by[2 * blocks.index((ts[0], 0)) - 1] >= (k + 1) * STEPS

    with ExitStack() as ctx:
        bank = [ctx.enter_context(nc.psum_tensor(f"ap_bank{n}", [P, BANK], F32)) for n in range(8)]
        qk, tr, ob = (bank[0:2], bank[2:4]), bank[4:6], bank[6:8]
        q_in = [sem(f"ap_q_in{n}") for n in range(2)]
        k_hi_set, q_hi_set, q_lo_set = sem("ap_k_hi_set"), sem("ap_q_hi_set"), sem("ap_q_lo_set")
        qk_done, maxed, exped, turned, turned_out, pv_done, o_out = (
            sem("ap_" + n) for n in ("qk_done", "maxed", "exped", "turned", "turned_out", "pv_done", "o_out"))
        inv_set = sem("ap_inv_set")
        o_turned, o_copied = sem("ap_o_turned"), sem("ap_o_copied")
        block = ctx.enter_context(nc.Block())

        @block.sync
        def _(sp):
            for t in range(PT):
                if t >= 2:
                    sp.wait_ge(q_lo_set, t - 1)
                sp.dma_start(q[:, t % 2], io["q_t"][:, :, t * P:(t + 1) * P].rearrange("j p t -> p j t")).then_inc(q_in[t % 2], 16)

        @block.gpsimd
        def _(pool):
            pool.wait_ge(k_hi_set, 1)
            pool.tensor_tensor(k_lo[:, :, :], k_sb[:, :, 0:T_PROMPT], k_hi[:, :, :].bitcast(F32), ALU.subtract)
            for t in range(PT):
                pool.wait_ge(q_hi_set, t + 1)
                pool.tensor_tensor(q_lo[:, t % 2], q[:, t % 2], q_hi[:, t % 2].bitcast(F32), ALU.subtract).then_inc(q_lo_set, 1)

        @block.tensor
        def _(pe):
            def scores(n, half):
                t, j = blocks[n]
                rows = slice(half * HEAD_D, (half + 1) * HEAD_D)
                if j == 0:
                    pe.wait_ge(q_lo_set, t + 1)
                if n:
                    pe.wait_ge(maxed, 2 * n + half - 1)
                for c, (a, e) in enumerate(pieces((t + 1) * P)):
                    out, keys = qk[half][c][:, 0:e - a], (rows, j // GROUP, slice(a, e))
                    pe.matmul(out, q_hi[rows, t % 2, j, :], k_hi[keys], start=True, stop=False)
                    pe.matmul(out, q_lo[rows, t % 2, j, :], k_hi[keys], start=False, stop=False)
                    i = pe.matmul(out, q_hi[rows, t % 2, j, :], k_lo[keys], start=False, stop=True)
                i.then_inc(qk_done, 1)

            def turn(n, half):
                t, j = blocks[n]
                pe.wait_ge(exped, 2 * n + half + 1)
                if n or half:
                    pe.wait_ge(turned_out, 2 * n + half)
                for c in range(t + 1):
                    i = pe.transpose(tr[c // 4][:, c % 4 * P:(c % 4 + 1) * P], probs[:, half, c * P:(c + 1) * P], const["ident"][:, :])
                i.then_inc(turned, 1)

            def values(n, half):
                t, j = blocks[n]
                pe.wait_ge(turned_out, 2 * n + half + 1)
                if n:
                    pe.wait_ge(o_out, 2 * n + half - 1)
                    if half:
                        pe.wait_ge(o_copied, n)
                col = (j // GROUP * 2 + half) * HEAD_D
                for c in range(t + 1):
                    i = pe.matmul(ob[half][:, 0:HEAD_D], probs_t[:, half, c * P:(c + 1) * P], v_sb[:, c, col:col + HEAD_D],
                                  start=c == 0, stop=c == t)
                i.then_inc(pv_done, 1)

            def turn_o(n):
                pe.wait_ge(o_out, 2 * n + 2)
                pe.transpose(ob[1][:, P:2 * P], o[:, :], const["ident"][:, :]).then_inc(o_turned, 1)

            for n in range(len(blocks) + 1):
                for half in range(2):
                    if n:
                        turn(n - 1, half)
                    if n < len(blocks):
                        scores(n, half)
                    if n > 1 and half == 0:
                        turn_o(n - 2)
                    if n:
                        values(n - 1, half)
            turn_o(len(blocks) - 1)

        @block.scalar
        def _(act):
            def copy_out(n):
                t, j = blocks[n]
                act.wait_ge(o_turned, n + 1)
                act.activation(o_t[:, j, t * P:(t + 1) * P], ob[1][:, P:2 * P], ACT.Copy).then_inc(o_copied, 1)

            def split_q(t):
                act.wait_ge(q_in[t % 2], 16 * (t // 2 + 1))
                if t >= 2:
                    act.wait_ge(qk_done, 2 * QB * (t - 1))
                act.activation(q_hi[:, t % 2], q[:, t % 2], ACT.Copy).then_inc(q_hi_set, 1)

            act.activation(k_hi[:, :, :], k_sb[:, :, 0:T_PROMPT], ACT.Copy).then_inc(k_hi_set, 1)
            split_q(0)
            for n in range(len(blocks) + 1):
                if n % QB == QB // 2 and n // QB + 1 < PT:
                    split_q(n // QB + 1)
                for half in range(2):
                    if n:
                        t = blocks[n - 1][0]
                        act.wait_ge(turned, 2 * (n - 1) + half + 1)
                        if n > 1:
                            act.wait_ge(pv_done, 2 * (n - 1) + half - 1)
                        for c, (a, e) in enumerate(pieces((t + 1) * P)):
                            i = act.activation(probs_t[:, half, a:e], tr[c][:, 0:e - a], ACT.Copy)
                        i.then_inc(turned_out, 1)
                    if n < len(blocks):
                        keys = (blocks[n][0] + 1) * P
                        act.wait_ge(maxed, 2 * n + half + 1)
                        if n:
                            act.wait_ge(inv_set, 2 * n + half - 1)
                        act.activation(probs[:, half, 0:keys], probs[:, half, 0:keys], ACT.Exp, bias=neg_max[:, half],
                                       accum_out=total[:, half]).then_inc(exped, 1)
                    if n > 1 and half == 0:
                        copy_out(n - 2)
                    if n:
                        act.wait_ge(pv_done, 2 * (n - 1) + half + 1)
                        act.wait_ge(inv_set, 2 * (n - 1) + half + 1)
                        act.activation(o[:, half * HEAD_D:(half + 1) * HEAD_D], ob[half][:, 0:HEAD_D], ACT.Copy,
                                       scale=inv[:, (n - 1) % 2, half]).then_inc(o_out, 1)
            copy_out(len(blocks) - 1)

        @block.vector
        def _(dve):
            def take_top(first, end):
                for r in range(first, end):
                    ts = tops[row_of[r]]
                    scores = [score_p[:, score_at(t):score_at(t + 1)] for t in ts] if ts else [score_s[:, :]]
                    top_step(dve, top, scores, r % 2)
                    if r % STEPS < STEPS - 1:
                        continue
                    dve.drain()
                    if ts:
                        for t, score in zip(ts, scores):
                            mask_from(dve, mask_p[:, mask_at(t):mask_at(t + 1)], score)
                    else:
                        score = score_s
                        mask_from(dve, mask_s[:, 0:PAST], score[:, 0:PAST])
                        mask_from(dve, tail[:, :], score[:, PAST:S_KEYS])
                        dve.drain()
                        dst = mask_s[:, PAST:A_KEYS].rearrange("p (b t) -> p b t", t=DEC_T)
                        dve.tensor_tensor(dst, spread(tail[:, :].unsqueeze(1), dst.shape), spread(other[:, :].unsqueeze(2), dst.shape),
                                          ALU.add)

            def invert(u):
                n, half = divmod(u, 2)
                dve.wait_ge(exped, u + 1)
                if n > 1:
                    dve.wait_ge(o_out, u - 3)
                dve.reciprocal(inv[:, n % 2, half], total[:, half]).then_inc(inv_set, 1)

            for n, (t, j) in enumerate(blocks):
                for half in range(2):
                    u = 2 * n + half
                    dve.wait_ge(qk_done, u + 1)
                    if n:
                        dve.wait_ge(turned, u - 1)
                    parts = pieces((t + 1) * P)
                    for c, (a, e) in enumerate(parts):
                        dve.tensor_tensor_reduce(out=probs[:, half, a:e], in0=qk[half][c][:, 0:e - a],
                                                 in1=mask_p[:, mask_at(t) + a:mask_at(t) + e], scale=1.0, scalar=-3e38,
                                                 op0=ALU.add, op1=ALU.max, accum_out=part_max[:, half, c:c + 1])
                    dve.drain()
                    if len(parts) == 2:
                        dve.tensor_tensor(part_max[:, half, 0:1], part_max[:, half, 0:1], part_max[:, half, 1:2], ALU.max)
                        dve.drain()
                    dve.tensor_scalar(neg_max[:, half], part_max[:, half, 0:1], -1.0, None, ALU.mult).then_inc(maxed, 1)
                    if u:
                        invert(u - 1)
                    take_top(steps_by[u - 1] if u else 0, steps_by[u])
            invert(2 * len(blocks) - 1)
            dve.drain()


def attend_sample_phase(nc, env, x):
    io, const, sem, tick = env["io"], env["const"], env["sem"], env["tick"]
    k_sb, v_sb, mask_s, o_t = env["k"], env["v"], env["mask_s"], env["o_t"]
    take = Space(nc, env["o_end"], env["end"]).take
    keys, vals = take("as_keys", [P, 2, PAST]), take("as_vals", [P, 2, PAST // P, N_KV * HEAD_D])
    probs, probs_t = take("as_probs", [P, 2, A_KEYS]), take("as_probs_t", [P, A_KEYS])
    q = take("as_q", [P, QB, T_SAMPLE])
    q_u = take("as_q_u", [P, 2, GROUP, DEC_T])
    rows_of = take("as_rows_of", [P, DEC_B, P], BF16)
    chunks = pieces(A_KEYS)
    NCHK = len(chunks)
    part_max, neg_max = take("as_part_max", [P, 2, NCHK]), take("as_neg_max", [P, 2, 1])
    total, inv = take("as_total", [P, 2, 1]), take("as_inv", [P, 2, 1])
    o = take("as_o", [P, P])
    tiles = [(a // P, e // P) for a, e in chunks]
    UNITS = 2 * DEC_B

    with ExitStack() as ctx:
        bank = [ctx.enter_context(nc.psum_tensor(f"as_bank{n}", [P, BANK], F32)) for n in range(8)]
        qk, tr, ob = bank[0:NCHK], bank[5:7], bank[7]
        consts_in = sem("as_consts_in")
        keys_in = [sem(f"as_keys_in{n}") for n in range(2)]
        vals_in = [sem(f"as_vals_in{n}") for n in range(2)]
        q_set, qk_done, read, exped, turned, turned_out, pv_done, o_out, o_turned, o_copied = (
            sem("as_" + n) for n in ("q_set", "qk_done", "read", "exped", "turned", "turned_out", "pv_done", "o_out", "o_turned", "o_copied"))
        maxed = sem("as_maxed")
        block = ctx.enter_context(nc.Block())

        @block.sync
        def _(sp):
            tk = tick["sp"]
            sp.dma_start(q[:, :, :], io["q_t"][:, :, T_PROMPT:T].rearrange("j p t -> p j t")).then_inc(consts_in, 16)
            sp.dma_start(rows_of[:, :, :], io["spread_b"]).then_inc(consts_in, 16)

            def load(b, par):
                for p in range(2):
                    if not isinstance(b, int):
                        hold(sp, qk_done, (b * 2 + (p - 1)) * NCHK, tk)
                    elif b:
                        sp.wait_ge(qk_done, (b * 2 + p - 1) * NCHK)
                    sp.dma_start(keys[:, p], io["cache_k"][b, p]).then_inc(keys_in[p], 16)
                if not (isinstance(b, int) and b < 2):
                    hold(sp, pv_done, b * 2 - 2, tk)
                sp.dma_start(vals[:, par], io["cache_v"][b]).then_inc(vals_in[par], 16)

            load(0, 0)
            load(1, 1)
            with sp.Fori(1, DEC_B // 2) as m:
                load(m * 2, 0)
                load(m * 2 + 1, 1)

        @block.gpsimd
        def _(pool):
            pool.wait_ge(consts_in, 32)

            def put_q(b):
                for p in range(2):
                    hold(pool, qk_done, (b * 2 + (p - 1)) * NCHK, tick["pool"])
                    pool.tensor_copy(q_u[:, p], q[:, GROUP * p:GROUP * (p + 1), :].rearrange("p g (b t) -> p g b t", t=DEC_T)[:, :, b, :])\
                        .then_inc(q_set, 1)

            put_q(0)
            with pool.Fori(1, DEC_B) as b:
                put_q(b)

        @block.tensor
        def _(pe):
            tk = tick["pe"]
            pe.wait_ge(consts_in, 32)

            def scores(u, b, p, half_b, c):
                a, e = chunks[c]
                if c == 0:
                    hold(pe, q_set, u + 1, tk)
                    hold(pe, keys_in[p], (b + 1) * 16, tk)
                hold(pe, read, (u - 1) * NCHK + c + 1, tk)
                out = qk[c]
                pe.matmul(out[:, 0:e - a], rows_of[:, b, :], mask_s[:, a:e], start=True, stop=False)
                for half in range(2):
                    rows = slice(half * HEAD_D, (half + 1) * HEAD_D)
                    rhs = keys[rows, p, a:e] if c < NCHK - 1 else k_sb[rows, p, T_PROMPT:T]
                    i = pe.matmul(out[rows, 0:e - a], q_u[rows, p].rearrange("p g t -> p (g t)"), rhs, start=False, stop=True)
                i.then_inc(qk_done, 1)

            def turn(u, p, c):
                if c == 0:
                    hold(pe, exped, u + 1, tk)
                hold(pe, turned_out, u * NCHK + c - 1, tk)
                lo, hi = tiles[c]
                for n in range(lo, hi):
                    i = pe.transpose(tr[(c + p * NCHK) % 2][:, (n - lo) * P:(n - lo + 1) * P], probs[:, p, n * P:(n + 1) * P], const["ident"][:, :])
                i.then_inc(turned, 1)

            def values(u, b, p, par, half_b):
                hold(pe, turned_out, (u + 1) * NCHK, tk)
                if p == 0:
                    hold(pe, vals_in[par], (half_b + 1) * 16, tk)
                hold(pe, o_copied, u, tk)
                n = PAST // P
                for c in range(n + 1):
                    rhs = vals[:, par, c, p * P:(p + 1) * P] if c < n else v_sb[:, NT - 1, p * P:(p + 1) * P]
                    i = pe.matmul(ob[:, 0:P], probs_t[:, c * P:(c + 1) * P], rhs, start=c == 0, stop=c == n)
                i.then_inc(pv_done, 1)

            def turn_o(u):
                hold(pe, o_out, u + 1, tk)
                pe.transpose(ob[:, P:2 * P], o[:, :], const["ident"][:, :]).then_inc(o_turned, 1)

            def body(b, par, half_b, first=False):
                for p in range(2):
                    u = b * 2 + p
                    for c in range(NCHK):
                        scores(u, b, p, half_b, c)
                        if not (first and p == 0):
                            turn(u - 1, 1 - p, c)
                    if not (first and p == 0):
                        if p == 0:
                            values(u - 1, b - 1, 1, 1 - par, None)
                        else:
                            values(u - 1, b, 0, par, half_b)
                        turn_o(u - 1)

            body(0, 0, 0, True)
            body(1, 1, 0)
            with pe.Fori(1, DEC_B // 2) as m:
                body(m * 2, 0, m)
                body(m * 2 + 1, 1, m)
            for c in range(NCHK):
                turn(UNITS - 1, 1, c)
            values(UNITS - 1, DEC_B - 1, 1, 1, None)
            turn_o(UNITS - 1)

        @block.scalar
        def _(act):
            tk = tick["act"]

            def softmax(u, p):
                hold(act, maxed, u + 1, tk)
                act.activation(probs[:, p], probs[:, p], ACT.Exp, bias=neg_max[:, p], accum_out=total[:, p]).then_inc(exped, 1)

            def copy(u, p, c):
                a, e = chunks[c]
                hold(act, turned, u * NCHK + c + 1, tk)
                if c == 0:
                    hold(act, pv_done, u, tk)
                act.activation(probs_t[:, a:e], tr[(c + p * NCHK) % 2][:, 0:e - a], ACT.Copy).then_inc(turned_out, 1)

            def body(b, first=False):
                for p in range(2):
                    u = b * 2 + p
                    if not (first and p == 0):
                        for c in range(NCHK):
                            copy(u - 1, 1 - p, c)
                    softmax(u, p)

            body(0, True)
            with act.Fori(1, DEC_B) as b:
                body(b)
            for c in range(NCHK):
                copy(UNITS - 1, 1, c)

        @block.vector
        def _(dve):
            tk = tick["dve"]

            def maxima(u, p):
                for c, (a, e) in enumerate(chunks):
                    hold(dve, qk_done, u * NCHK + c + 1, tk)
                    if c == 0:
                        hold(dve, turned, (u - 1) * NCHK, tk)
                    dve.tensor_scalar(probs[:, p, a:e], qk[c][:, 0:e - a], 0.0, None, ALU.add, ALU.max,
                                      accum_out=part_max[:, p, c:c + 1]).then_inc(read, 1)
                dve.drain()
                dve.reduce_max(neg_max[:, p], part_max[:, p, :], AX.X)
                dve.drain()
                dve.tensor_scalar(neg_max[:, p], neg_max[:, p], -1.0, None, ALU.mult).then_inc(maxed, 1)

            def outputs(u, b, p):
                hold(dve, exped, u + 1, tk)
                dve.reciprocal(inv[:, p], total[:, p])
                hold(dve, pv_done, u + 1, tk)
                hold(dve, o_turned, u, tk)
                dve.drain()
                dve.tensor_scalar(o[:, :], ob[:, 0:P], inv[:, p], None, ALU.mult).then_inc(o_out, 1)
                hold(dve, o_turned, u + 1, tk)
                for half in range(2):
                    rows = slice(half * HEAD_D, (half + 1) * HEAD_D)
                    dst = o_t[rows, GROUP * p:GROUP * (p + 1), T_PROMPT:T].rearrange("p g (b t) -> p g b t", t=DEC_T)[:, :, b, :]
                    src = ob[rows, P + half * HEAD_D:P + (half + 1) * HEAD_D].rearrange("p (g t) -> p g t", t=DEC_T)
                    i = dve.tensor_copy(dst, src)
                i.then_inc(o_copied, 1)

            def body(b, first=False):
                for p in range(2):
                    maxima(b * 2 + p, p)
                    if not (first and p == 0):
                        outputs(b * 2 + p - 1, b - (1 - p), 1 - p)

            body(0, True)
            with dve.Fori(1, DEC_B) as b:
                body(b)
            outputs(UNITS - 1, DEC_B - 1, 1)
            dve.drain()


def attend_out_phase(nc, env, x):
    io, sem, tick, o_t = env["io"], env["sem"], env["tick"], env["o_t"]
    take = Space(nc, env["o_end"], env["end"]).take
    o_hi = take("ao_o_hi", [P, QB, T], F32R)
    o_lo = take("ao_o_lo", [P, QB, T], F32R, at=env["free"])
    assert 4 * QB * T <= t_at["o_t"] - env["free"]
    raw = take("ao_raw", [P, 2, SLAB])
    w_hi, w_lo = take("ao_w_hi", [P, 2, SLAB], F32R), take("ao_w_lo", [P, 2, SLAB], F32R)

    with ExitStack() as ctx:
        lin = [ctx.enter_context(nc.psum_tensor(f"ao_lin{g}", [P, BANK], F32)) for g in range(G)]
        W = Slabs(nc, sem, "ao", io["weights"], HG_SLABS + FFN_SLABS + DSA_PROJ, KB, 2, raw, w_hi, w_lo, tick)
        hi_set, lo_set, added = sem("ao_hi_set"), sem("ao_lo_set"), sem("ao_added")
        block = ctx.enter_context(nc.Block())

        @block.sync
        def _(sp):
            W.load_all(sp)

        @block.scalar
        def _(act):
            for kb in range(QB):
                act.activation(o_hi[:, kb], o_t[:, kb], ACT.Copy).then_inc(hi_set, 1)
                if kb == 0:
                    W.split_hi(act, 0, 0, 0, 0, 0)
            for s in range(1, KB):
                W.split_hi(act, s, s // 2, s % 2, s % 2, 3 * (s - 1))

        @block.vector
        def _(dve):
            for kb in range(QB):
                dve.wait_ge(hi_set, kb + 1)
                dve.tensor_tensor(o_lo[:, kb], o_t[:, kb], o_hi[:, kb].bitcast(F32), ALU.subtract).then_inc(lo_set, 1)
                if kb == 0:
                    W.split_lo(dve, 0, 0, 0)
            for s in range(KB):
                if s + 1 < KB:
                    W.split_lo(dve, s + 1, (s + 1) % 2, (s + 1) % 2)
                for g in range(G):
                    dve.wait_ge(W.units, 3 * s + g + 1)
                    xs = x[:, s, g * GT:(g + 1) * GT]
                    dve.tensor_tensor(xs, xs, lin[g][:, 0:GT], ALU.add).then_inc(added, 1)
            dve.drain()

        @block.tensor
        def _(pe):
            pe.wait_ge(lo_set, QB)
            for s in range(KB):
                pe.wait_ge(W.lo_done, s + 1)
                for g in range(G):
                    if s:
                        pe.wait_ge(added, 3 * (s - 1) + g + 1)
                    W.block(pe, lin[g][:, 0:GT], s % 2, o_hi, o_lo, g).then_inc(W.units, 1)


def final_phase(nc, env, x):
    io, const, sem, tick = env["io"], env["const"], env["sem"], env["tick"]
    take = Space(nc, env["free"], env["end"]).take
    sq = take("fn_sq", [P, KB, GT])
    std = take("fn_std", [P, G, GT])
    y = take("fn_y", [P, 2, KB, GT])
    gain = take("fn_gain", [P, KB])
    with ExitStack() as ctx:
        bank = [ctx.enter_context(nc.psum_tensor(f"fn_bank{g}", [P, BANK], F32)) for g in range(G)]
        gain_in, squared, summed, rooted, scaled = (sem("fn_" + n) for n in ("gain_in", "squared", "summed", "rooted", "scaled"))
        y_out = [sem(f"fn_y_out{n}") for n in range(2)]
        block = ctx.enter_context(nc.Block())

        @block.sync
        def _(sp):
            sp.dma_start(gain[:, :], io["gains"][4]).then_inc(gain_in, 16)
            for g in range(G):
                sp.wait_ge(scaled, g + 1)
                sp.dma_start(io["y"][:, :, g * GT:(g + 1) * GT], y[:, g % 2]).then_inc(y_out[g % 2], 16)
            sp.wait_ge(y_out[0], 32)
            sp.wait_ge(y_out[1], 16)

        @block.scalar
        def _(act):
            for g in range(G):
                for kb in range(KB):
                    if g:
                        act.wait_ge(summed, (g - 1) * KB + kb + 1)
                    act.activation(sq[:, kb], x[:, kb, g * GT:(g + 1) * GT], ACT.Square).then_inc(squared, 1)
                act.wait_ge(summed, (g + 1) * KB)
                act.activation(std[:, g], bank[g][:, 0:GT], ACT.Sqrt, bias=EPS).then_inc(rooted, 1)

        @block.tensor
        def _(pe):
            for u in range(G * KB):
                pe.wait_ge(squared, u + 1)
                pe.matmul(bank[u // KB][:, 0:GT], const["ones"][:, :], sq[:, u % KB], start=u % KB == 0,
                          stop=u % KB == KB - 1).then_inc(summed, 1)

        @block.vector
        def _(dve):
            dve.wait_ge(gain_in, 16)
            for g in range(G):
                dve.wait_ge(rooted, g + 1)
                dve.reciprocal(std[:, g], std[:, g])
                dve.drain()
                if g >= 2:
                    dve.wait_ge(y_out[g % 2], 16)
                for kb in range(KB):
                    i = dve.scalar_tensor_tensor(y[:, g % 2, kb], x[:, kb, g * GT:(g + 1) * GT], gain[:, kb:kb + 1], std[:, g],
                                                 ALU.mult, ALU.mult)
                i.then_inc(scaled, 1)


FFN_SLABS = 3 * FB
HG_SLABS = 5 * HEADS


def constants():
    s, t = np.arange(P)[:, None], np.arange(P)[None, :]
    tri = (s % CH <= np.arange(CH)[None, :]).astype(np.float32)
    own = ((s // DEC_T == t // DEC_T) & (s <= t)).astype(np.float32)
    own_b = (s // DEC_T == np.arange(DEC_B)[None, :]).astype(np.float32)
    pos = np.arange(T)
    start = np.where(pos < T_PROMPT, pos % CH == 0, pos % DEC_T == 0)
    keep = np.broadcast_to(1.0 - start, (P, T)).astype(mybir.dt.np(BF16))
    return {"tri": tri, "own": own, "own_b": own_b, "keep": keep, "ident": np.eye(P, dtype=np.float32),
            **dsa_constants(),
            "ones": np.full((P, P), 1.0 / D, np.float32), "ones_v": np.full((P, P), 1.0 / P, np.float32)}


def layout(i):
    x = np.concatenate([i["x_prompt"].reshape(T_PROMPT, D), i["x_sample"].reshape(T_SAMPLE, D)])
    w = i["hg_w_in"][0]
    q, f, v, g = (in_slabs(w[:, n * D:(n + 1) * D]) for n in range(4))
    out = down_slabs(i["hg_w_out"][0])
    order = []
    for h in range(HEADS + 2):
        if h >= 2:
            order.append(out[h - 2])
        if h < HEADS:
            order += [f[h], v[h], q[h], g[h]]
    slabs = [np.stack(order)]

    def ffn(layer):
        gate, up = in_slabs(i["ffn_w_in"][layer][:, :D_FF]), in_slabs(i["ffn_w_in"][layer][:, D_FF:])
        down = down_slabs(i["ffn_w_down"][layer])
        order = []
        for c in range(FB // 2 + 1):
            if c < FB // 2:
                order += [gate[2 * c], up[2 * c], gate[2 * c + 1], up[2 * c + 1]]
            if c:
                order += [down[2 * c - 2], down[2 * c - 1]]
        return np.stack(order)

    slabs.append(ffn(0))
    slabs.append(dsa_slabs(i))
    slabs.append(ffn(1))
    gains = np.stack([i["norm_mix"][0], i["norm_ffn"][0], i["norm_mix"][1], i["norm_ffn"][1], i["norm_final"]])
    a = {
        "x": x.T.reshape(KB, P, T).transpose(1, 0, 2),
        "weights": np.concatenate(slabs),
        "gains": gains.reshape(5, KB, P).transpose(0, 2, 1),
        "hg_lb": i["hg_lb"].reshape(2, HEADS, P, 1).transpose(2, 0, 1, 3),
        "hg_norm": i["hg_norm"][0].reshape(P, 1),
        "state_hgrn": i["state_hgrn"][0].transpose(1, 2, 0, 3),
        "state_conv": i["state_conv"].reshape(2, DEC_B, 2, FB, P).transpose(0, 4, 3, 1, 2),
        "conv_p": np.concatenate([i["ffn_conv_w"], i["ffn_conv_b"][:, None]], axis=1).reshape(2, 4, FB, P).transpose(0, 3, 2, 1),
    }
    a.update(dsa_layout(i))
    return {k: np.ascontiguousarray(v) for k, v in {**a, **constants()}.items()}


OUTS = {
    "ki_out": (HEAD_D, T),
    "k_out": (P, 2, T),
    "v_out": (P, NT, N_KV * HEAD_D),
    "y": (P, KB, T),
    "hgrn_p": (HEADS, P, P),
    "hgrn_s": (HEADS, P, DEC_B, P),
    "conv_out": (2, P, FB, (1 + DEC_B) * (CONV_W - 1)),
}


def load_x(sp, io, x, x_in, g):
    cols = slice(g * GT, (g + 1) * GT)
    sp.dma_start(x[:, :, cols], io["x"][:, :, cols]).then_inc(x_in[g], 16)


def program(nc, io, phases=None):
    io["q_t"] = nc.dram_tensor("q_t", (QB, P, T), F32, kind="Internal").ap()
    io["qi_t"] = nc.dram_tensor("qi_t", (IDX_B, P, T), F32, kind="Internal").ap()
    with ExitStack() as ctx:
        sem = lambda name: ctx.enter_context(nc.semaphore(name))
        tick = {e: sem("tick_" + e) for e in ("pe", "act", "dve", "pool", "sp")}

        end = nc.sbuf_usable_end // 32 * 32
        free = (nc.sbuf_base + 31) // 32 * 32
        arena = ctx.enter_context(nc.sbuf_tensor("arena", [P, (end - free) // 4 - 16], F32))
        sp_ = Space(nc, free, end)
        x = sp_.take("x", [P, KB, T])
        const = {n: sp_.take("c_" + n, [P, P]) for n in ("ident", "ones", "ones_v")}
        env = {"io": io, "const": const, "sem": sem, "tick": tick, "free": sp_.at, "end": end,
               "x_in": [sem(f"x_in{g}") for g in range(G)], "ffn_first": FFN_FIRST, "ffn_gain": (1, 3),
               "norms": 0, "norm_sems": [sem("norm_" + n) for n in ("squared", "summed", "rooted", "scaled", "hi_done", "lo_done")]}
        consts_in = sem("consts_in")
        with nc.Block() as block:
            @block.sync
            def _(sp):
                load_x(sp, io, x, env["x_in"], 0)
                for n in const:
                    sp.dma_start(const[n][:, :], io[n]).then_inc(consts_in, 16)
                sp.wait_ge(consts_in, 16 * len(const))
        for name, phase in PHASES:
            if phases is None or name in phases:
                phase(nc, env, x)


PHASES = [("hgrn", hgrn_phase), ("ffn0", lambda nc, env, x: ffn_phase(nc, env, x, 0)), ("proj", project_phase),
          ("select", select_phase), ("attp", attend_prompt_phase), ("atts", attend_sample_phase), ("ato", attend_out_phase),
          ("ffn1", lambda nc, env, x: ffn_phase(nc, env, x, 1)), ("final", final_phase)]
FFN_FIRST = (HG_SLABS, HG_SLABS + FFN_SLABS + DSA_PROJ + KB)


def kernel(**inputs):
    import concourse.bacc as bacc
    from concourse.bass_utils import run_bass_kernel_spmd

    nc = bacc.Bacc("TRN2", target_bir_lowering=False, num_devices=1)
    arrays = layout({name: np.asarray(a) for name, a in inputs.items()})
    io = {name: nc.dram_tensor("in_" + name, a.shape, mybir.dt.from_np(a.dtype), kind="ExternalInput").ap()
          for name, a in arrays.items()}
    for name, shape in OUTS.items():
        io[name] = nc.dram_tensor("out_" + name, shape, F32, kind="ExternalOutput").ap()
    program(nc, io)
    r = run_bass_kernel_spmd(nc, [{"in_" + name: a for name, a in arrays.items()}], core_ids=[0]).results[0]
    out = {name: r["out_" + name] for name in OUTS}

    def frames(a, tail):
        return a[:T_PROMPT].reshape((1, T_PROMPT) + tail), a[T_PROMPT:].reshape((DEC_B, DEC_T) + tail)

    y_p, y_s = frames(out["y"].transpose(2, 1, 0).reshape(T, D), (D,))
    k_p, k_s = frames(out["k_out"].transpose(2, 1, 0).reshape(T, N_KV * HEAD_D), (N_KV, HEAD_D))
    v_p, v_s = frames(out["v_out"].transpose(1, 0, 2).reshape(T, N_KV * HEAD_D), (N_KV, HEAD_D))
    ki_p, ki_s = frames(out["ki_out"].T, (HEAD_D,))
    conv = out["conv_out"].transpose(0, 3, 2, 1).reshape(2, 1 + DEC_B, CONV_W - 1, D_FF)
    return (y_p, y_s, k_p[None], v_p[None], ki_p[None], out["hgrn_p"][None, None], conv[:, :1],
            k_s[None], v_s[None], ki_s[None], out["hgrn_s"].transpose(2, 0, 1, 3)[None], conv[:, 1:])
```
